# Optimizing a Trainium2 kernel written in Bass

```python
import jax
import jax.numpy as jnp
from jax import lax

D_MODEL = 1024
BATCH = 1
SEQ = 256
DEPTH = 2

MLA_HEADS = 8
MLA_Q_RANK = 256
MLA_KV_RANK = 128
MLA_NOPE = 64
MLA_ROPE = 32
MLA_V = 64
MLA_QK = MLA_NOPE + MLA_ROPE
ROPE_THETA = 10000.0
ATTN_Q_BLOCK = 128

GDN_HEADS = 8
GDN_DK = 64
GDN_DV = 64
GDN_CONV = 4
GDN_CHUNK = 64
GDN_CONV_CH = 2 * GDN_HEADS * GDN_DK + GDN_HEADS * GDN_DV

MOBA_HEADS = 8
MOBA_DH = 64
MOBA_BLOCK = 256
MOBA_TOPK = 3
MOBA_Q_CHUNK = 32

N_BRANCH = 3
BRANCH_W = 512

PEER_HEADS = 8
PEER_NKEYS = 128
PEER_EXPERTS = PEER_NKEYS * PEER_NKEYS
PEER_DQ = 256
PEER_TOPK = 16
PEER_TOK_CHUNK = 128

NORM_EPS = 1e-6
NEG_INF = -1e30

SPLIT_SIZES = (
    MLA_Q_RANK, MLA_KV_RANK, MLA_ROPE,
    GDN_HEADS * GDN_DK, GDN_HEADS * GDN_DK,
    GDN_HEADS * GDN_DV, GDN_HEADS * GDN_DV,
    GDN_HEADS, GDN_HEADS,
    MOBA_HEADS * MOBA_DH, MOBA_HEADS * MOBA_DH, MOBA_HEADS * MOBA_DH,
    N_BRANCH * D_MODEL,
)
IN_COLS = sum(SPLIT_SIZES)
SPLIT_POINTS = tuple(sum(SPLIT_SIZES[:i + 1]) for i in range(len(SPLIT_SIZES) - 1))

kernel_name = 'hybrid_mla_gdn_moba_peer_adaln'

def rms_norm(x, gain=None):
    xf = x.astype(jnp.float32)
    y = xf * lax.rsqrt(jnp.mean(xf * xf, axis=-1, keepdims=True) + NORM_EPS)
    if gain is not None:
        y = y * gain.astype(jnp.float32)
    return y.astype(x.dtype)

def l2_norm(x):
    xf = x.astype(jnp.float32)
    return xf * lax.rsqrt(jnp.sum(xf * xf, axis=-1, keepdims=True) + NORM_EPS)

def modulate(x, shift, scale):
    return rms_norm(x) * (1.0 + scale[:, None, :]) + shift[:, None, :]

def apply_rope(x, positions):
    half = x.shape[-1] // 2
    inv_freq = ROPE_THETA ** (-jnp.arange(half, dtype=jnp.float32) / half)
    ang = positions.astype(jnp.float32)[..., None] * inv_freq
    cos, sin = jnp.cos(ang)[:, :, None, :], jnp.sin(ang)[:, :, None, :]
    xf = x.astype(jnp.float32)
    x1, x2 = xf[..., :half], xf[..., half:]
    return jnp.concatenate([x1 * cos - x2 * sin, x1 * sin + x2 * cos], axis=-1).astype(x.dtype)

def causal_attention(q, k, v, scale):
    B, S, H, Dq = q.shape
    nq = S // ATTN_Q_BLOCK
    qb = q.reshape(B, nq, ATTN_Q_BLOCK, H, Dq).transpose(1, 0, 2, 3, 4)
    kpos = jnp.arange(S)

    def one_block(args):
        qi, i = args
        s = jnp.einsum('bqhd,bkhd->bhqk', qi, k, preferred_element_type=jnp.float32) * scale
        qpos = i * ATTN_Q_BLOCK + jnp.arange(ATTN_Q_BLOCK)
        s = jnp.where(kpos[None, :] <= qpos[:, None], s, NEG_INF)
        p = jax.nn.softmax(s, axis=-1).astype(v.dtype)
        return jnp.einsum('bhqk,bkhd->bqhd', p, v)

    o = lax.map(one_block, (qb, jnp.arange(nq)))
    return o.transpose(1, 0, 2, 3, 4).reshape(B, S, H, v.shape[-1])

def mla_branch(cq, ckv, k_rope, positions, q_gain, w_uq, kv_gain, w_ukv, qn_gain, kn_gain):
    B, S, _ = cq.shape
    q = (rms_norm(cq, q_gain) @ w_uq).reshape(B, S, MLA_HEADS, MLA_QK)
    kv = (rms_norm(ckv, kv_gain) @ w_ukv).reshape(B, S, MLA_HEADS, MLA_NOPE + MLA_V)
    k_nope, v = kv[..., :MLA_NOPE], kv[..., MLA_NOPE:]
    k_pe = jnp.broadcast_to(k_rope[:, :, None, :], (B, S, MLA_HEADS, MLA_ROPE))
    k = jnp.concatenate([k_nope, k_pe], axis=-1)
    q = rms_norm(q, qn_gain)
    k = rms_norm(k, kn_gain)
    q = jnp.concatenate([q[..., :MLA_NOPE], apply_rope(q[..., MLA_NOPE:], positions)], axis=-1)
    k = jnp.concatenate([k[..., :MLA_NOPE], apply_rope(k[..., MLA_NOPE:], positions)], axis=-1)
    o = causal_attention(q, k, v, MLA_QK ** -0.5)
    return o.reshape(B, S, MLA_HEADS * MLA_V)

def causal_conv(x, w):
    C = x.shape[-1]
    return lax.conv_general_dilated(
        x, w[:, None, :].astype(x.dtype), window_strides=(1,), padding=[(GDN_CONV - 1, 0)],
        dimension_numbers=('NWC', 'WIO', 'NWC'), feature_group_count=C)

def gated_delta_rule_chunked(q, k, v, g, beta):
    B, S, H, DK = q.shape
    DV = v.shape[-1]
    C = GDN_CHUNK
    N = S // C
    f32 = jnp.float32

    def chunks(t):
        return t.astype(f32).reshape(B, N, C, H, -1).transpose(0, 3, 1, 2, 4)

    q, k, v = chunks(q), chunks(k), chunks(v)
    g = chunks(g[..., None])[..., 0]
    beta = chunks(beta[..., None])[..., 0]
    gc = jnp.cumsum(g, axis=-1)
    tri = jnp.tril(jnp.ones((C, C), dtype=bool))
    strict = jnp.tril(jnp.ones((C, C), dtype=bool), -1)
    diff = gc[..., :, None] - gc[..., None, :]
    decay = jnp.where(tri, jnp.exp(jnp.where(tri, diff, 0.0)), 0.0)
    k_beta = k * beta[..., None]
    a_mat = jnp.where(strict, jnp.einsum('bhnid,bhnjd->bhnij', k_beta, k) * decay, 0.0) + jnp.eye(C, dtype=f32)
    rhs = jnp.concatenate([v * beta[..., None], k_beta * jnp.exp(gc)[..., None]], axis=-1)
    sol = lax.linalg.triangular_solve(a_mat, rhs, left_side=True, lower=True, unit_diagonal=True)
    u, w = sol[..., :DV], sol[..., DV:]
    attn = jnp.einsum('bhnid,bhnjd->bhnij', q, k) * decay

    def step(state, xs):
        q_i, k_i, u_i, w_i, attn_i, gc_i = xs
        v_new = u_i - jnp.einsum('bhcd,bhde->bhce', w_i, state)
        o_i = (jnp.einsum('bhcd,bhde->bhce', q_i * jnp.exp(gc_i)[..., None], state)
               + jnp.einsum('bhij,bhje->bhie', attn_i, v_new))
        g_last = gc_i[..., -1:]
        state = (state * jnp.exp(g_last)[..., None]
                 + jnp.einsum('bhcd,bhce->bhde', k_i * jnp.exp(g_last - gc_i)[..., None], v_new))
        return state, o_i

    xs = tuple(jnp.moveaxis(t, 2, 0) for t in (q, k, u, w, attn, gc))
    state0 = jnp.zeros((B, H, DK, DV), f32)
    _, o = lax.scan(step, state0, xs)
    return o.transpose(1, 0, 3, 2, 4).reshape(B, S, H, DV)

def gdn_branch(q, k, v, z, a, b, conv_w, a_log, dt_bias, o_gain):
    B, S, _ = q.shape
    f32 = jnp.float32
    qkv = jax.nn.silu(causal_conv(jnp.concatenate([q, k, v], axis=-1), conv_w))
    qd, kd = GDN_HEADS * GDN_DK, 2 * GDN_HEADS * GDN_DK
    q = l2_norm(qkv[..., :qd].reshape(B, S, GDN_HEADS, GDN_DK)) * (GDN_DK ** -0.5)
    k = l2_norm(qkv[..., qd:kd].reshape(B, S, GDN_HEADS, GDN_DK))
    v = qkv[..., kd:].reshape(B, S, GDN_HEADS, GDN_DV)
    beta = jax.nn.sigmoid(b.astype(f32))
    g = -jnp.exp(a_log.astype(f32)) * jax.nn.softplus(a.astype(f32) + dt_bias.astype(f32))
    o = gated_delta_rule_chunked(q, k, v, g, beta).astype(z.dtype)
    o = rms_norm(o, o_gain) * jax.nn.silu(z.reshape(B, S, GDN_HEADS, GDN_DV))
    return o.reshape(B, S, GDN_HEADS * GDN_DV)

def moba_branch(q, k, v, qn_gain, kn_gain):
    B, S, _ = q.shape
    H, Dh, L = MOBA_HEADS, MOBA_DH, MOBA_BLOCK
    nb = -(-S // L)
    s_pad = nb * L
    topk = min(MOBA_TOPK, nb)
    f32 = jnp.float32
    q = rms_norm(q.reshape(B, S, H, Dh), qn_gain).transpose(0, 2, 1, 3)
    k = rms_norm(k.reshape(B, S, H, Dh), kn_gain).transpose(0, 2, 1, 3)
    v = v.reshape(B, S, H, Dh).transpose(0, 2, 1, 3)
    pad = ((0, 0), (0, 0), (0, s_pad - S), (0, 0))
    kb = jnp.pad(k, pad).reshape(B, H, nb, L, Dh)
    vb = jnp.pad(v, pad).reshape(B, H, nb, L, Dh)
    k_mean = jnp.mean(kb.astype(f32), axis=3)
    gate = jnp.einsum('bhsd,bhnd->bhsn', q.astype(f32), k_mean)
    q_blk = jnp.arange(S) // L
    gate = jnp.where(jnp.arange(nb)[None, :] < q_blk[:, None], gate, NEG_INF)
    _, sel = lax.top_k(gate, topk)
    valid = jnp.arange(topk)[None, :] < q_blk[:, None]
    scale = Dh ** -0.5
    gather = jax.vmap(jax.vmap(lambda blocks, idx: blocks[idx]))

    def one_chunk(ci):
        start = ci * MOBA_Q_CHUNK
        qc = lax.dynamic_slice_in_dim(q, start, MOBA_Q_CHUNK, axis=2)
        sc = lax.dynamic_slice_in_dim(sel, start, MOBA_Q_CHUNK, axis=2)
        vmask = lax.dynamic_slice_in_dim(valid, start, MOBA_Q_CHUNK, axis=0)
        k_sel = gather(kb, sc)
        v_sel = gather(vb, sc)
        s_sel = jnp.einsum('bhqd,bhqjld->bhqjl', qc, k_sel, preferred_element_type=f32) * scale
        s_sel = jnp.where(vmask[None, None, :, :, None], s_sel, NEG_INF)
        own = start // L
        k_own = lax.dynamic_index_in_dim(kb, own, axis=2, keepdims=False)
        v_own = lax.dynamic_index_in_dim(vb, own, axis=2, keepdims=False)
        s_own = jnp.einsum('bhqd,bhld->bhql', qc, k_own, preferred_element_type=f32) * scale
        qpos = start + jnp.arange(MOBA_Q_CHUNK)
        kpos = own * L + jnp.arange(L)
        s_own = jnp.where(kpos[None, :] <= qpos[:, None], s_own, NEG_INF)
        s = jnp.concatenate([s_sel.reshape(B, H, MOBA_Q_CHUNK, topk * L), s_own], axis=-1)
        p = jax.nn.softmax(s, axis=-1).astype(v.dtype)
        p_sel = p[..., :topk * L].reshape(B, H, MOBA_Q_CHUNK, topk, L)
        return (jnp.einsum('bhqjl,bhqjld->bhqd', p_sel, v_sel)
                + jnp.einsum('bhql,bhld->bhqd', p[..., topk * L:], v_own))

    o = lax.map(one_chunk, jnp.arange(S // MOBA_Q_CHUNK))
    return o.transpose(1, 0, 3, 2, 4).reshape(B, S, H * Dh)

def peer_ffn(h, w_query, sub_keys, expert_u, expert_v):
    B, S, D = h.shape
    T = B * S
    K = PEER_TOPK
    ht = h.reshape(T, D)
    qry = (ht @ w_query).reshape(T, PEER_HEADS, 2, PEER_DQ // 2)
    s_half = jnp.einsum('thpd,hpnd->thpn', qry, sub_keys, preferred_element_type=jnp.float32)
    v_half, i_half = lax.top_k(s_half, K)
    cand = v_half[:, :, 0, :, None] + v_half[:, :, 1, None, :]
    cand_idx = i_half[:, :, 0, :, None] * PEER_NKEYS + i_half[:, :, 1, None, :]
    top_s, top_pos = lax.top_k(cand.reshape(T, PEER_HEADS, K * K), K)
    experts = jnp.take_along_axis(cand_idx.reshape(T, PEER_HEADS, K * K), top_pos, axis=-1)
    gates = jax.nn.softmax(top_s, axis=-1)
    nchunk = T // PEER_TOK_CHUNK

    def one_chunk(args):
        x_c, e_c, g_c = args
        u = expert_u[e_c]
        act = jax.nn.gelu(jnp.einsum('td,thkd->thk', x_c, u), approximate=False)
        wgt = (g_c * act.astype(jnp.float32)).astype(x_c.dtype)
        return jnp.einsum('thk,thkd->td', wgt, expert_v[e_c])

    out = lax.map(one_chunk, (ht.reshape(nchunk, PEER_TOK_CHUNK, D),
                              experts.reshape(nchunk, PEER_TOK_CHUNK, PEER_HEADS, K),
                              gates.reshape(nchunk, PEER_TOK_CHUNK, PEER_HEADS, K)))
    return out.reshape(B, S, D)

def setup_inputs(seed: int = 0) -> dict:
    key = jax.random.key(seed)
    ks = jax.random.split(key, 24)
    f32 = jnp.float32

    def nrm(k, shape, scale):
        return jax.random.normal(k, shape, f32) * scale

    def gain(k, shape):
        return 1.0 + 0.02 * jax.random.normal(k, shape, f32)

    dt = jnp.exp(jax.random.uniform(ks[13], (DEPTH, GDN_HEADS), f32, minval=jnp.log(1e-3), maxval=jnp.log(1e-1)))
    positions = (jax.random.randint(ks[2], (BATCH, 1), 0, 1024, dtype=jnp.int32)
                 + jnp.arange(SEQ, dtype=jnp.int32)[None, :])
    return {
        'x': nrm(ks[0], (BATCH, SEQ, D_MODEL), 1.0),
        'c': nrm(ks[1], (BATCH, D_MODEL), 1.0),
        'positions': positions,
        'w_mod': nrm(ks[3], (DEPTH, D_MODEL, 6 * D_MODEL), 0.5 * D_MODEL ** -0.5),
        'b_mod': nrm(ks[4], (DEPTH, 6 * D_MODEL), 0.02),
        'w_in': nrm(ks[5], (DEPTH, D_MODEL, IN_COLS), D_MODEL ** -0.5),
        'mla_q_gain': gain(ks[6], (DEPTH, MLA_Q_RANK)),
        'mla_w_uq': nrm(ks[7], (DEPTH, MLA_Q_RANK, MLA_HEADS * MLA_QK), MLA_Q_RANK ** -0.5),
        'mla_kv_gain': gain(ks[8], (DEPTH, MLA_KV_RANK)),
        'mla_w_ukv': nrm(ks[9], (DEPTH, MLA_KV_RANK, MLA_HEADS * (MLA_NOPE + MLA_V)), MLA_KV_RANK ** -0.5),
        'mla_qn_gain': gain(ks[10], (DEPTH, MLA_QK)),
        'mla_kn_gain': gain(ks[11], (DEPTH, MLA_QK)),
        'gdn_conv_w': nrm(ks[12], (DEPTH, GDN_CONV, GDN_CONV_CH), GDN_CONV ** -0.5),
        'gdn_a_log': jnp.log(jax.random.uniform(ks[14], (DEPTH, GDN_HEADS), f32, minval=1.0, maxval=16.0)),
        'gdn_dt_bias': dt + jnp.log(-jnp.expm1(-dt)),
        'gdn_o_gain': gain(ks[15], (DEPTH, GDN_DV)),
        'moba_qn_gain': gain(ks[16], (DEPTH, MOBA_DH)),
        'moba_kn_gain': gain(ks[17], (DEPTH, MOBA_DH)),
        'w_branch': nrm(ks[18], (DEPTH, N_BRANCH, BRANCH_W, D_MODEL), BRANCH_W ** -0.5),
        'w_out': nrm(ks[19], (DEPTH, D_MODEL, D_MODEL), D_MODEL ** -0.5),
        'peer_w_query': nrm(ks[20], (DEPTH, D_MODEL, PEER_HEADS * PEER_DQ), D_MODEL ** -0.5),
        'peer_sub_keys': nrm(ks[21], (DEPTH, PEER_HEADS, 2, PEER_NKEYS, PEER_DQ // 2), (PEER_DQ // 2) ** -0.5),
        'peer_u': nrm(ks[22], (DEPTH, PEER_EXPERTS, D_MODEL), D_MODEL ** -0.5),
        'peer_v': nrm(ks[23], (DEPTH, PEER_EXPERTS, D_MODEL), PEER_HEADS ** -0.5),
    }

def reference(x, c, positions, w_mod, b_mod, w_in, mla_q_gain, mla_w_uq, mla_kv_gain, mla_w_ukv,
              mla_qn_gain, mla_kn_gain, gdn_conv_w, gdn_a_log, gdn_dt_bias, gdn_o_gain,
              moba_qn_gain, moba_kn_gain, w_branch, w_out, peer_w_query, peer_sub_keys,
              peer_u, peer_v):
    B, S, D = x.shape
    c_act = jax.nn.silu(c)
    for l in range(DEPTH):
        mod = c_act @ w_mod[l] + b_mod[l]
        sh_a, sc_a, g_a, sh_f, sc_f, g_f = jnp.split(mod, 6, axis=-1)
        h = modulate(x, sh_a, sc_a)
        (cq, ckv, k_rope, gq, gk, gv, gz, ga, gb,
         mq, mk, mv, gate_logits) = jnp.split(h @ w_in[l], SPLIT_POINTS, axis=-1)
        o_mla = mla_branch(cq, ckv, k_rope, positions, mla_q_gain[l], mla_w_uq[l], mla_kv_gain[l],
                           mla_w_ukv[l], mla_qn_gain[l], mla_kn_gain[l])
        o_gdn = gdn_branch(gq, gk, gv, gz, ga, gb, gdn_conv_w[l], gdn_a_log[l], gdn_dt_bias[l], gdn_o_gain[l])
        o_moba = moba_branch(mq, mk, mv, moba_qn_gain[l], moba_kn_gain[l])
        branches = jnp.stack([o_mla, o_gdn, o_moba], axis=2)
        proj = jnp.einsum('bsnw,nwd->bsnd', branches, w_branch[l])
        gates = jax.nn.sigmoid(gate_logits.reshape(B, S, N_BRANCH, D))
        y = jnp.einsum('bsnd,bsnd->bsd', gates, proj) @ w_out[l]
        x = x + g_a[:, None, :] * y
        h2 = modulate(x, sh_f, sc_f)
        x = x + g_f[:, None, :] * peer_ffn(h2, peer_w_query[l], peer_sub_keys[l], peer_u[l], peer_v[l])
    return x


_drawn_inputs = setup_inputs


def setup_inputs(seed=0):
    import zlib

    import numpy as np

    out = dict(_drawn_inputs(seed))
    spreads = {}
    factors = {'mla_q_gain': 8.0,
     'mla_kv_gain': 8.0,
     'mla_qn_gain': 8.0,
     'mla_kn_gain': 8.0,
     'gdn_o_gain': 8.0,
     'moba_qn_gain': 8.0,
     'moba_kn_gain': 8.0}
    for name, (base, spread) in spreads.items():
        noise = np.random.default_rng([zlib.crc32(name.encode()), seed]).standard_normal(out[name].shape)
        drawn = base * np.exp(spread * noise) if base else spread * noise
        out[name] = jnp.asarray(drawn.astype(out[name].dtype))
    for name, factor in factors.items():
        out[name] = (out[name] * factor).astype(out[name].dtype)
    return out
```

```python
from contextlib import ExitStack

import numpy as np

import concourse.bass as bass
from concourse import mybir

F32 = mybir.dt.float32
F32R = mybir.dt.float32r
BF16 = mybir.dt.bfloat16
U32 = mybir.dt.uint32
ALU = mybir.AluOpType
ACT = mybir.ActivationFunctionType
AX = mybir.AxisListType.X

P = 128
D = 1024
T = 256
NT = T // P
DEPTH = 2
KD = D // P
H = 8
HC = H // 2
EPS = 1e-6
NEG = -1e30
QR, KVR, ROPE, NOPE, MV = 256, 128, 32, 64, 64
QK = NOPE + ROPE
CH = 64
LEVELS = (1, 2, 4, 8, 16, 32)
NK, TOPK = 128, 16
BLK = 8 * P

PAIR_CKV, PAIR_GK, PAIR_GQ, PAIR_GV, PAIR_CQ = 0, 1, 3, 5, 7
PAIR_UKV, PAIR_UQ, PAIR_MQ, PAIR_MK, PAIR_MV, PAIR_Z = 8, 9, 10, 12, 14, 16
PAIR_BR = 18
PAIR_OUT = 36
PAIR_QRY = 40
PAIR_U = 48
PAIR_V = 112
PAIRS = 176
RING = 4

SMALL = {}
_at = 0
for _n, _w in (("conv", 48), ("q_gain", 2), ("kv_gain", 1), ("mq_gain", 1), ("mk_gain", 1), ("o_gain", 1),
               ("b_mod", 48), ("qn_row", QK), ("kn_row", QK), ("dt_row", H), ("alog_row", H)):
    SMALL[_n] = (_at, _at + _w)
    _at += _w
NSMALL = _at


def schedule():
    g = []
    for t in range(NT):
        g += [("decay", t), ("build", t)] + [("level", (t, s)) for s in LEVELS[1:]] + [("uw", t)]
    g += [("chunk", n) for n in range(T // CH)]
    a = [("proj", PAIR_MQ), ("proj", PAIR_MQ + 1), ("mnorm", 0), ("proj", PAIR_MK), ("proj", PAIR_MK + 1),
         ("mnorm", 1), ("proj", PAIR_MV), ("proj", PAIR_MV + 1), ("mlakv", 0), ("mlaq", 0), ("mlaT", 0),
         ("proj", PAIR_Z), ("proj", PAIR_Z + 1)]
    a = [("mlakv", 0), ("mlaq", 0)] + [x for x in a if x[0] not in ("mlakv", "mlaq")]
    a += [("head", i) for i in range(2 * H + 3)]
    out, n = [], 0
    for i, x in enumerate(g):
        out.append(x)
        while n < len(a) * (i + 1) // len(g):
            out.append(a[n])
            n += 1
    return out + a[n:]


SCHEDULE = schedule()


class Steps:

    def __init__(self, eng, sem):
        self.eng, self.sem, self.n = eng, sem, 0

    def __call__(self, ins):
        self.n += 1
        ins.then_inc(self.sem, 1)
        return self.n

    def done(self, n=None):
        self.eng.wait_ge(self.sem, self.n if n is None else n)


def build(nc, xT, cT, pos, invf, stream, modw, small, subk, spill, out):
    with ExitStack() as ctx:
        def sb(name, n, dt=F32):
            return ctx.enter_context(nc.sbuf_tensor(name, [P, n], dt))

        sems = []

        def sem(name):
            s = ctx.enter_context(nc.semaphore(name))
            sems.append(s)
            return s

        def twin(name, n):
            t = sb(name, n)
            return t, nc.alloc_sbuf_tensor_at(name + "_r", [P, n], F32R, offset=nc.sbuf_base - 4 * n)

        X, X_r = twin("X", KD * T)
        HT, HT_r = twin("HT", KD * T)
        ring, ring_r = zip(*[twin(f"ring{i}", 2 * BLK) for i in range(RING)])
        arena = sb("arena", P * T)
        ident = sb("ident", P)
        ones = sb("ones", P)
        iota = sb("iota", P)
        cst = sb("cst", 4)
        sml = sb("sml", NSMALL)
        modc = sb("modc", 6 * KD)
        cact = sb("cact", 2 * KD)
        rope = sb("rope", 2 * NT * 16)
        upper, upper_r = twin("upper", 4 * BLK)
        route_ = sb("route", 2176)
        tiny_f = sb("tiny_f", 64)

        def A(at, n):
            return arena[:, at:at + n]

        def col(name, i=0, n=1):
            a, _ = SMALL[name]
            return sml[:, a + i:a + i + n]

        x3 = X[:, :].rearrange("p (k t) -> p k t", k=KD)
        h3 = HT[:, :].rearrange("p (k t) -> p k t", k=KD)
        MODR = [A(2048 * i, 2048) for i in range(3)]
        ACC = A(6144, 1024)
        PRE = A(7168, 12 * 260).rearrange("p (c t) -> p c t", c=12)
        AM, TM, UM, YM, CM = (A(1024 * i, 1024).rearrange("p (g c j) -> p g c j", g=2, c=HC) for i in range(5))
        ATT = [A(5120 + 1024 * i, 1024).rearrange("p (g c j) -> p g c j", g=2, c=HC) for i in range(NT)]
        KBG = A(7168, 1024).rearrange("p (t n) -> p t n", t=NT)
        VB = A(8192, 1024).rearrange("p (t n) -> p t n", t=NT)
        KDEC = A(9216, 1024).rearrange("p (t n) -> p t n", t=NT)
        CONV = A(10288, 3072).rearrange("p (c t) -> p c t", c=12)
        KT, QT, VT = CONV[:, 0:4], CONV[:, 4:8], CONV[:, 8:12]
        QG = A(13360, 1024).rearrange("p (c t) -> p c t", c=HC)
        UV = A(14384, 1024).rearrange("p (t n) -> p t n", t=NT)
        ZS = A(15408, 1024).rearrange("p (c t) -> p c t", c=HC)
        CQ = A(16432, 512).rearrange("p (c t) -> p c t", c=2)
        CKV = A(16944, 256)
        MISC = A(17200, 256)
        MQ = A(17456, 1024).rearrange("p (c t) -> p c t", c=HC)
        MK = A(18480, 1024).rearrange("p (c t) -> p c t", c=HC)
        MVT = A(19504, 1024).rearrange("p (t n) -> p t n", t=NT)
        QTOK = A(20528, 1536).rearrange("p (t n) -> p t n", t=NT)
        KVTOK = A(22064, 2048).rearrange("p (t n) -> p t n", t=NT)
        QTH = A(24112, 2048).rearrange("p (h t) -> p h t", h=H)
        KTH = A(26160, 2048).rearrange("p (h t) -> p h t", h=H)
        PB = [A(28208 + 384 * i, 384) for i in range(3)]
        PTB = [A(28208 + 1152 + 384 * i, 384) for i in range(2)]
        KFULL = A(28208, 1536).rearrange("p (t n) -> p t n", t=NT)
        TA, TB = A(30128, 1024), A(31152, 1024)
        WT = TA.rearrange("p (t c j) -> p t c j", t=NT, c=HC)
        O_MLA = QTOK.rearrange("p t n -> p (t n)")[:, 0:1024].rearrange("p (c t) -> p c t", c=HC)
        O_MOBA = A(16432, 1024).rearrange("p (c t) -> p c t", c=HC)
        O_GDN = VT
        MERGED = A(24112, 2048).rearrange("p (k t) -> p k t", k=KD)
        GATE = [A(26160 + 512 * i, 512) for i in range(4)]
        XSQ, XSUM, XRSTD = A(24112, 2048), A(26160, 256), A(26416, 256)
        sp = [32176]

        def tiny(n):
            a = A(sp[0], n)
            sp[0] += n
            assert sp[0] <= 32768
            return a

        MT = tiny(NT * 48).rearrange("p (t n) -> p t n", t=NT)
        G1, G2, G3, GG, BETA, EGC, EDEC, EB = (tiny(NT * H).rearrange("p (t n) -> p t n", t=NT) for _ in range(8))
        GCL = tiny(NT * 16).rearrange("p (t n) -> p t n", t=NT)
        NEGA = tiny(H)
        SSQ, SSK = (tiny(NT * H).rearrange("p (t n) -> p t n", t=NT) for _ in range(2))
        SSPE = tiny(NT)
        PESQ = tiny(NT * ROPE).rearrange("p (t n) -> p t n", t=NT)
        KPG = tiny(NT * ROPE).rearrange("p (t n) -> p t n", t=NT)
        KROPE = tiny(NT * ROPE).rearrange("p (t n) -> p t n", t=NT)
        MX, NM, RS, RI = (tiny(3 * 2).rearrange("p (b t) -> p b t", b=3) for _ in range(4))
        EGL = tiny(HC * 4).rearrange("p (c n) -> p c n", c=HC)
        ST = upper[:, 0:512].rearrange("p (c j) -> p c j", c=HC)
        EGB = upper[:, 512:2560].rearrange("p (g c t) -> p g c t", g=2, c=HC)
        same = upper[:, 2560:2688]
        strict = upper[:, 2688:2816]
        incl = upper[:, 2816:2944]
        cmask = upper[:, 2944:3328]
        lmask = upper[:, 3328:3328 + len(LEVELS) * P]
        SK = A(0, 2048).rearrange("p (h j n) -> p h j n", h=H, j=2)
        QRY = [A(24576 + 512 * i, 512).rearrange("p (j t) -> p j t", j=2) for i in range(2)]
        TV = A(25600, 512).rearrange("p (t j h k) -> p t j h k", t=NT, j=2, h=H)
        TI = A(26112, 512).bitcast(U32).rearrange("p (t j h k) -> p t j h k", t=NT, j=2, h=H)
        TS = A(26624, 256).rearrange("p (t h k) -> p t h k", t=NT, h=H)
        TP = A(26880, 256).bitcast(U32).rearrange("p (t n) -> p t n", t=NT)
        WORK = [A(27136 + 128 * i, 128) for i in range(4)]
        CAND = A(27648, 512).rearrange("p (t n) -> p t n", t=NT)
        CWORK = A(28160, 512).rearrange("p (t n) -> p t n", t=NT)
        EQ = A(28672, 2048).rearrange("p (h k a) -> p h k a", h=H, k=TOPK)
        TAB = A(30720, 512).rearrange("p (j n) -> p j n", j=2)
        TABU = A(31232, 512).bitcast(U32).rearrange("p (j n) -> p j n", j=2)
        TIF = A(31744, 512).rearrange("p (t j h k) -> p t j h k", t=NT, j=2, h=H)
        IDX = A(32256, 512).rearrange("p (t j n) -> p t j n", t=NT, j=2)
        SM1 = tiny_f[:, 0:NT * H].rearrange("p (t h) -> p t h", t=NT)
        SM2 = tiny_f[:, 16:32].rearrange("p (t h) -> p t h", t=NT)
        IDXT = route_[:, 0:2 * T].rearrange("p (j t) -> p j t", j=2)
        GATES = route_[:, 512:896].bitcast(BF16).rearrange("p (t j) -> p t j", j=3)
        GRP = 4
        TOK = 2 * GRP
        EH = NK // 2
        OHA = [route_[:, 896 + 256 * i:1152 + 256 * i].bitcast(BF16).rearrange("p (t n) -> p t n", t=GRP) for i in range(2)]
        OHB = [route_[:, 1408 + 384 * i:1792 + 384 * i].bitcast(BF16).rearrange("p (t j n) -> p t j n", t=GRP, j=3)
               for i in range(2)]
        GREST = route_[:, 1408:1664]
        I1C = [tiny_f[:, 32 + GRP * i:32 + GRP * (i + 1)] for i in range(2)]
        I1D = [tiny_f[:, 40 + GRP * i:40 + GRP * (i + 1)] for i in range(2)]
        UP = [upper_r[:, BLK * i:BLK * (i + 1)].rearrange("p (k n) -> p k n", k=8) for i in range(4)]
        LOW = [[ring_r[s][:, BLK * b:BLK * (b + 1)].rearrange("p (k n) -> p k n", k=8) for b in range(2)]
               for s in range(RING)]
        HUP = X_r[:, :].rearrange("p (k t) -> p k t", k=KD)
        HLOW = HT_r[:, :].rearrange("p (k t) -> p k t", k=KD)
        AUP = [HT_r[:, 1024 * i:1024 * i + 512] for i in range(2)]
        ALOW = [HT_r[:, 1024 * i + 512:1024 * i + 1024] for i in range(2)]
        act3 = arena[:, :].rearrange("p (e t) -> p e t", e=P)

        bank = [ctx.enter_context(nc.psum_tensor(f"bank{i}", [P, 512], F32)) for i in range(8)]
        PT, SB = bank[:2], bank[2:]

        mod_landed = [sem(f"mod_landed{i}") for i in range(3)]
        s_load = sem("first_loads")
        s_sml = sem("small_loaded")
        s_cst = sem("constants_built")
        s_pro = sem("prologue_done")
        first_sem = len(sems)
        landed = [sem(f"pair_landed{i}") for i in range(RING)]
        begun = sem("pair_begun")
        mod_used = sem("mod_pair_used")
        block_begun = sem("split_block_begun")
        up_ready = sem("upper_halves_ready")
        low_pool = sem("lower_halves_by_gpsimd")
        low_dve = sem("lower_halves_by_vector")
        aup_ready, alow_ready = sem("activations_upper"), sem("activations_lower")
        spilled, reloaded = sem("x_in_dram"), sem("x_back")
        i1_ready = sem("i1_copied")
        mod_acc = sem("mod_partial_ready")
        mod_done = sem("mod_columns_ready")
        p_ready = sem("streamed_product_ready")
        p_evac = sem("streamed_product_taken")
        side_ready = [sem(f"bank{i}_ready") for i in range(6)]
        side_free = [sem(f"bank{i}_free") for i in range(6)]
        c_dve, c_act, c_pool = sem("dve_steps"), sem("act_steps"), sem("pool_steps")
        E = {}
        for n in ("xsq", "xsum", "xstd", "h", "conv", "silu", "gsq", "gstd", "gnorm", "cstd", "cnorm", "csq",
                  "misc", "spa", "spe", "spl", "g", "gcl", "egc", "egb", "diff", "decay", "att", "a", "tok", "t", "u", "y", "cm",
                  "uw", "wt", "vnew", "state", "qg", "msq", "mstd", "mnorm", "qtok", "kvtok", "qksq", "qkss", "qkstd",
                  "qkfull", "qkT", "pmask", "pexp", "pnorm", "pT", "o", "zs", "gate", "branch", "merged", "x",
                  "osq", "ostd", "ognorm", "qry", "topd", "tope", "idx", "idxT", "ohb", "oha", "wready", "wdone",
                  "sk", "vdone", "zero", "masks", "hup", "hsplit"):
            E[n] = sem("e_" + n)
        last_sem = len(sems)

        with nc.Block() as block:
            @block.sync
            def _(sp_):
                sp_.dma_start(X[:, :], xT).then_inc(s_load, 16)
                sp_.dma_start(cact[:, 0:KD], cT).then_inc(s_load, 16)
                sp_.dma_start(rope[:, 0:16], invf).then_inc(s_load, 16)
                sp_.dma_start(TA[:, 0:NT].bitcast(mybir.dt.int32), pos).then_inc(s_load, 16)
                sp_.wait_ge(s_load, 64)

            @block.gpsimd
            def _(g):
                st = Steps(g, c_pool)
                for t, v in ((ident, 0.0), (ones, 1.0), (cst, 1.0)):
                    st(g.memset(t[:, :], v))
                st(g.iota(iota[:, :], [[1, P]], base=0, channel_multiplier=0, allow_small_or_imprecise_dtypes=True))
                st.done()
                st(g.memset(cst[:, 0:1], EPS))
                st(g.memset(cst[:, 1:2], 64 * EPS))
                st(g.affine_select(out=ident[:, :], in_=ident[:, :], compare_op=ALU.not_equal, fill=1.0, base=0,
                                   pattern=[[-1, P]], channel_multiplier=1))
                st.done()

            @block.vector
            def _(v):
                st = Steps(v, c_dve)
                v.wait_ge(s_load, 64)
                ang = TB[:, 0:64].rearrange("p (w t f) -> p w t f", w=2, t=NT)
                k = TB[:, 64:128].rearrange("p (w t f) -> p w t f", w=2, t=NT)
                st(v.tensor_copy(TA[:, 8:8 + NT], TA[:, 0:NT].bitcast(mybir.dt.int32)))
                st.done()
                for w in range(2):
                    for t in range(NT):
                        st(v.tensor_scalar(ang[:, w, t], rope[:, 0:16], TA[:, 8 + t:9 + t], None, ALU.mult))
                st.done()
                half = float(np.float32(np.pi / 2))
                for w in range(2):
                    st(v.tensor_scalar(k[:, w], ang[:, w], half if w == 0 else 0.0, 1.0 / (2 * np.pi), ALU.add, ALU.mult))
                st.done()
                st(v.tensor_scalar(k[:, :], k[:, :], 12582912.0, -12582912.0, ALU.add, ALU.add))
                st.done()
                c1 = 6.28125
                c2 = round((2 * np.pi - c1) * 2 ** 20) / 2 ** 20
                c3 = float(2 * np.pi - c1 - c2)
                for c in (c1, c2, c3):
                    st(v.scalar_tensor_tensor(ang[:, :], k[:, :], -c, ang[:, :], ALU.mult, ALU.add))
                    st.done()
                st(v.tensor_scalar(ang[:, 0], ang[:, 0], half, None, ALU.add))
                st.done()
                v.tensor_scalar(ang[:, :], ang[:, :], 3.1415925, -3.1415925, ALU.min, ALU.max).then_inc(s_cst, 1)

            @block.scalar
            def _(a):
                a.wait_ge(s_load, 64)
                a.activation(cact[:, KD:2 * KD], cact[:, 0:KD], ACT.Silu).then_inc(s_pro, 1)
                a.wait_ge(s_cst, 1)
                a.activation(rope[:, :], TB[:, 0:64], ACT.Sin).then_inc(s_pro, 1)

        nc.multi_engine_barrier(list(mybir.ALL_ENGINES),
                                sems_to_clear=range(s_load.num, sems[-1].num + 1))

        COS = rope[:, 0:NT * 16].rearrange("p (t f) -> p t f", t=NT)
        SIN = rope[:, NT * 16:2 * NT * 16].rearrange("p (t f) -> p t f", t=NT)

        with nc.Fori(0, DEPTH) as layer:
            with nc.Block() as block:
                jobs = {}
                njobs = [0]

                def take(eng, name):
                    b, n = jobs[name]
                    eng.wait_ge(side_ready[b], n)
                    return SB[b], side_free[b]

                def freed(eng, name):
                    b, n = jobs[name]
                    eng.wait_ge(side_free[b], n)

                def qk_transposed(eng):
                    for t in range(NT):
                        for j in range(2):
                            freed(eng, f"T0{t}{j}")
                            freed(eng, f"T1{t}{j}")

                prod = {}
                for p in ([*range(0, 8)] + [p for k, p in SCHEDULE if k == "proj"]
                          + [PAIR_BR + 6 * b + 3 * j + i for b in range(3) for j in range(2) for i in range(2)]
                          + [*range(PAIR_QRY, PAIR_QRY + 8)]):
                    prod[p] = len(prod)
                NPROD = len(prod)
                NPOOL = 2 * (PAIR_U + NK // 4 - PAIR_QRY)
                VB0 = 2 * (PAIR_V - PAIR_QRY)
                UH = EH // 2
                assert NPROD % 2 == 0

                @block.tensor
                def _(pe):
                    def side(name):
                        b, n = njobs[0] % 6, njobs[0] // 6
                        njobs[0] += 1
                        if n:
                            pe.wait_ge(side_free[b], n)
                        jobs[name] = (b, n + 1)
                        return SB[b], side_ready[b]

                    def pair_in(p):
                        pe.wait_ge(landed[p % RING], 16 * (p // RING + 1))
                        return ring[p % RING][:, :].rearrange("p (b k n) -> p b k n", b=2, k=8)

                    def project(p, token_major=False):
                        w = pair_in(p)
                        n = prod[p]
                        if n >= 2:
                            pe.wait_ge(p_evac, n - 1)
                        o = PT[n % 2]
                        first = True
                        for b in range(2):
                            for t in range(NT if token_major else 1):
                                for k in range(KD):
                                    if token_major:
                                        mm = pe.matmul(o[:, (2 * b + t) * P:(2 * b + t + 1) * P],
                                                       h3[:, k, t * P:(t + 1) * P], w[:, b, k], start=k == 0, stop=k == 7)
                                    else:
                                        mm = pe.matmul(o[:, b * T:(b + 1) * T], w[:, b, k], h3[:, k], start=k == 0, stop=k == 7)
                                    if first:
                                        mm.then_inc(begun, 1)
                                        first = False
                        mm.then_inc(p_ready, 1)

                    def modsum(m):
                        pe.wait_ge(mod_acc, m + 1)
                        o, rdy = side(f"mod{m}")
                        for j in range(KD):
                            mm = pe.matmul(o[:, j:j + 1], ACC[:, j * P:(j + 1) * P], ones[:, 0:1], start=True, stop=True)
                        mm.then_inc(rdy, 1)

                    def mm1(name, lhsT, rhs, n):
                        o, rdy = side(name)
                        pe.matmul(o[:, 0:n], lhsT, rhs, start=True, stop=True).then_inc(rdy, 1)

                    modsum(0)
                    modsum(1)
                    pe.wait_ge(E["xsum"], 1)
                    mm1("xss0", ones[:, :], XSUM, T)
                    pe.wait_ge(E["h"], 1)
                    project(0)
                    project(1)
                    project(2)
                    modsum(2)
                    project(3)
                    project(4)
                    modsum(3)
                    project(5)
                    project(6)
                    modsum(4)
                    pe.wait_ge(p_evac, 1)
                    o, rdy = side("misc")
                    for t in range(NT):
                        mm = pe.transpose(o[:, t * 48:(t + 1) * 48], MISC[0:48, t * P:(t + 1) * P], ident[0:48, 0:48])
                    mm.then_inc(rdy, 1)
                    project(PAIR_CQ)
                    modsum(5)
                    pe.wait_ge(E["csq"], 1)
                    o, rdy = side("css")
                    for c in range(2):
                        pe.matmul(o[:, 0:T], ones[:, :], TA[:, c * T:(c + 1) * T], start=c == 0, stop=c == 1)
                    pe.matmul(o[:, T:2 * T], ones[:, :], TA[:, 2 * T:3 * T], start=True, stop=True).then_inc(rdy, 1)
                    pe.wait_ge(E["masks"], 1)
                    for i in range(2):
                        pe.wait_ge(E["gsq"], i + 1)
                        for j in range(2):
                            mm1(f"gss{i}{j}", same, TB[:, j * 512:(j + 1) * 512], 512)
                    pe.wait_ge(E["g"], 1)
                    o, rdy = side("gcl")
                    for t in range(NT):
                        pe.matmul(o[:, t * 16:t * 16 + 8], incl, GG[:, t], start=True, stop=True)
                        mm = pe.matmul(o[:, t * 16 + 8:t * 16 + 16], same, GG[:, t], start=True, stop=True)
                    mm.then_inc(rdy, 1)
                    for name, src, ev, n in (("k", KT, "gnorm", 1), ("v", VT, "silu", 3)):
                        pe.wait_ge(E[ev], n)
                        for t in range(NT):
                            o, rdy = side(f"tok{name}{t}")
                            for c in range(HC):
                                mm = pe.transpose(o[:, c * P:(c + 1) * P], src[:, c, t * P:(t + 1) * P], ident[:, :])
                            mm.then_inc(rdy, 1)

                    def half(par):
                        return slice(par * CH, par * CH + CH)

                    def head_step(i):
                        if i < 2 * H:
                            o, rdy = side(f"S{i}")
                            if i < H:
                                if i == 0:
                                    qk_transposed(pe)
                                q, k = QTH[0:QK, i], KTH[0:QK, i]
                            else:
                                if i == H:
                                    pe.wait_ge(E["mnorm"], 2)
                                h = i - H
                                q, k = MQ[half(h % 2), h // 2], MK[half(h % 2), h // 2]
                            pe.matmul(o[:, 0:P], q[:, 0:P], k[:, 0:P], start=True, stop=True)
                            pe.matmul(o[:, P:3 * P], q[:, P:T], k[:, 0:T], start=True, stop=True).then_inc(rdy, 1)
                        i2 = i - 2
                        if 0 <= i2 < 2 * H:
                            pe.wait_ge(E["pnorm"], i2 + 1)
                            o, rdy = side(f"PT{i2}")
                            for b in range(3):
                                mm = pe.transpose(o[:, b * P:(b + 1) * P], PB[i2 % 3][:, b * P:(b + 1) * P], ident[:, :])
                            mm.then_inc(rdy, 1)
                        i3 = i - 3
                        if 0 <= i3 < 2 * H:
                            freed(pe, f"PT{i3}")
                            if i3 == H:
                                pe.wait_ge(p_evac, prod[PAIR_MV + 1] + 1)
                            o, rdy = side(f"O{i3}")
                            oo = o[half(i3 % 2), :]
                            for t in range(NT):
                                v = (KVTOK[:, t, i3 * P + NOPE:(i3 + 1) * P] if i3 < H
                                     else MVT[:, t, (i3 - H) * CH:(i3 - H + 1) * CH])
                                src = PTB[i3 % 2][:, 0:T] if t == 0 else PTB[i3 % 2][:, T:T + P]
                                mm = pe.matmul(oo[:, t * P:T], v, src, start=t == 0, stop=t == 1, skip_group_check=True)
                            mm.then_inc(rdy, 1)

                    for kind, i in SCHEDULE:
                        if kind == "proj":
                            project(i, token_major=i in (PAIR_MV, PAIR_MV + 1))
                        elif kind == "mnorm":
                            pe.wait_ge(E["msq"], i + 1)
                            for j in range(2):
                                mm1(f"mss{i}{j}", same, TB[:, j * 512:(j + 1) * 512], 512)
                        elif kind == "mlakv":
                            w = pair_in(PAIR_UKV)
                            pe.wait_ge(E["cnorm"], 1)
                            for t in range(NT):
                                for j in range(2):
                                    o, rdy = side(f"kv{t}{j}")
                                    for k in range(2):
                                        mm = pe.matmul(o[:, k * T:(k + 1) * T], CKV[:, t * P:(t + 1) * P],
                                                       w[:, 0, 4 * j + 2 * k:4 * j + 2 * k + 2].rearrange("p k n -> p (k n)"),
                                                       start=True, stop=True)
                                        if t == j == k == 0:
                                            mm.then_inc(begun, 1)
                                    mm.then_inc(rdy, 1)
                        elif kind == "mlaq":
                            w = [pair_in(PAIR_UQ)[:, c].rearrange("p k n -> p (k n)") for c in range(2)]
                            for t in range(NT):
                                for j in range(2):
                                    o, rdy = side(f"q{t}{j}")
                                    n = 512 if j == 0 else 256
                                    for c in range(2):
                                        mm = pe.matmul(o[:, 0:n], CQ[:, c, t * P:(t + 1) * P], w[c][:, 512 * j:512 * j + n],
                                                       start=c == 0, stop=c == 1)
                                        if t == j == c == 0:
                                            mm.then_inc(begun, 1)
                                    mm.then_inc(rdy, 1)
                        elif kind == "mlaT":
                            for n, src in enumerate((QTOK, KFULL)):
                                pe.wait_ge(E["qkfull"], n + 1)
                                for t in range(NT):
                                    for j in range(2):
                                        o, rdy = side(f"T{n}{t}{j}")
                                        for h in range(4):
                                            a = (4 * j + h) * QK
                                            mm = pe.transpose(o[0:QK, h * P:(h + 1) * P], src[:, t, a:a + QK], ident[:, :])
                                        mm.then_inc(rdy, 1)
                        elif kind == "head":
                            head_step(i)
                        elif kind == "decay":
                            for par in range(2):
                                o, rdy = side(f"gcb{i}{par}")
                                for c in range(HC):
                                    h = 2 * c + par
                                    mm = pe.matmul(o[:, c * P:(c + 1) * P], GG[:, i, h:h + 1].to_broadcast([P, P]), incl,
                                                   start=True, stop=True)
                                mm.then_inc(rdy, 1)
                        elif kind == "build":
                            t = slice(i * P, (i + 1) * P)
                            pe.wait_ge(E["gnorm"], 2)
                            for name, b in (("G", QT), ("G", KT))[::-1]:
                                for par in range(2):
                                    o, rdy = side(f"{'GK' if b is KT else 'GQ'}{i}{par}")
                                    for c in range(HC):
                                        mm = pe.matmul(o[:, c * P:(c + 1) * P], KT[half(par), c, t], b[half(par), c, t],
                                                       start=True, stop=True)
                                    mm.then_inc(rdy, 1)
                            pe.wait_ge(E["cm"], len(LEVELS) * i + 1)
                            for par in range(2):
                                o, rdy = side(f"Y{i}{1}{par}")
                                for c in range(HC):
                                    mm = pe.matmul(o[:, c * P:(c + 1) * P], CM[:, par, c], ident[:, :], start=True, stop=True)
                                mm.then_inc(rdy, 1)
                        elif kind == "level":
                            t, s = i
                            n = len(LEVELS) * t + LEVELS.index(s)
                            pe.wait_ge(E["cm"], n + 1)
                            pe.wait_ge(E["u"], n)
                            for par in range(2):
                                o, rdy = side(f"Y{t}{s}{par}")
                                for c in range(HC):
                                    mm = pe.matmul(o[:, c * P:(c + 1) * P], CM[:, par, c], UM[:, par, c], start=True, stop=True)
                                mm.then_inc(rdy, 1)
                            pe.wait_ge(E["y"], (len(LEVELS) - 1) * t + LEVELS.index(s))
                            pe.wait_ge(E["t"], (len(LEVELS) - 1) * t + LEVELS.index(s))
                            for par in range(2):
                                o, rdy = side(f"U{t}{s}{par}")
                                for c in range(HC):
                                    mm = pe.matmul(o[:, c * P:(c + 1) * P], TM[:, par, c], YM[:, par, c], start=True, stop=True)
                                mm.then_inc(rdy, 1)
                            if s != LEVELS[-1]:
                                for par in range(2):
                                    o, rdy = side(f"TT{t}{s}{par}")
                                    for c in range(HC):
                                        mm = pe.matmul(o[:, c * P:(c + 1) * P], YM[:, par, c], TM[:, par, c],
                                                       start=True, stop=True)
                                    mm.then_inc(rdy, 1)
                        elif kind == "uw":
                            pe.wait_ge(E["u"], len(LEVELS) * (i + 1))
                            pe.wait_ge(E["tok"], 3 * NT)
                            for par in range(2):
                                o, rdy = side(f"uu{i}{par}")
                                for c in range(HC):
                                    mm = pe.matmul(o[:, c * P:(c + 1) * P], UM[:, par, c], VB[:, i, c * P:(c + 1) * P],
                                                   start=True, stop=True)
                                mm.then_inc(rdy, 1)
                            o, rdy = side(f"wt{i}")
                            for c in range(HC):
                                for par in range(2):
                                    h = 2 * c + par
                                    mm = pe.matmul(o[half(par), c * P:(c + 1) * P], KBG[:, i, h * CH:(h + 1) * CH], UM[:, par, c],
                                                   start=True, stop=True, skip_group_check=True)
                            mm.then_inc(rdy, 1)
                        elif kind == "chunk":
                            n, t, hf = i, i // 2, half(i % 2)
                            cols = slice((i % 2) * CH, (i % 2) * CH + CH)
                            pe.wait_ge(E["state"], n + 1)
                            if n == 0:
                                pe.wait_ge(E["wt"], NT)
                            o, rdy = side(f"ws{n}")
                            for c in range(HC):
                                mm = pe.matmul(o[hf, c * P:(c + 1) * P], WT[:, t, c, cols], ST[:, c], start=True, stop=True)
                            mm.then_inc(rdy, 1)
                            pe.wait_ge(E["vnew"], n + 1)
                            pe.wait_ge(E["qg"], 8)
                            o, rdy = side(f"og{n}")
                            for c in range(HC):
                                pe.matmul(o[:, c * CH:(c + 1) * CH], ST[:, c], QG[:, c, n * CH:(n + 1) * CH],
                                          start=c == 0, stop=False, skip_group_check=True)
                            for c in range(HC):
                                for par in range(2):
                                    h = 2 * c + par
                                    mm = pe.matmul(o[half(par), c * CH:(c + 1) * CH], UV[:, t, h * CH:(h + 1) * CH],
                                                   ATT[t][:, par, c, cols], start=False, stop=True, skip_group_check=True)
                            mm.then_inc(rdy, 1)
                            if n < T // CH - 1:
                                o, rdy = side(f"ds{n}")
                                for c in range(HC):
                                    mm = pe.matmul(o[:, c * P:(c + 1) * P], KDEC[hf, t, c * P:(c + 1) * P],
                                                   UV[hf, t, c * P:(c + 1) * P], start=True, stop=True)
                                mm.then_inc(rdy, 1)
                    pe.wait_ge(E["osq"], 1)
                    for j in range(2):
                        mm1(f"oss{j}", same, TB[:, j * 512:(j + 1) * 512], 512)
                    for b in range(3):
                        for j in range(2):
                            p = PAIR_BR + 6 * b + 3 * j
                            project(p)
                            project(p + 1)
                            w = pair_in(p + 2)
                            src = (O_MLA, O_MOBA, O_GDN)[b]
                            if j == 0:
                                if b == 2:
                                    pe.wait_ge(E["ognorm"], 1)
                                else:
                                    for h in range(H):
                                        freed(pe, f"O{b * H + h}")
                            for i in range(2):
                                o, rdy = side(f"br{b}{j}{i}")
                                for jj in range(2):
                                    for k in range(HC):
                                        mm = pe.matmul(o[:, jj * T:(jj + 1) * T], w[:, i, 4 * jj + k], src[:, k],
                                                       start=k == 0, stop=k == HC - 1)
                                        if i == 0 and jj == 0 and k == 0:
                                            mm.then_inc(begun, 1)
                                mm.then_inc(rdy, 1)
                    pe.wait_ge(E["merged"], 4)
                    for p in range(4):
                        w = pair_in(PAIR_OUT + p)
                        o, rdy = side(f"y{p}")
                        for b in range(2):
                            for k in range(KD):
                                mm = pe.matmul(o[:, b * T:(b + 1) * T], w[:, b, k], MERGED[:, k], start=k == 0, stop=k == 7)
                                if b == 0 and k == 0:
                                    mm.then_inc(begun, 1)
                        mm.then_inc(rdy, 1)
                    pe.wait_ge(E["xsum"], 2)
                    mm1("xss1", ones[:, :], XSUM, T)
                    pe.wait_ge(E["hsplit"], 1)
                    pe.wait_ge(E["sk"], 16)

                    def split_products(slot, b, low_sem, n_low, out_of, up, low, first_of=None):
                        pe.wait_ge(low_sem, n_low)
                        wu, wl = UP[2 * (slot % 2) + b], LOW[slot][b]
                        for k in range(KD):
                            for i, (w, x) in enumerate(((wu, up), (wu, low), (wl, up))):
                                o, start, stop = out_of(k, i)
                                mm = pe.matmul(o, w[:, k], x(k), start=start, stop=stop, skip_group_check=True)
                                if k == 0 and i == 0 and b == 0:
                                    mm.then_inc(begun, 1)
                                if k == 0 and i == 1:
                                    mm.then_inc(block_begun, 1)
                        return mm

                    def against_h(slot, o, low_sem, n_low):
                        for b in range(2):
                            mm = split_products(slot, b, low_sem, n_low + b,
                                                lambda k, i, b=b: (o[:, b * T:(b + 1) * T], k == 0 and i == 0, k == KD - 1 and i == 2),
                                                lambda k: HUP[:, k], lambda k: HLOW[:, k])
                        mm.then_inc(p_ready, 1)

                    for h in range(H + 1):
                        if h < H:
                            p = PAIR_QRY + h
                            pe.wait_ge(p_evac, prod[p] - 1)
                            against_h(p % RING, PT[prod[p] % 2], low_pool, 2 * h + 1)
                        if h:
                            pe.wait_ge(p_evac, prod[PAIR_QRY + h - 1] + 1)
                            o, rdy = side(f"sc{h - 1}")
                            for t in range(NT):
                                for j in range(2):
                                    mm = pe.matmul(o[:, (2 * t + j) * P:(2 * t + j + 1) * P],
                                                   QRY[(h - 1) % 2][:, j, t * P:(t + 1) * P], SK[:, h - 1, j],
                                                   start=True, stop=True)
                            mm.then_inc(rdy, 1)

                    def route(n, slot, n_free):
                        if n_free is not None:
                            pe.wait_ge(E["wdone"], n_free)
                        for s in range(2):
                            pe.wait_ge(E["ohb"], n + s)
                            pe.wait_ge(E["oha"], n + s)
                            for k in range(GRP):
                                a = (GRP * s + k) * EH
                                for j in range(3):
                                    mm = pe.matmul(SB[4 + slot][:, a:a + EH], OHA[s][:, k], OHB[s][:, k, j],
                                                   start=j == 0, stop=j == 2)
                            mm.then_inc(E["wready"], 1)

                    with pe.Fori(0, UH // RING) as i:
                        for s in range(RING):
                            pe.wait_ge(p_evac, RING * i + (NPROD + s - 1))
                            against_h(s, PT[s % 2], low_pool, 8 * i + (2 * H + 2 * s + 1))
                    pe.wait_ge(E["idx"], 1)
                    for t in range(NT):
                        o, rdy = side(f"ix{t}")
                        for j in range(3):
                            src = IDX[:, t, j] if j < 2 else TS[:, t].rearrange("p h k -> p (h k)")
                            mm = pe.transpose(o[:, j * P:(j + 1) * P], src, ident[:, :])
                        mm.then_inc(rdy, 1)
                    for b in range(6):
                        pe.wait_ge(side_free[b], sum(1 for k, _ in jobs.values() if k == b))

                    def u_and_route(i, s, n_free):
                        pe.wait_ge(p_evac, RING * i + (NPROD + UH + s - 1))
                        against_h(s, PT[s % 2], low_dve, 8 * i + (2 * s + 1))
                        route(8 * i + (2 * s + 1), s % 2, n_free)

                    for s in range(RING):
                        u_and_route(0, s, s - 1 if s >= 2 else None)
                    with pe.Fori(1, UH // RING) as i:
                        for s in range(RING):
                            u_and_route(i, s, RING * i + (s - 1))

                    def expert_out(slot, n_low, n_act, first=False, last=False):
                        pe.wait_ge(alow_ready, n_act)
                        for b in range(2):
                            mm = split_products(slot, b, low_dve, n_low + b,
                                                lambda k, i, b=b: (SB[k // 2][:, (k % 2) * T:(k % 2 + 1) * T],
                                                                   first and b == 0 and k % 2 == 0 and i == 0,
                                                                   last and b == 1 and i == 2),
                                                lambda k, b=b: AUP[slot % 2][:, b * T:(b + 1) * T],
                                                lambda k, b=b: ALOW[slot % 2][:, b * T:(b + 1) * T])
                        return mm

                    def v_and_route(i, s, first=False):
                        expert_out(s, 8 * i + (2 * UH + 2 * s + 1), RING * i + (s + 1), first)
                        route(8 * i + (T // GRP + 2 * s + 1), s % 2, RING * i + (T // TOK + s - 1))

                    for s in range(RING):
                        v_and_route(0, s, s == 0)
                    with pe.Fori(1, UH // RING) as i:
                        for s in range(RING):
                            v_and_route(i, s)
                    with pe.Fori(UH // RING, 2 * UH // RING - 1) as i:
                        for s in range(RING):
                            expert_out(s, 8 * i + (2 * UH + 2 * s + 1), RING * i + (s + 1))
                    i = 2 * UH // RING - 1
                    for s in range(RING):
                        mm = expert_out(s, 8 * i + (2 * UH + 2 * s + 1), RING * i + (s + 1), last=s == RING - 1)
                    mm.then_inc(E["vdone"], 1)

                @block.scalar
                def _(act):
                    st = Steps(act, c_act)

                    def f(o, i, fn, ev=None, **kw):
                        ins = act.activation(o, i, fn, **kw)
                        if ev is None:
                            return st(ins)
                        ins.then_inc(ev, 1)

                    def evac(p, o, i, fn=ACT.Copy):
                        f(o, i, fn, p_evac)

                    def got(p):
                        n = prod[p]
                        act.wait_ge(p_ready, n + 1)
                        return PT[n % 2]

                    def std(name, o, i, scale, bias, ev):
                        b, free = take(act, name)
                        f(o, b[:, i[0]:i[1]], ACT.Sqrt, free, scale=scale, bias=bias)

                    eps, eps64, one = cst[:, 0:1], cst[:, 1:2], cst[:, 2:3]
                    f(XSQ, X[:, :], ACT.Square, E["xsq"])
                    std("xss0", XRSTD, (0, T), 1.0 / D, eps, "xstd")
                    for p in range(PAIR_CQ):
                        b = got(p)
                        if p == PAIR_CKV:
                            evac(p, A(16944, 512), b[:, :])
                        else:
                            c = 2 * (p - PAIR_GK)
                            evac(p, PRE[:, c:c + 2, 3:3 + T], b[:, :].rearrange("p (b t) -> p b t", b=2))
                    b = got(PAIR_CQ)
                    evac(PAIR_CQ, CQ[:, :, :].rearrange("p c t -> p (c t)"), b[:, :])
                    act.wait_ge(p_evac, PAIR_CQ + 1)
                    f(TA[:, 0:768], A(16432, 768), ACT.Square, E["csq"])
                    for i in range(3):
                        act.wait_ge(E["conv"], i + 1)
                        g = CONV[:, 4 * i:4 * i + 4]
                        f(g, g, ACT.Silu, E["silu"])
                    act.wait_ge(E["spa"], 1)
                    f(G1, G1, ACT.Exp, E["spe"], scale=-1.0)
                    f(BETA, MT[:, :, 40:48], ACT.Exp, E["spe"], scale=-1.0)
                    f(NEGA, col("alog_row", 0, H), ACT.Exp, E["spe"])
                    act.wait_ge(E["spe"], 3)
                    f(G1, G1, ACT.Ln, E["spl"], bias=one)
                    b, free = take(act, "css")
                    f(TA[:, 0:256], b[:, 0:T], ACT.Sqrt, E["cstd"], scale=1.0 / QR, bias=eps)
                    f(TA[:, 256:512], b[:, T:2 * T], ACT.Sqrt, free, scale=1.0 / KVR, bias=eps)
                    act.wait_ge(E["silu"], 3)
                    for i in range(2):
                        if i:
                            act.wait_ge(E["gnorm"], 1)
                        src = CONV[:, 4 * i:4 * i + 4].rearrange("p c t -> p (c t)")
                        f(TB, src, ACT.Square, E["gsq"])
                        for j in range(2):
                            if j == 0:
                                take(act, f"gss{i}1")
                            std(f"gss{i}{j}", TB[:, j * 512:(j + 1) * 512], (0, 512), 64.0 if i else 1.0, eps64 if i else eps, None)

                    act.wait_ge(E["gcl"], 2)
                    f(EGC, GCL[:, :, 0:8], ACT.Exp, E["egc"])
                    f(EDEC, EDEC, ACT.Exp, E["egc"])

                    def evac_act(name, o, i, ev=None, fn=ACT.Copy):
                        b, free = take(act, name)
                        f(o, i(b), fn, free)

                    for kind, i in SCHEDULE:
                        if kind == "proj":
                            b = got(i)
                            if i in (PAIR_MQ, PAIR_MQ + 1):
                                evac(i, MQ[:, 2 * (i - PAIR_MQ):2 * (i - PAIR_MQ) + 2].rearrange("p c t -> p (c t)"), b[:, :])
                            elif i in (PAIR_MK, PAIR_MK + 1):
                                evac(i, MK[:, 2 * (i - PAIR_MK):2 * (i - PAIR_MK) + 2].rearrange("p c t -> p (c t)"), b[:, :])
                            elif i in (PAIR_MV, PAIR_MV + 1):
                                a = 2 * P * (i - PAIR_MV)
                                evac(i, MVT[:, :, a:a + 2 * P].rearrange("p t (b n) -> p b t n", b=2),
                                     b[:, :].rearrange("p (b t n) -> p b t n", b=2, t=NT))
                            else:
                                evac(i, ZS[:, 2 * (i - PAIR_Z):2 * (i - PAIR_Z) + 2].rearrange("p c t -> p (c t)"), b[:, :],
                                     ACT.Silu)
                        elif kind == "mnorm":
                            src = (MQ, MK)[i]
                            act.wait_ge(p_evac, prod[(PAIR_MQ, PAIR_MK)[i] + 1] + 1)
                            act.wait_ge(E["gnorm"], 2) if i == 0 else act.wait_ge(E["mnorm"], 1)
                            f(TB, src[:, :].rearrange("p c t -> p (c t)"), ACT.Square, E["msq"])
                            take(act, f"mss{i}1")
                            for j in range(2):
                                std(f"mss{i}{j}", TB[:, j * 512:(j + 1) * 512], (0, 512), 1.0 / CH, eps, None)
                        elif kind == "mlakv":
                            for t in range(NT):
                                for j in range(2):
                                    evac_act(f"kv{t}{j}", KVTOK[:, t, j * 512:(j + 1) * 512], lambda b: b[:, :])
                        elif kind == "mlaq":
                            for t in range(NT):
                                for j in range(2):
                                    n = 512 if j == 0 else 256
                                    evac_act(f"q{t}{j}", QTOK[:, t, j * 512:j * 512 + n], lambda b, n=n: b[:, 0:n])
                        elif kind == "mlaT":
                            act.wait_ge(E["qkss"], 1)
                            f(SSQ, SSQ, ACT.Sqrt, E["qkstd"], scale=1.0 / QK, bias=eps)
                            f(SSK, SSK, ACT.Sqrt, E["qkstd"], scale=1.0 / QK, bias=eps)
                            for n, dst in enumerate((QTH, KTH)):
                                for t in range(NT):
                                    for j in range(2):
                                        b, free = take(act, f"T{n}{t}{j}")
                                        f(dst[0:QK, 4 * j:4 * j + 4, t * P:(t + 1) * P],
                                          b[0:QK, :].rearrange("p (h t) -> p h t", h=4), ACT.Copy, free)
                        elif kind == "head":
                            if i < 2 * H:
                                act.wait_ge(E["pmask"], i + 1)
                                sc = QK ** -0.5 if i < H else CH ** -0.5
                                for t in range(NT):
                                    a = slice(0, P) if t == 0 else slice(P, 3 * P)
                                    act.activation(PB[i % 3][:, a], PB[i % 3][:, a], ACT.Exp, bias=NM[:, i % 3, t:t + 1],
                                                   scale=sc, accum_out=RS[:, i % 3, t:t + 1]).then_inc(E["pexp"], 1)
                            i2 = i - 2
                            if 0 <= i2 < 2 * H:
                                if i2 >= 2:
                                    take(act, f"O{i2 - 2}")
                                b, free = take(act, f"PT{i2}")
                                f(PTB[i2 % 2], b[:, 0:384], ACT.Copy, free)
                            i3 = i - 3
                            if 0 <= i3 < 2 * H:
                                b, free = take(act, f"O{i3}")
                                rows = slice((i3 % 2) * CH, (i3 % 2) * CH + CH)
                                dst = O_MLA[rows, i3 // 2] if i3 < H else O_MOBA[rows, i3 // 2 - HC]
                                f(dst, b[rows, 0:T], ACT.Copy, free)
                        elif kind == "decay":
                            for par in range(2):
                                b, free = take(act, f"gcb{i}{par}")
                                f(EGB[:, par, :, i * P:(i + 1) * P], b[:, :].rearrange("p (c t) -> p c t", c=HC), ACT.Exp, E["egb"])
                            act.wait_ge(E["diff"], 16 * (i + 1))
                            f(AM[:, :], AM[:, :], ACT.Exp, E["decay"], scale=-1.0)
                            f(ATT[i][:, :], ATT[i][:, :], ACT.Exp, E["decay"])
                        elif kind == "level":
                            t, s = i
                            for par in range(2):
                                b, free = take(act, f"Y{t}{s}{par}")
                                f(YM[:, par].rearrange("p c j -> p (c j)"), b[:, :], ACT.Copy, free if par == 0 else E["y"])
                        elif kind == "chunk":
                            b, free = take(act, f"og{i}")
                            f(O_GDN[:, :, i * CH:(i + 1) * CH], b[:, 0:HC * CH].rearrange("p (c t) -> p c t", c=HC), ACT.Copy, free)
                    for n in range(T // CH):
                        freed(act, f"og{n}")
                    act.wait_ge(E["mnorm"], 2)
                    f(TB, VT.rearrange("p c t -> p (c t)"), ACT.Square, E["osq"])
                    take(act, "oss1")
                    for j in range(2):
                        std(f"oss{j}", TB[:, j * 512:(j + 1) * 512], (0, 512), 1.0 / CH, eps, None)
                    for b in range(3):
                        for j in range(2):
                            for i in range(2):
                                p = PAIR_BR + 6 * b + 3 * j + i
                                n = 4 * b + 2 * j + i
                                if n >= 4:
                                    act.wait_ge(E["gate"], n - 3)
                                o = got(p)
                                evac(p, GATE[n % 4], o[:, :], ACT.Sigmoid)
                    act.wait_ge(E["x"], 8)
                    f(XSQ, X[:, :], ACT.Square, E["xsq"])
                    std("xss1", XRSTD, (0, T), 1.0 / D, eps, "xstd")
                    act.wait_ge(spilled, 16)
                    act.wait_ge(E["h"], 2)
                    f(X_r[:, :], HT[:, :], ACT.Copy, E["hup"])

                    def upper_of(slot, b, n_landed, n_begun):
                        act.wait_ge(landed[slot], n_landed)
                        if n_begun is not None:
                            act.wait_ge(block_begun, n_begun)
                        at = BLK * (2 * (slot % 2) + b)
                        f(upper_r[:, at:at + BLK], ring[slot][:, BLK * b:BLK * (b + 1)], ACT.Copy, up_ready)

                    def upper_pair(j):
                        for b in range(2):
                            p = PAIR_QRY + j
                            upper_of(p % RING, b, 16 * (p // RING + 1), 2 * j + b - 2 if j >= 2 else None)

                    upper_pair(0)
                    for h in range(H):
                        upper_pair(h + 1)
                        if h >= 2:
                            take(act, f"sc{h - 2}")
                        o = got(PAIR_QRY + h)
                        evac(PAIR_QRY + h, QRY[h % 2].rearrange("p j t -> p (j t)"), o[:, :])
                    take(act, f"sc{H - 1}")

                    def gelu(n, slot, e):
                        act.wait_ge(p_ready, n)
                        f(act3[:, bass.ds(e, 2)].rearrange("p a t -> p (a t)"), PT[slot % 2][:, :], ACT.Gelu, p_evac)

                    def u_loop(lo, hi):
                        with act.Fori(lo, hi) as i:
                            for s in range(RING):
                                for b in range(2):
                                    upper_of((s + 1) % RING, b, 16 * i + 16 * (PAIR_U // RING + (2 if s == RING - 1 else 1)),
                                             8 * i + (2 * H + 2 * s + b))
                                gelu(RING * i + (NPROD + s + 1), s, 2 * RING * i + 2 * s)

                    u_loop(0, 4)
                    act.wait_ge(E["topd"], 1)
                    f(TS[:, :, :, :], TS[:, :, :, :], ACT.Exp, E["tope"])
                    u_loop(4, UH // RING)
                    act.wait_ge(E["idxT"], NT)
                    u_loop(UH // RING, 2 * UH // RING)

                    def act_upper(slot, n_begun, e, n_w):
                        if n_begun is not None:
                            act.wait_ge(block_begun, n_begun)
                        act.wait_ge(E["wdone"], n_w)
                        f(AUP[slot % 2], act3[:, bass.ds(e, 2)].rearrange("p a t -> p (a t)"), ACT.Copy, aup_ready)

                    act.wait_ge(p_ready, NPROD + 2 * UH)
                    act_upper(0, None, 0, T // TOK)

                    def v_unit(i, s, n_w):
                        for b in range(2):
                            upper_of((s + 1) % RING, b, 16 * i + 16 * (PAIR_V // RING + (2 if s == RING - 1 else 1)),
                                     8 * i + (VB0 + 2 * s + b))
                        if s == 0 and n_w is None:
                            act_upper(1, None, 2, T // TOK)
                        else:
                            act_upper(s + 1, 8 * i + (VB0 + 2 * s + 1), 2 * RING * i + 2 * (s + 1), n_w or T // TOK)

                    for s in range(RING):
                        v_unit(0, s, None)
                    with act.Fori(1, UH // RING - 1) as i:
                        for s in range(RING):
                            v_unit(i, s, T // TOK)
                    for s in range(RING):
                        v_unit(UH // RING - 1, s, 2 * T // TOK if s == RING - 1 else T // TOK)
                    with act.Fori(UH // RING, 2 * UH // RING - 1) as i:
                        for s in range(RING):
                            v_unit(i, s, 2 * T // TOK)
                    for s in range(RING - 1):
                        v_unit(2 * UH // RING - 1, s, 2 * T // TOK)

                @block.vector
                def _(v):
                    st = Steps(v, c_dve)

                    def mod(m):
                        for kp in range(4):
                            n = 4 * m + kp
                            v.wait_ge(mod_landed[n % 3], 16 * (n // 3 + 1) + 16 * 8 * layer)
                            for kk in range(2):
                                k = 2 * kp + kk
                                w = MODR[n % 3][:, kk * D:(kk + 1) * D]
                                c = cact[:, KD + k:KD + k + 1]
                                if k == 0:
                                    if m:
                                        take(v, f"mod{m - 1}")
                                    ins = v.tensor_scalar(ACC, w, c, None, ALU.mult)
                                else:
                                    st.done() if kk else v.wait_ge(mod_used, n)
                                    ins = v.scalar_tensor_tensor(ACC, w, c, ACC, ALU.mult, ALU.add)
                                if k == 7:
                                    ins.then_inc(mod_acc, 1)
                                elif kk == 1:
                                    ins.then_inc(mod_used, 1)
                                else:
                                    st(ins)
                            if kp == 3:
                                v.wait_ge(mod_acc, m + 1)
                                v.engine_nop().then_inc(mod_used, 1)

                    def modcol(m):
                        b, free = take(v, f"mod{m}")
                        o = modc[:, m * KD:(m + 1) * KD]
                        v.tensor_tensor(o, b[:, 0:KD], col("b_mod", m * KD, KD), ALU.add).then_inc(free, 1)
                        if m in (1, 4):
                            freed(v, f"mod{m}")
                            st(v.tensor_scalar(o, o, 1.0, None, ALU.add))
                            st.done()

                    def modulate(n, sh, sc):
                        v.wait_ge(E["xsq"], n)
                        v.tensor_reduce(XSUM, XSQ.rearrange("p (k t) -> p t k", k=KD), AX, ALU.add).then_inc(E["xsum"], 1)
                        freed(v, f"xss{n - 1}")
                        st(v.reciprocal(XRSTD, XRSTD))
                        st.done()
                        st(v.tensor_tensor(h3, x3, XRSTD[:, None, :].to_broadcast([P, KD, T]), ALU.mult))
                        st.done()
                        for k in range(KD):
                            a, c = modc[:, sc * KD + k:sc * KD + k + 1], modc[:, sh * KD + k:sh * KD + k + 1]
                            ins = v.tensor_scalar(h3[:, k], h3[:, k], a, c, ALU.mult, ALU.add)
                            ins.then_inc(E["h"], 1) if k == KD - 1 else st(ins)

                    v.wait_ge(s_sml, 16)
                    mod(0)
                    mod(1)
                    modcol(0)
                    modcol(1)
                    modulate(1, 0, 1)
                    v.memset(PRE[:, :, 0:3], 0.0).then_inc(E["zero"], 1)

                    def conv(i):
                        v.wait_ge(p_evac, 2 * i + 3)
                        v.wait_ge(E["zero"], 1)
                        last = [0] * 4
                        for j in range(4):
                            for c in range(4):
                                cc = 4 * i + c
                                src, w, o = PRE[:, cc, j:j + T], col("conv", cc * 4 + j), CONV[:, cc]
                                if j:
                                    st.done(last[c])
                                    ins = v.scalar_tensor_tensor(o, src, w, o, ALU.mult, ALU.add)
                                else:
                                    ins = v.tensor_scalar(o, src, w, None, ALU.mult)
                                if j == 3 and c == 3:
                                    ins.then_inc(E["conv"], 1)
                                else:
                                    last[c] = st(ins)

                    mod(2)
                    conv(0)
                    mod(3)
                    conv(1)
                    mod(4)
                    conv(2)
                    for m in range(2, 5):
                        modcol(m)
                    b, free = take(v, "misc")
                    v.tensor_copy(MT, b[:, 0:NT * 48].rearrange("p (t n) -> p t n", t=NT)).then_inc(free, 1)
                    freed(v, "misc")
                    st(v.tensor_tensor(G2, MT[:, :, 32:40], col("dt_row", 0, H)[:, None, :].to_broadcast([P, NT, H]), ALU.add))
                    st.done()
                    v.scalar_tensor_tensor(G1, G2, -1.0, G2, ALU.mult, ALU.max).then_inc(E["spa"], 1)
                    mod(5)
                    v.wait_ge(E["spe"], 3)
                    st(v.tensor_scalar(BETA, BETA, 1.0, None, ALU.add))
                    st.done()
                    st(v.reciprocal(BETA, BETA))
                    v.wait_ge(E["spl"], 1)
                    st(v.scalar_tensor_tensor(G3, G2, 0.0, G1, ALU.max, ALU.add))
                    st.done()
                    v.scalar_tensor_tensor(GG, G3, -1.0, NEGA[:, None, :].to_broadcast([P, NT, H]),
                                           ALU.mult, ALU.mult).then_inc(E["g"], 1)
                    v.wait_ge(E["cstd"], 1)
                    freed(v, "css")
                    st(v.reciprocal(TA[:, 512:1024], TA[:, 0:512]))
                    st.done()
                    for c in range(2):
                        st(v.scalar_tensor_tensor(CQ[:, c], CQ[:, c], col("q_gain", c), TA[:, 512:768], ALU.mult, ALU.mult))
                    v.scalar_tensor_tensor(CKV, CKV, col("kv_gain"), TA[:, 768:1024], ALU.mult, ALU.mult).then_inc(E["cnorm"], 1)

                    def norm_by(names, dst, ev, gain=None):
                        for nm in names:
                            freed(v, nm)
                        st(v.reciprocal(TB, TB))
                        st.done()
                        flat = dst.rearrange("p c t -> p (c t)")
                        if gain is None:
                            v.tensor_tensor(flat, flat, TB, ALU.mult).then_inc(ev, 1)
                        else:
                            v.scalar_tensor_tensor(flat, flat, gain, TB, ALU.mult, ALU.mult).then_inc(ev, 1)

                    norm_by(("gss00", "gss01"), KT, E["gnorm"])
                    norm_by(("gss10", "gss11"), QT, E["gnorm"])
                    modcol(5)
                    b, free = take(v, "gcl")
                    v.tensor_copy(GCL, b[:, 0:NT * 16].rearrange("p (t n) -> p t n", t=NT)).then_inc(E["gcl"], 1)
                    v.wait_ge(E["gcl"], 1)
                    v.engine_nop().then_inc(free, 1)
                    v.tensor_tensor(EDEC, GCL[:, :, 8:16], GCL[:, :, 0:8], ALU.subtract).then_inc(E["gcl"], 1)
                    v.wait_ge(E["egc"], 2)
                    st(v.tensor_tensor(EB, BETA, EGC, ALU.mult))
                    v.wait_ge(E["masks"], 1)
                    for t in range(NT):
                        b, free = take(v, f"tokk{t}")
                        s3 = b[:, :].rearrange("p (h d) -> p h d", h=H)
                        st.done()
                        for dst, sc in ((KBG, EB), (KDEC, EDEC)):
                            v.tensor_tensor(dst[:, t].rearrange("p (h d) -> p h d", h=H), s3,
                                            sc[:, t, :, None].to_broadcast([P, H, CH]), ALU.mult).then_inc(E["tok"], 1)
                        v.wait_ge(E["tok"], 2 * t + 2)
                        v.engine_nop().then_inc(free, 1)
                    for t in range(NT):
                        b, free = take(v, f"tokv{t}")
                        v.tensor_tensor(VB[:, t].rearrange("p (h d) -> p h d", h=H), b[:, :].rearrange("p (h d) -> p h d", h=H),
                                        BETA[:, t, :, None].to_broadcast([P, H, CH]), ALU.mult).then_inc(E["tok"], 1)
                        v.wait_ge(E["tok"], 2 * NT + t + 1)
                        v.engine_nop().then_inc(free, 1)
                    st(v.memset(upper[:, 0:512], 0.0))

                    def rotate(dst, x1, x2, t, shape, tmp):
                        cb = COS[:, t, None, :].to_broadcast(shape)
                        sb_ = SIN[:, t, None, :].to_broadcast(shape)
                        n = shape[1] * 16
                        t1, t2, t3, t4 = (tmp[:, i * n:(i + 1) * n].rearrange("p (h f) -> p h f", h=shape[1]) for i in range(4))
                        st(v.tensor_tensor(t1, x1, cb, ALU.mult))
                        st(v.tensor_tensor(t2, x2, sb_, ALU.mult))
                        st(v.tensor_tensor(t3, x1, sb_, ALU.mult))
                        st(v.tensor_tensor(t4, x2, cb, ALU.mult))
                        st.done()
                        st(v.tensor_tensor(dst[:, :, 0:16], t1, t2, ALU.subtract))
                        return v.tensor_tensor(dst[:, :, 16:32], t3, t4, ALU.add)

                    def head_step(i):
                        if i < 2 * H:
                            b, free = take(v, f"S{i}")
                            if i >= 3:
                                take(v, f"PT{i - 3}")
                            else:
                                qk_transposed(v)
                            pb = PB[i % 3]
                            st(v.tensor_tensor(pb, b[:, 0:384], cmask, ALU.add))
                            st.done()
                            st(v.tensor_reduce(MX[:, i % 3, 0:1], pb[:, 0:P], AX, ALU.max))
                            v.tensor_reduce(MX[:, i % 3, 1:2], pb[:, P:3 * P], AX, ALU.max).then_inc(free, 1)
                            freed(v, f"S{i}")
                            sc = QK ** -0.5 if i < H else CH ** -0.5
                            v.tensor_scalar(NM[:, i % 3], MX[:, i % 3], -sc, None, ALU.mult).then_inc(E["pmask"], 1)
                        i1 = i - 1
                        if 0 <= i1 < 2 * H:
                            v.wait_ge(E["pexp"], 2 * i1 + 2)
                            st(v.reciprocal(RI[:, i1 % 3], RS[:, i1 % 3]))
                            st.done()
                            st(v.tensor_scalar(PB[i1 % 3][:, 0:P], PB[i1 % 3][:, 0:P], RI[:, i1 % 3, 0:1], None, ALU.mult))
                            v.tensor_scalar(PB[i1 % 3][:, P:3 * P], PB[i1 % 3][:, P:3 * P], RI[:, i1 % 3, 1:2], None,
                                            ALU.mult).then_inc(E["pnorm"], 1)

                    for kind, i in SCHEDULE:
                        if kind == "mnorm":
                            norm_by((f"mss{i}0", f"mss{i}1"), (MQ, MK)[i], E["mnorm"], col(("mq_gain", "mk_gain")[i]))
                        elif kind == "mlaT":
                            for t in range(NT):
                                for j in range(2):
                                    for nm in (f"kv{t}{j}", f"q{t}{j}"):
                                        freed(v, nm)
                            qf, kf = (a.rearrange("p t (h n) -> p t h n", h=H) for a in (QTOK, KFULL))
                            kv4 = KVTOK[:, :].rearrange("p t (h n) -> p t h n", h=H)
                            sq = TA.rearrange("p (h n) -> p h n", h=H)
                            for t in range(NT):
                                st.done()
                                st(v.tensor_tensor(sq[:, :, 0:QK], qf[:, t], qf[:, t], ALU.mult))
                                st.done()
                                st(v.tensor_reduce(SSQ[:, t], sq[:, :, 0:QK], AX, ALU.add))
                                st.done()
                                st(v.tensor_tensor(sq[:, :, 0:NOPE], kv4[:, t, :, 0:NOPE], kv4[:, t, :, 0:NOPE], ALU.mult))
                                st.done()
                                st(v.tensor_reduce(SSK[:, t], sq[:, :, 0:NOPE], AX, ALU.add))
                                st(v.tensor_tensor(PESQ[:, t], MT[:, t, 0:ROPE], MT[:, t, 0:ROPE], ALU.mult))
                                st(v.tensor_tensor(KPG[:, t], MT[:, t, 0:ROPE], col("kn_row", NOPE, ROPE), ALU.mult))
                                st.done()
                                st(v.tensor_reduce(SSPE[:, t:t + 1], PESQ[:, t], AX, ALU.add))
                                st.done()
                                ins = v.tensor_scalar(SSK[:, t], SSK[:, t], SSPE[:, t:t + 1], None, ALU.add)
                                ins.then_inc(E["qkss"], 1) if t == NT - 1 else st(ins)
                            for t in range(NT):
                                kr = KROPE[:, t, None, :]
                                kp = KPG[:, t, None, :]
                                st(rotate(kr, kp[:, :, 0:16], kp[:, :, 16:32], t, [P, 1, 16], TA))
                                st.done()
                            v.wait_ge(E["qkstd"], 2)
                            for ss in (SSQ, SSK):
                                st(v.reciprocal(ss, ss))
                            st.done()
                            for t in range(NT):
                                st(v.tensor_tensor(qf[:, t], qf[:, t], SSQ[:, t, :, None].to_broadcast([P, H, QK]), ALU.mult))
                                st.done()
                                st(v.tensor_tensor(qf[:, t], qf[:, t], col("qn_row", 0, QK)[:, None, :].to_broadcast([P, H, QK]), ALU.mult))
                                st.done()
                                ins = rotate(qf[:, t, :, NOPE:QK], qf[:, t, :, NOPE:NOPE + 16], qf[:, t, :, NOPE + 16:QK], t, [P, H, 16], TA)
                                if t == NT - 1:
                                    ins.then_inc(E["qkfull"], 1)
                                else:
                                    st(ins)
                                    st.done()
                            for t in range(NT):
                                st(v.tensor_tensor(kf[:, t, :, 0:NOPE], kv4[:, t, :, 0:NOPE],
                                                   SSK[:, t, :, None].to_broadcast([P, H, NOPE]), ALU.mult))
                                st.done()
                                st(v.tensor_tensor(kf[:, t, :, 0:NOPE], kf[:, t, :, 0:NOPE],
                                                   col("kn_row", 0, NOPE)[:, None, :].to_broadcast([P, H, NOPE]), ALU.mult))
                                ins = v.tensor_tensor(kf[:, t, :, NOPE:QK], KROPE[:, t, None, :].to_broadcast([P, H, ROPE]),
                                                      SSK[:, t, :, None].to_broadcast([P, H, ROPE]), ALU.mult)
                                if t == NT - 1:
                                    ins.then_inc(E["qkfull"], 1)
                                else:
                                    st(ins)
                        elif kind == "head":
                            head_step(i)
                        elif kind == "decay":
                            if i:
                                v.wait_ge(E["uw"], 1)
                            for par in range(2):
                                b, free = take(v, f"gcb{i}{par}")
                                v.wait_ge(E["egb"], 2 * i + par + 1)
                                for c in range(HC):
                                    gc = GCL[:, i, 2 * c + par:2 * c + par + 1]
                                    src = b[:, c * P:(c + 1) * P]
                                    v.tensor_scalar(AM[:, par, c], src, gc, 0.0, ALU.subtract, ALU.max).then_inc(E["diff"], 1)
                                    v.tensor_scalar(ATT[i][:, par, c], src, gc, 0.0, ALU.subtract, ALU.min).then_inc(E["diff"], 1)
                                v.wait_ge(E["diff"], 16 * i + 8 * par + 8)
                                v.engine_nop().then_inc(free, 1)
                            v.wait_ge(E["decay"], 2 * i + 2)
                            for m, mask in ((AM, strict), (ATT[i], incl)):
                                mm = m[:, :].rearrange("p g c j -> p (g c) j")
                                st(v.tensor_tensor(mm, mm, mask[:, None, :].to_broadcast([P, H, P]), ALU.mult))
                            ts = slice(i * P, (i + 1) * P)
                            v.wait_ge(E["gnorm"], 2)
                            for par in range(2):
                                r = slice(par * CH, par * CH + CH)
                                for q2 in range(2):
                                    cs = slice(2 * q2, 2 * q2 + 2)
                                    v.tensor_tensor(QG[r, cs, ts], QT[r, cs, ts], EGB[r, par, cs, ts], ALU.mult).then_inc(E["qg"], 1)
                        elif kind == "build":
                            for par in range(2):
                                b, free = take(v, f"GK{i}{par}")
                                st.done()
                                for c in range(HC):
                                    st(v.scalar_tensor_tensor(AM[:, par, c], b[:, c * P:(c + 1) * P],
                                                              BETA[:, i, 2 * c + par:2 * c + par + 1], AM[:, par, c],
                                                              ALU.mult, ALU.mult))
                                st.done()
                                v.engine_nop().then_inc(free, 1)
                            for par in range(2):
                                b, free = take(v, f"GQ{i}{par}")
                                a = ATT[i][:, par].rearrange("p c j -> p (c j)")
                                v.tensor_tensor(a, b[:, :], a, ALU.mult).then_inc(free, 1)
                            flat = lambda m: m[:, :].rearrange("p g c j -> p (g c) j")
                            idb = ident[:, None, :].to_broadcast([P, H, P])
                            v.tensor_tensor(flat(CM), flat(AM), lmask[:, None, 0:P].to_broadcast([P, H, P]), ALU.mult)\
                             .then_inc(E["cm"], 1)
                            v.wait_ge(E["cm"], len(LEVELS) * i + 1)
                            v.scalar_tensor_tensor(flat(TM), flat(CM), -1.0, idb, ALU.mult, ALU.add).then_inc(E["t"], 1)
                            for par in range(2):
                                b, free = take(v, f"Y{i}{1}{par}")
                                ins = v.scalar_tensor_tensor(UM[:, par], b[:, :].rearrange("p (c j) -> p c j", c=HC), -1.0,
                                                             ident[:, None, :].to_broadcast([P, HC, P]), ALU.mult, ALU.add)
                                if par == 0:
                                    ins.then_inc(free, 1)
                                else:
                                    ins.then_inc(E["u"], 1)
                                    v.wait_ge(E["u"], len(LEVELS) * i + 1)
                                    v.engine_nop().then_inc(free, 1)
                            v.tensor_tensor(flat(CM), flat(AM), lmask[:, None, P:2 * P].to_broadcast([P, H, P]), ALU.mult)\
                             .then_inc(E["cm"], 1)
                        elif kind == "level":
                            t, s = i
                            li = LEVELS.index(s)
                            flat = lambda m: m[:, :].rearrange("p g c j -> p (g c) j")
                            v.wait_ge(E["y"], (len(LEVELS) - 1) * t + li)
                            v.engine_nop().then_inc(side_free[jobs[f"Y{t}{s}1"][0]], 1)
                            if s != LEVELS[-1]:
                                v.tensor_tensor(flat(CM), flat(AM), lmask[:, None, (li + 1) * P:(li + 2) * P]
                                                .to_broadcast([P, H, P]), ALU.mult).then_inc(E["cm"], 1)
                            for par in range(2):
                                b, free = take(v, f"U{t}{s}{par}")
                                ins = v.tensor_tensor(UM[:, par], UM[:, par], b[:, :].rearrange("p (c j) -> p c j", c=HC), ALU.subtract)
                                if par == 0:
                                    ins.then_inc(free, 1)
                                else:
                                    ins.then_inc(E["u"], 1)
                                    v.wait_ge(E["u"], len(LEVELS) * t + li + 1)
                                    v.engine_nop().then_inc(free, 1)
                            if s != LEVELS[-1]:
                                for par in range(2):
                                    b, free = take(v, f"TT{t}{s}{par}")
                                    if par == 0:
                                        take(v, f"TT{t}{s}1")
                                    ins = v.tensor_tensor(TM[:, par], TM[:, par], b[:, :].rearrange("p (c j) -> p c j", c=HC),
                                                          ALU.subtract)
                                    if par == 0:
                                        ins.then_inc(free, 1)
                                    else:
                                        ins.then_inc(E["t"], 1)
                                        v.wait_ge(E["t"], (len(LEVELS) - 1) * t + li + 1)
                                        v.engine_nop().then_inc(free, 1)
                        elif kind == "uw":
                            for par in range(2):
                                b, free = take(v, f"uu{i}{par}")
                                v.tensor_copy(UV[:, i].rearrange("p (c g d) -> p c g d", c=HC, g=2)[:, :, par],
                                              b[:, :].rearrange("p (c g d) -> p c g d", c=HC, g=2)[:, :, par]).then_inc(free, 1)
                            b, free = take(v, f"wt{i}")
                            v.tensor_copy(WT[:, i], b[:, :].rearrange("p (c j) -> p c j", c=HC)).then_inc(E["wt"], 1)
                            v.wait_ge(E["wt"], i + 1)
                            v.engine_nop().then_inc(free, 1)
                            v.engine_nop().then_inc(E["uw"], 1)
                            if i == NT - 1:
                                for par in range(2):
                                    r = slice(par * CH, par * CH + CH)
                                    st(v.tensor_copy(EGL[r], EGB[r, par, :, CH - 1:T:CH]))
                                v.engine_nop().then_inc(E["state"], 1)
                                st.done()
                        elif kind == "chunk":
                            n, t, r = i, i // 2, slice((i % 2) * CH, (i % 2) * CH + CH)
                            b, free = take(v, f"ws{n}")
                            v.tensor_tensor(UV[r, t], UV[r, t], b[r, :], ALU.subtract).then_inc(E["vnew"], 1)
                            v.wait_ge(E["vnew"], n + 1)
                            v.engine_nop().then_inc(free, 1)
                            if n < T // CH - 1:
                                b, free = take(v, f"ds{n}")
                                st(v.tensor_tensor(ST, ST, EGL[:, :, n:n + 1].to_broadcast([P, HC, P]), ALU.mult))
                                ds = YM[:, 0]
                                v.tensor_tensor(ds, b[:, :].rearrange("p (c j) -> p c j", c=HC),
                                                same[:, None, :].to_broadcast([P, HC, P]), ALU.mult).then_inc(free, 1)
                                freed(v, f"ds{n}")
                                v.tensor_tensor(ST, ST, ds, ALU.add).then_inc(E["state"], 1)
                    for nm in ("oss0", "oss1"):
                        freed(v, nm)
                    v.wait_ge(p_evac, prod[PAIR_Z + 1] + 1)
                    st(v.reciprocal(TB, TB))
                    st.done()
                    og = VT.rearrange("p c t -> p (c t)")
                    st(v.scalar_tensor_tensor(og, og, col("o_gain"), TB, ALU.mult, ALU.mult))
                    st.done()
                    v.tensor_tensor(og, og, ZS[:, :].rearrange("p c t -> p (c t)"), ALU.mult).then_inc(E["ognorm"], 1)
                    last = [0] * 4
                    for b in range(3):
                        for j in range(2):
                            for i in range(2):
                                n = 4 * b + 2 * j + i
                                o, free = take(v, f"br{b}{j}{i}")
                                v.wait_ge(p_evac, prod[PAIR_BR + 6 * b + 3 * j + i] + 1)
                                gt = GATE[n % 4]
                                m = MERGED[:, 4 * j + 2 * i:4 * j + 2 * i + 2].rearrange("p k t -> p (k t)")
                                if b == 0:
                                    last[2 * j + i] = st(v.tensor_tensor(m, gt, o[:, :], ALU.mult))
                                    st.done()
                                    v.engine_nop().then_inc(free, 1)
                                    v.engine_nop().then_inc(E["gate"], 1)
                                else:
                                    v.tensor_tensor(gt, gt, o[:, :], ALU.mult).then_inc(free, 1)
                                    freed(v, f"br{b}{j}{i}")
                                    v.tensor_tensor(m, m, gt, ALU.add).then_inc(E["gate"], 1)
                                    if b == 1:
                                        v.wait_ge(E["gate"], n + 1)
                                    else:
                                        v.wait_ge(E["gate"], n + 1)
                                        v.engine_nop().then_inc(E["merged"], 1)
                    for p in range(4):
                        b, free = take(v, f"y{p}")
                        for i in range(2):
                            k = 2 * p + i
                            v.scalar_tensor_tensor(x3[:, k], b[:, i * T:(i + 1) * T], modc[:, 2 * KD + k:2 * KD + k + 1], x3[:, k],
                                                   ALU.mult, ALU.add).then_inc(E["x"], 1)
                        v.wait_ge(E["x"], 2 * p + 2)
                        v.engine_nop().then_inc(free, 1)
                    modulate(2, 3, 4)
                    v.wait_ge(E["hup"], 1)
                    v.wait_ge(E["h"], 2)
                    v.tensor_tensor(HT_r[:, :], HT[:, :], X_r[:, :].bitcast(F32), ALU.subtract).then_inc(E["hsplit"], 1)

                    def top16(srcs, vals, idxs, works):
                        n = len(srcs)
                        for k in range(n):
                            st(v.max(vals[k][:, 0:8], srcs[k]))
                        st.done()
                        for k in range(n):
                            st(v.max_index(idxs[k][:, 0:8], vals[k][:, 0:8], srcs[k]))
                            st(v.match_replace(works[k], vals[k][:, 0:8], srcs[k], -3.0e38))
                        st.done()
                        for k in range(n):
                            st(v.max(vals[k][:, 8:16], works[k]))
                        st.done()
                        for k in range(n):
                            st(v.max_index(idxs[k][:, 8:16], vals[k][:, 8:16], works[k]))

                    for h in range(H):
                        b, free = take(v, f"sc{h}")
                        tj = [(t, j) for t in range(NT) for j in range(2)]
                        top16([b[:, (2 * t + j) * P:(2 * t + j + 1) * P] for t, j in tj], [TV[:, t, j, h] for t, j in tj],
                              [TI[:, t, j, h] for t, j in tj], WORK)
                        st.done()
                        v.engine_nop().then_inc(free, 1)
                        for t in range(NT):
                            st(v.tensor_tensor(CAND[:, t].rearrange("p (a b) -> p a b", a=TOPK),
                                               TV[:, t, 0, h, :, None].to_broadcast([P, TOPK, TOPK]),
                                               TV[:, t, 1, h, None, :].to_broadcast([P, TOPK, TOPK]), ALU.add))
                        st.done()
                        top16([CAND[:, t] for t in range(NT)], [TS[:, t, h] for t in range(NT)],
                              [TP[:, t, h * TOPK:(h + 1) * TOPK] for t in range(NT)], [CWORK[:, t] for t in range(NT)])
                        st.done()
                    TS3 = TS[:, :, :, :].rearrange("p t h k -> p (t h) k")
                    st(v.tensor_copy(SM1.rearrange("p t h -> p (t h)"), TS3[:, :, 0]))
                    st.done()
                    smb = SM1.rearrange("p t h -> p (t h)")[:, :, None].to_broadcast([P, NT * H, TOPK])
                    v.tensor_tensor(TS3, TS3, smb, ALU.subtract).then_inc(E["topd"], 1)
                    st(v.tensor_copy(TIF[:, :, :, :, :].rearrange("p t j h k -> p (t j h k)"),
                                     TI[:, :, :, :, :].rearrange("p t j h k -> p (t j h k)")))
                    for t in range(NT):
                        st.done()
                        st(v.tensor_scalar(TABU[:, 0, 0:P], TP[:, t], 4, None, ALU.logical_shift_right))
                        st(v.tensor_scalar(TABU[:, 1, 0:P], TP[:, t], 15, None, ALU.bitwise_and))
                        st.done()
                        st(v.tensor_copy(TAB[:, :, 0:P], TABU[:, :, 0:P]))
                        st.done()
                        for j in range(2):
                            ab = TAB[:, j, 0:P].rearrange("p (h k) -> p h k", h=H)[:, :, :, None].to_broadcast([P, H, TOPK, TOPK])
                            st(v.tensor_tensor(EQ, iota[:, None, None, 0:TOPK].to_broadcast([P, H, TOPK, TOPK]), ab, ALU.is_equal))
                            st.done()
                            st(v.tensor_tensor(EQ, EQ, TIF[:, t, j, :, None, :].to_broadcast([P, H, TOPK, TOPK]), ALU.mult))
                            st.done()
                            st(v.tensor_reduce(IDX[:, t, j].rearrange("p (h k) -> p h k", h=H), EQ, AX, ALU.add))
                            st.done()
                    v.wait_ge(E["tope"], 1)
                    st(v.tensor_reduce(SM1.rearrange("p t h -> p (t h)"), TS3, AX, ALU.add))
                    st.done()
                    st(v.reciprocal(SM2.rearrange("p t h -> p (t h)"), SM1.rearrange("p t h -> p (t h)")))
                    st.done()
                    v.tensor_tensor(TS3, TS3, SM2.rearrange("p t h -> p (t h)")[:, :, None].to_broadcast([P, NT * H, TOPK]),
                                    ALU.mult).then_inc(E["idx"], 1)
                    for t in range(NT):
                        b, free = take(v, f"ix{t}")
                        ts = slice(t * P, (t + 1) * P)
                        st(v.tensor_copy(IDXT[:, :, ts], b[:, 0:2 * P].rearrange("p (j t) -> p j t", j=2)))
                        g = b[:, 2 * P:3 * P]
                        st(v.tensor_copy(GATES[:, ts, 0], g))
                        st.done()
                        st(v.tensor_tensor(GREST[:, ts], g, GATES[:, ts, 0], ALU.subtract))
                        st.done()
                        v.engine_nop().then_inc(free, 1)
                        st(v.tensor_copy(GATES[:, ts, 1], GREST[:, ts]))
                        st.done()
                        st(v.tensor_tensor(GREST[:, ts], GREST[:, ts], GATES[:, ts, 1], ALU.subtract))
                        st.done()
                        v.tensor_copy(GATES[:, ts, 2], GREST[:, ts]).then_inc(E["idxT"], 1)
                    v.wait_ge(E["idxT"], NT)

                    def lower(slot, b, n):
                        v.wait_ge(up_ready, n)
                        cols = slice(BLK * b, BLK * (b + 1))
                        at = BLK * (2 * (slot % 2) + b)
                        v.tensor_tensor(ring_r[slot][:, cols], ring[slot][:, cols], upper_r[:, at:at + BLK].bitcast(F32), ALU.subtract).then_inc(low_dve, 1)

                    def onehot_b(c, t0, slot, n_used):
                        if n_used is not None:
                            v.wait_ge(E["wready"], n_used)
                        for k in range(GRP):
                            ins = v.scalar_tensor_tensor(OHB[slot][:, k], iota[:, None, c * EH:(c + 1) * EH].to_broadcast([P, 3, EH]),
                                                         IDXT[:, 1, bass.ds(t0 + k, 1)],
                                                         GATES[:, bass.ds(t0 + k, 1), :].rearrange("p a j -> p (a j)")[:, :, None]
                                                         .to_broadcast([P, 3, EH]), ALU.is_equal, ALU.mult)
                        ins.then_inc(E["ohb"], 1)

                    def apply(c, t0, slot, n):
                        v.wait_ge(E["wready"], n)
                        a = act3[:, c * EH:(c + 1) * EH, bass.ds(t0, TOK)]
                        v.tensor_tensor(a, a, SB[4 + slot][:, :].rearrange("p (t e) -> p e t", t=TOK), ALU.mult)\
                         .then_inc(E["wdone"], 1)

                    def u_unit(i, s, first=False):
                        for b in range(2):
                            lower(s, b, 8 * i + (NPOOL + 2 * s + b + 1))
                        for g in range(2):
                            onehot_b(0, RING * TOK * i + TOK * s + GRP * g, g, None if first else 8 * i + (2 * s + g - 1))
                        if first:
                            return
                        apply(0, RING * TOK * i + TOK * (s - 1), (s - 1) % 2, 8 * i + 2 * s)

                    v.wait_ge(p_evac, NPROD + UH)
                    for s in range(RING):
                        u_unit(0, s, first=s == 0)
                    with v.Fori(1, UH // RING) as i:
                        for s in range(RING):
                            u_unit(i, s)
                    apply(0, T - TOK, 1, T // GRP)

                    def act_lower(slot, e, n):
                        v.wait_ge(aup_ready, n)
                        v.tensor_tensor(ALOW[slot % 2], act3[:, bass.ds(e, 2)].rearrange("p a t -> p (a t)"),
                                        AUP[slot % 2].bitcast(F32), ALU.subtract).then_inc(alow_ready, 1)

                    def v_unit(i, s, w=True, first=False):
                        for b in range(2):
                            lower(s, b, 8 * i + (VB0 + 2 * s + b + 1))
                            if b == 0:
                                act_lower(s, 2 * RING * i + 2 * s, RING * i + (s + 1))
                        if not w:
                            return
                        for g in range(2):
                            onehot_b(1, RING * TOK * i + TOK * s + GRP * g, g, 8 * i + (T // GRP + 2 * s + g - 1))
                        if not first:
                            apply(1, RING * TOK * i + TOK * (s - 1), (s - 1) % 2, 8 * i + (T // GRP + 2 * s))

                    v.wait_ge(p_evac, NPROD + 2 * UH)
                    for s in range(RING):
                        v_unit(0, s, first=s == 0)
                    with v.Fori(1, UH // RING) as i:
                        for s in range(RING):
                            v_unit(i, s)
                    apply(1, T - TOK, 1, 2 * T // GRP)
                    with v.Fori(UH // RING, 2 * UH // RING) as i:
                        for s in range(RING):
                            v_unit(i, s, w=False)
                    v.wait_ge(E["vdone"], 1)
                    v.wait_ge(reloaded, 16)
                    for k in range(KD):
                        v.scalar_tensor_tensor(x3[:, k], SB[k // 2][:, (k % 2) * T:(k % 2 + 1) * T], modc[:, 5 * KD + k:5 * KD + k + 1],
                                               x3[:, k], ALU.mult, ALU.add).then_inc(E["x"], 1)
                    v.wait_ge(E["x"], 2 * KD)

                @block.gpsimd
                def _(g):
                    st = Steps(g, c_pool)
                    for n in range(24):
                        if n >= 3:
                            g.wait_ge(mod_used, n - 2)
                        g.dma_start(MODR[n % 3], modw[bass.ds(layer * 24 + n, 1)].rearrange("a p n -> p (a n)"))\
                         .then_inc(mod_landed[n % 3], 16)
                    for m in (same, cmask, lmask):
                        st(g.memset(m, 0.0))
                    st.done()
                    st(g.memset(same[0:CH, 0:CH], 1.0))
                    st.done()
                    st(g.memset(same[CH:P, CH:P], 1.0))
                    st.done()
                    for i, s in enumerate(LEVELS):
                        m = lmask[:, i * P:(i + 1) * P].rearrange("p (b j) -> p b j", j=2 * s)
                        st(g.memset(m[:, :, 0:s], 1.0))
                    for a in (0, 2 * P):
                        st(g.affine_select(out=cmask[:, a:a + P], in_=cmask[:, a:a + P], compare_op=ALU.is_ge, fill=NEG,
                                           base=0, pattern=[[-1, P]], channel_multiplier=1))
                    st.done()
                    st(g.affine_select(out=strict, in_=same, compare_op=ALU.is_gt, fill=0.0, base=0,
                                       pattern=[[-1, P]], channel_multiplier=1))
                    st(g.affine_select(out=incl, in_=same, compare_op=ALU.is_ge, fill=0.0, base=0,
                                       pattern=[[1, P]], channel_multiplier=-1))
                    for i, s in enumerate(LEVELS):
                        m = lmask[:, i * P:(i + 1) * P].rearrange("p (b j) -> p b j", j=2 * s)
                        st(g.affine_select(out=m, in_=m, compare_op=ALU.is_ge, fill=0.0, base=-s,
                                           pattern=[[-2 * s, P // (2 * s)], [0, 2 * s]], channel_multiplier=1))
                    st.done()
                    for i, s in enumerate(LEVELS):
                        m = lmask[:, i * P:(i + 1) * P].rearrange("p (b j) -> p b j", j=2 * s)
                        st(g.affine_select(out=m, in_=m, compare_op=ALU.is_ge, fill=0.0, base=2 * s - 1,
                                           pattern=[[2 * s, P // (2 * s)], [0, 2 * s]], channel_multiplier=-1))
                    st.done()
                    g.memset(tiny_f[:, 48:64], 0.0).then_inc(E["masks"], 1)

                    def lower(slot, b, n):
                        g.wait_ge(up_ready, n)
                        cols = slice(BLK * b, BLK * (b + 1))
                        g.tensor_tensor(ring_r[slot][:, cols], ring[slot][:, cols], upper_r[:, BLK * (2 * (slot % 2) + b):BLK * (2 * (slot % 2) + b + 1)].bitcast(F32),
                                        ALU.subtract).then_inc(low_pool, 1)

                    with g.Fori(0, NPOOL // 8) as i:
                        for s in range(RING):
                            for b in range(2):
                                lower(s, b, 8 * i + (2 * s + b + 1))

                    g.wait_ge(E["idxT"], NT)

                    def onehot_a(t0, slot, n_ready, n_used):
                        if n_used is not None:
                            g.wait_ge(E["wready"], n_used)
                        g.tensor_copy(I1C[slot], IDXT[:, 0, bass.ds(t0, GRP)]).then_inc(i1_ready, 1)
                        g.wait_ge(i1_ready, n_ready)
                        g.tensor_tensor(I1D[slot], I1C[slot], ones[:, 0:GRP], ALU.mult).then_inc(c_pool, 1)
                        for k in range(GRP):
                            ins = g.tensor_scalar(OHA[slot][:, k], iota[:, :], I1C[slot][:, k:k + 1], None, ALU.is_equal)
                        ins.then_inc(E["oha"], 1)

                    for s in range(2):
                        onehot_a(GRP * s, s, s + 1, None)
                    with g.Fori(1, T // TOK) as i:
                        for s in range(2):
                            onehot_a(TOK * i + GRP * s, s, 2 * i + (s + 1), 2 * i + (s - 1))
                    with g.Fori(0, T // TOK) as i:
                        for s in range(2):
                            onehot_a(TOK * i + GRP * s, s, 2 * i + (s + 1 + T // GRP), 2 * i + (s - 1 + T // GRP))

                @block.sync
                def _(sp_):
                    sp_.dma_start(sml[:, :], small[bass.ds(layer, 1)].rearrange("a p n -> p (a n)")).then_inc(s_sml, 16)

                    def fetch(q, slot):
                        sp_.dma_start(ring[slot][:, :], stream[bass.ds(layer * PAIRS + q, 1)].rearrange("a p n -> p (a n)"))\
                           .then_inc(landed[slot], 16)

                    for s in range(RING):
                        fetch(s, s)
                    def refill(i, slots=range(RING)):
                        for s in slots:
                            sp_.wait_ge(begun, RING * i + (s - 2))
                            fetch(RING * i + s, s)

                    def loop(lo, hi):
                        with sp_.Fori(lo, hi) as i:
                            refill(i)

                    loop(1, PAIR_OUT // RING)
                    sp_.wait_ge(E["ognorm"], 1)
                    sp_.dma_start(A(0, 2048), subk[bass.ds(layer, 1)].rearrange("a p n -> p (a n)")).then_inc(E["sk"], 16)
                    loop(PAIR_OUT // RING, PAIR_QRY // RING)
                    refill(PAIR_QRY // RING, range(3))
                    sp_.wait_ge(E["h"], 2)
                    sp_.dma_start(spill, X[:, :]).then_inc(spilled, 16)
                    refill(PAIR_QRY // RING, range(3, 4))
                    loop(PAIR_QRY // RING + 1, PAIR_V // RING + 1)
                    sp_.wait_ge(begun, PAIR_V + 1)
                    sp_.wait_ge(spilled, 16)
                    sp_.dma_start(X[:, :], spill).then_inc(reloaded, 16)
                    loop(PAIR_V // RING + 1, PAIRS // RING)

            nc.multi_engine_barrier(list(mybir.ALL_ENGINES), sems_to_clear=range(s_load.num, sems[-1].num + 1))
        with nc.Block() as block:
            @block.sync
            def _(sp_):
                sp_.dma_start(out, X[:, :]).then_inc(s_load, 16)
                sp_.wait_ge(s_load, 16)


def _blocks(w, k):
    n = w.shape[1] // P
    return w.reshape(k, P, n, P).transpose(2, 1, 0, 3)


def _layer_stream(l, w_in, w_uq, w_ukv, w_branch, w_out, w_query, peer_u, peer_v):
    sizes = (QR, KVR, ROPE, 512, 512, 512, 512, H, H, 512, 512, 512, 3 * D)
    cuts = np.cumsum(sizes)[:-1]
    cq, ckv, kr, gq, gk, gv, gz, ga, gb, mq, mk, mv, gates = np.split(w_in[l], cuts, axis=1)
    pad = np.zeros((D, P - ROPE - 2 * H), np.float32)
    misc = np.concatenate([kr, ga, gb, pad], axis=1)
    g = [gates[:, b * D:(b + 1) * D] for b in range(3)]
    order = (0, 2, 1)
    head = np.concatenate([ckv, misc, gk, gq, gv, cq], axis=1)
    out = np.zeros((PAIRS, 2, P, 8, P), np.float32)
    flat = out.reshape(PAIRS * 2, P, 8, P)

    def put(pair, blocks):
        flat[2 * pair:2 * pair + len(blocks)] = blocks

    put(0, _blocks(head, 8))
    flat[2 * PAIR_UKV] = w_ukv[l].reshape(P, 8, P)
    for c in range(2):
        flat[2 * PAIR_UQ + c, :, 0:6] = w_uq[l, c * P:(c + 1) * P].reshape(P, 6, P)
    put(PAIR_MQ, _blocks(np.concatenate([mq, mk, mv, gz], axis=1), 8))
    for n, b in enumerate(order):
        gb_ = _blocks(g[b], 8)
        br = w_branch[l, b].reshape(HC, P, 4, 2, P).transpose(2, 1, 3, 0, 4).reshape(4, P, 8, P)
        for j in range(2):
            put(PAIR_BR + 6 * n + 3 * j, gb_[4 * j:4 * j + 4])
            put(PAIR_BR + 6 * n + 3 * j + 2, br[2 * j:2 * j + 2])
    put(PAIR_OUT, _blocks(w_out[l], 8))
    put(PAIR_QRY, _blocks(w_query[l], 8))
    put(PAIR_U, peer_u[l].reshape(NK, NK, 8, P).transpose(1, 3, 2, 0))
    put(PAIR_V, peer_v[l].reshape(NK, NK, 8, P).transpose(1, 0, 2, 3))
    return out.transpose(0, 2, 1, 3, 4).reshape(PAIRS, P, 2 * BLK)


def kernel(x, c, positions, w_mod, b_mod, w_in, mla_q_gain, mla_w_uq, mla_kv_gain, mla_w_ukv, mla_qn_gain,
           mla_kn_gain, gdn_conv_w, gdn_a_log, gdn_dt_bias, gdn_o_gain, moba_qn_gain, moba_kn_gain, w_branch,
           w_out, peer_w_query, peer_sub_keys, peer_u, peer_v):
    import concourse.bacc as bacc
    from concourse.bass_utils import run_bass_kernel_spmd

    def row(a):
        return np.broadcast_to(a[None, :], (P, a.shape[0]))

    (x, c, positions, w_mod, b_mod, w_in, mla_w_uq, mla_w_ukv, gdn_conv_w, w_branch, w_out, peer_w_query, peer_sub_keys,
     peer_u, peer_v) = (np.asarray(a) for a in (x, c, positions, w_mod, b_mod, w_in, mla_w_uq, mla_w_ukv, gdn_conv_w,
                                                w_branch, w_out, peer_w_query, peer_sub_keys, peer_u, peer_v))
    small = np.zeros((DEPTH, P, NSMALL), np.float32)
    for l in range(DEPTH):
        def put(name, a):
            lo, hi = SMALL[name]
            small[l, :, lo:hi] = a
        cw = np.concatenate([gdn_conv_w[l][:, 512:1024], gdn_conv_w[l][:, 0:512], gdn_conv_w[l][:, 1024:]], axis=1)
        put("conv", cw.reshape(4, 12, P).transpose(2, 1, 0).reshape(P, 48))
        put("q_gain", np.asarray(mla_q_gain[l]).reshape(2, P).T)
        put("kv_gain", np.asarray(mla_kv_gain[l]).reshape(1, P).T)
        put("mq_gain", np.tile(moba_qn_gain[l], 2)[:, None])
        put("mk_gain", np.tile(moba_kn_gain[l], 2)[:, None])
        put("o_gain", np.tile(gdn_o_gain[l], 2)[:, None])
        put("b_mod", b_mod[l].reshape(48, P).T)
        put("qn_row", row(np.asarray(mla_qn_gain[l])))
        put("kn_row", row(np.asarray(mla_kn_gain[l])))
        put("dt_row", row(np.asarray(gdn_dt_bias[l])))
        put("alog_row", row(np.asarray(gdn_a_log[l])))
    stream = np.concatenate([_layer_stream(l, w_in, mla_w_uq, mla_w_ukv, w_branch, w_out, peer_w_query, peer_u, peer_v)
                             for l in range(DEPTH)])
    modw = w_mod.reshape(DEPTH, 4, 2, P, 6, D).transpose(0, 4, 1, 3, 2, 5).reshape(DEPTH * 24, P, 2 * D)
    subk = peer_sub_keys.transpose(0, 4, 1, 2, 3).reshape(DEPTH, P, 2048)
    invf = (10000.0 ** (-np.arange(16, dtype=np.float32) / np.float32(16))).astype(np.float32)
    arrays = {
        "xT": x[0].reshape(T, KD, P).transpose(2, 1, 0).reshape(P, KD * T),
        "cT": c[0].reshape(KD, P).T,
        "pos": positions[0].reshape(NT, P).T,
        "invf": row(invf),
        "stream": stream, "modw": modw, "small": small, "subk": subk,
    }
    arrays = {k: np.ascontiguousarray(a) for k, a in arrays.items()}
    nc = bacc.Bacc("TRN2", target_bir_lowering=False, num_devices=1)
    aps = {k: nc.dram_tensor(k, a.shape, mybir.dt.from_np(a.dtype), kind="ExternalInput").ap() for k, a in arrays.items()}
    out = nc.dram_tensor("out", (P, KD * T), F32, kind="ExternalOutput").ap()
    spill = nc.dram_tensor("spill", (P, KD * T), F32, kind="Internal").ap()
    build(nc, spill=spill, out=out, **aps)
    r = run_bass_kernel_spmd(nc, [arrays], core_ids=[0])
    got = r.results[0]["out"]
    return got.reshape(P, KD, T).transpose(2, 1, 0).reshape(1, T, D)
```

```python
from contextlib import ExitStack

import numpy as np

import concourse.bass as bass
from concourse import mybir

F32 = mybir.dt.float32
F32R = mybir.dt.float32r
BF16 = mybir.dt.bfloat16
U32 = mybir.dt.uint32
ALU = mybir.AluOpType
ACT = mybir.ActivationFunctionType
AX = mybir.AxisListType.X

P = 128
D = 1024
T = 256
NT = T // P
DEPTH = 2
KD = D // P
H = 8
HC = H // 2
EPS = 1e-6
NEG = -1e30
QR, KVR, ROPE, NOPE, MV = 256, 128, 32, 64, 64
QK = NOPE + ROPE
CH = 64
LEVELS = (1, 2, 4, 8, 16, 32)
NK, TOPK = 128, 16
BLK = 8 * P

PAIR_CKV, PAIR_GK, PAIR_GQ, PAIR_GV, PAIR_CQ = 0, 1, 3, 5, 7
PAIR_MQ, PAIR_MK, PAIR_UKV, PAIR_UQ, PAIR_MV, PAIR_Z = 8, 10, 12, 13, 14, 16
PAIR_BR = 18
PAIR_OUT = 36
PAIR_QRY = 40
PAIR_U = 48
PAIR_V = 112
PAIRS = 176
RING = 4

SMALL = {}
_at = 0
for _n, _w in (("conv", 48), ("q_gain", 2), ("kv_gain", 1), ("mq_gain", 1), ("mk_gain", 1), ("o_gain", 1),
               ("b_mod", 48), ("qn_row", QK), ("kn_row", QK), ("dt_row", H), ("alog_row", H)):
    SMALL[_n] = (_at, _at + _w)
    _at += _w
NSMALL = _at


SCHEDULE = [
    ("decay", 0), ("mlakv", 0), ("build", 0), ("mlaq", 0), ("msum", 0), ("level", (0, 2)), ("level", (0, 4)),
    ("mnorm", 0), ("proj", PAIR_MV), ("mlasq", 0), ("level", (0, 8)), ("msum", 1), ("level", (0, 16)),
    ("proj", PAIR_MV + 1), ("mnorm", 1), ("level", (0, 32)), ("mlan", 0), ("proj", PAIR_Z), ("uw", 0), ("mlaT", 0),
    ("decay", 1), ("proj", PAIR_Z + 1), ("head", 0), ("build", 1), ("head", 1), ("head", 2), ("level", (1, 2)),
    ("head", 3), ("level", (1, 4)), ("head", 4), ("head", 5), ("head", 6), ("level", (1, 8)), ("level", (1, 16)),
    ("head", 7), ("head", 8), ("level", (1, 32)), ("head", 9), ("head", 10), ("uw", 1), ("head", 11), ("chunk", 0),
    ("head", 12), ("head", 13), ("chunk", 1), ("head", 14), ("chunk", 2), ("head", 15), ("chunk", 3), ("head", 16),
    ("head", 17), ("head", 18),
]


class Steps:

    def __init__(self, eng, sem):
        self.eng, self.sem, self.n = eng, sem, 0

    def __call__(self, ins):
        self.n += 1
        ins.then_inc(self.sem, 1)
        return self.n

    def done(self, n=None):
        self.eng.wait_ge(self.sem, self.n if n is None else n)


def build(nc, xT, cT, pos, invf, stream, modw, small, subk, spill, out):
    with ExitStack() as ctx:
        def sb(name, n, dt=F32):
            return ctx.enter_context(nc.sbuf_tensor(name, [P, n], dt))

        sems = []

        def sem(name):
            s = ctx.enter_context(nc.semaphore(name))
            sems.append(s)
            return s

        def twin(name, n):
            t = sb(name, n)
            return t, nc.alloc_sbuf_tensor_at(name + "_r", [P, n], F32R, offset=nc.sbuf_base - 4 * n)

        X, X_r = twin("X", KD * T)
        HT, HT_r = twin("HT", KD * T)
        ring, ring_r = zip(*[twin(f"ring{i}", 2 * BLK) for i in range(RING)])
        arena = sb("arena", P * T)
        arena_at = nc.sbuf_base - 4 * P * T
        ident = sb("ident", P)
        ones = sb("ones", P)
        iota = sb("iota", P)
        cst = sb("cst", 4)
        sml = sb("sml", NSMALL)
        heads = sb("heads", 2)
        modn = sb("modn", 2 * KD)
        modc = sb("modc", 6 * KD)
        cact = sb("cact", 2 * KD)
        rope = sb("rope", 2 * NT * 16)
        upper, upper_r = twin("upper", 4 * BLK)
        route_, route_r = twin("route", 2176)
        tiny_f = sb("tiny_f", 64)

        def A(at, n):
            return arena[:, at:at + n]

        def A_r(name, at, n):
            return nc.alloc_sbuf_tensor_at(name, [P, n], F32R, offset=arena_at + 4 * at)[:, :]

        def col(name, i=0, n=1):
            a, _ = SMALL[name]
            return sml[:, a + i:a + i + n]

        x3 = X[:, :].rearrange("p (k t) -> p k t", k=KD)
        h3 = HT[:, :].rearrange("p (k t) -> p k t", k=KD)
        MODP = [A(2048 * i, 2048) for i in range(8)]
        MODR = [A(2048 + 2048 * i, 2048) for i in range(3)]
        ACC = [A(8192 + 1024 * i, 1024) for i in range(3)]
        ACCP = [A(16384 + 1024 * i, 1024) for i in range(2)]
        PRE = A(7168, 12 * 260).rearrange("p (c t) -> p c t", c=12)
        AM, TM, UM, YM, CM = (A(1024 * i, 1024).rearrange("p (g c j) -> p g c j", g=2, c=HC) for i in range(5))
        ATT = [A(5120 + 1024 * i, 1024).rearrange("p (g c j) -> p g c j", g=2, c=HC) for i in range(NT)]
        KBG = A(7168, 1024).rearrange("p (t n) -> p t n", t=NT)
        VB = A(8192, 1024).rearrange("p (t n) -> p t n", t=NT)
        KDEC = A(9216, 1024).rearrange("p (t n) -> p t n", t=NT)
        CONV = A(10288, 3072).rearrange("p (c t) -> p c t", c=12)
        KT, QT, VT = CONV[:, 0:4], CONV[:, 4:8], CONV[:, 8:12]
        QG = A(13360, 1024).rearrange("p (c t) -> p c t", c=HC)
        UV = A(14384, 1024).rearrange("p (t n) -> p t n", t=NT)
        ZS = A(15408, 1024).rearrange("p (c t) -> p c t", c=HC)
        CQ = A(16432, 512).rearrange("p (c t) -> p c t", c=2)
        CKV = A(16944, 256)
        MISC = A(17200, 256)
        MQ = A(17456, 1024).rearrange("p (c t) -> p c t", c=HC)
        MK = A(18480, 1024).rearrange("p (c t) -> p c t", c=HC)
        MVT = A(19504, 1024).rearrange("p (t n) -> p t n", t=NT)
        QTOK = A(20528, 1536).rearrange("p (t n) -> p t n", t=NT)
        KVTOK = A(22064, 2048).rearrange("p (t n) -> p t n", t=NT)
        QTH = A(24112, 2048).rearrange("p (h t) -> p h t", h=H)
        KTH = A(26160, 2048).rearrange("p (h t) -> p h t", h=H)
        PB = [A(28208 + 384 * i, 384) for i in range(3)]
        PTB = [A(28208 + 1152 + 384 * i, 384) for i in range(2)]
        KFULL = A(28208, 1536).rearrange("p (t n) -> p t n", t=NT)
        TA, TB = A(30128, 1024), A(31152, 1024)
        WT = TA.rearrange("p (t c j) -> p t c j", t=NT, c=HC)
        O_MLA = QTOK.rearrange("p t n -> p (t n)")[:, 0:1024].rearrange("p (c t) -> p c t", c=HC)
        O_MOBA = A(16432, 1024).rearrange("p (c t) -> p c t", c=HC)
        O_GDN = VT
        MERGED = A(24112, 2048).rearrange("p (k t) -> p k t", k=KD)
        GATE = [A(26160 + 512 * i, 512) for i in range(4)]
        XSQ, XSUM, XRSTD = A(26160, 2048), A(22064, 512), A(22576, 256)
        sp = [32176]

        def tiny(n):
            a = A(sp[0], n)
            sp[0] += n
            assert sp[0] <= 32768
            return a

        MT = tiny(NT * 48).rearrange("p (t n) -> p t n", t=NT)
        G1, G2, G3, GG, BETA, EGC, EDEC, EB = (tiny(NT * H).rearrange("p (t n) -> p t n", t=NT) for _ in range(8))
        GCL = tiny(NT * 16).rearrange("p (t n) -> p t n", t=NT)
        NEGA = tiny(H)
        SSQ, SSK = (tiny(NT * H).rearrange("p (t n) -> p t n", t=NT) for _ in range(2))
        SSPE = tiny(NT)
        PESQ = tiny(NT * ROPE).rearrange("p (t n) -> p t n", t=NT)
        KPG = tiny(NT * ROPE).rearrange("p (t n) -> p t n", t=NT)
        KROPE = tiny(NT * ROPE).rearrange("p (t n) -> p t n", t=NT)
        ROOT = tiny(32).rearrange("p (b t h) -> p b t h", b=2, t=NT)
        MX, NM, RS, RI = (tiny(3 * 2).rearrange("p (b t) -> p b t", b=3) for _ in range(4))
        EGL = tiny(HC * 4).rearrange("p (c n) -> p c n", c=HC)
        ST = upper[:, 2048:2560].rearrange("p (c j) -> p c j", c=HC)
        EGB = upper[:, 0:2048].rearrange("p (g c t) -> p g c t", g=2, c=HC)
        same = upper[:, 2560:2688]
        strict = upper[:, 2688:2816]
        incl = upper[:, 2816:2944]
        cmask = upper[:, 2944:3328]
        lmask = upper[:, 3328:3328 + len(LEVELS) * P]
        SK = A(0, 2048).rearrange("p (h j n) -> p h j n", h=H, j=2)
        QRY = [A(24576 + 512 * i, 512).rearrange("p (j t) -> p j t", j=2) for i in range(2)]
        TV = A(25600, 512).rearrange("p (t j h k) -> p t j h k", t=NT, j=2, h=H)
        TI = A(26112, 512).bitcast(U32).rearrange("p (t j h k) -> p t j h k", t=NT, j=2, h=H)
        TS = A(26624, 256).rearrange("p (t h k) -> p t h k", t=NT, h=H)
        TP = A(26880, 256).bitcast(U32).rearrange("p (t n) -> p t n", t=NT)
        WORK = [A(27136 + 128 * i, 128) for i in range(4)]
        CAND = A(27648, 512).rearrange("p (t n) -> p t n", t=NT)
        CWORK = A(28160, 512).rearrange("p (t n) -> p t n", t=NT)
        EQ = A(28672, 2048).rearrange("p (h k a) -> p h k a", h=H, k=TOPK)
        TAB = A(30720, 512).rearrange("p (j n) -> p j n", j=2)
        TABU = A(31232, 512).bitcast(U32).rearrange("p (j n) -> p j n", j=2)
        TIF = A(31744, 512).rearrange("p (t j h k) -> p t j h k", t=NT, j=2, h=H)
        IDX = A(32256, 512).rearrange("p (t j n) -> p t j n", t=NT, j=2)
        SM1 = tiny_f[:, 0:NT * H].rearrange("p (t h) -> p t h", t=NT)
        SM2 = tiny_f[:, 16:32].rearrange("p (t h) -> p t h", t=NT)
        IDXT = route_[:, 0:2 * T].rearrange("p (j t) -> p j t", j=2)
        GATES = route_[:, 512:896].bitcast(BF16).rearrange("p (t j) -> p t j", j=3)
        GRP = 4
        TOK = 2 * GRP
        EH = NK // 2
        OHA = [route_[:, 896 + 256 * i:1152 + 256 * i].bitcast(BF16).rearrange("p (t n) -> p t n", t=GRP) for i in range(2)]
        OHB = [route_[:, 1408 + 384 * i:1792 + 384 * i].bitcast(BF16).rearrange("p (t j n) -> p t j n", t=GRP, j=3)
               for i in range(2)]
        GREST = route_[:, 1408:1664]
        I1C = [tiny_f[:, 32 + GRP * i:32 + GRP * (i + 1)] for i in range(2)]
        I1D = [tiny_f[:, 40 + GRP * i:40 + GRP * (i + 1)] for i in range(2)]
        BH = (A_r("branch_h_upper", 22064, 2048).rearrange("p (k t) -> p k t", k=KD), HT_r[:, :].rearrange("p (k t) -> p k t", k=KD))
        OSPLIT = [(route_r[:, 1024 * i:1024 * (i + 1)] if i < 2 else A_r("gdn_upper", 31152, 1024),
                   A_r(f"branch_lower{i}", at, 1024), A(at, 1024))
                  for i, at in enumerate((20528, 16432, 12336))]
        MUP, MLOW = A_r("merged_upper", 28208, 2048), A_r("merged_lower", 24112, 2048)
        UP = [upper_r[:, BLK * i:BLK * (i + 1)].rearrange("p (k n) -> p k n", k=8) for i in range(4)]
        LOW = [[ring_r[s][:, BLK * b:BLK * (b + 1)].rearrange("p (k n) -> p k n", k=8) for b in range(2)]
               for s in range(RING)]
        HUP = X_r[:, :].rearrange("p (k t) -> p k t", k=KD)
        HLOW = HT_r[:, :].rearrange("p (k t) -> p k t", k=KD)
        AUP = [HT_r[:, 1024 * i:1024 * i + 512] for i in range(2)]
        ALOW = [HT_r[:, 1024 * i + 512:1024 * i + 1024] for i in range(2)]
        act3 = arena[:, :].rearrange("p (e t) -> p e t", e=P)

        bank = [ctx.enter_context(nc.psum_tensor(f"bank{i}", [P, 512], F32)) for i in range(8)]
        PT, SB = bank[:2], bank[2:]

        mod_landed = [sem(f"mod_landed{i}") for i in range(3)]
        s_load = sem("first_loads")
        s_sml = sem("small_loaded")
        s_cst = sem("constants_built")
        s_pro = sem("prologue_done")
        first_sem = len(sems)
        landed = [sem(f"pair_landed{i}") for i in range(RING)]
        begun = sem("pair_begun")
        mod0_landed = [sem(f"first_mod{i}") for i in range(8)]
        mod_used = sem("mod_pair_used")
        block_begun = sem("split_block_begun")
        up_ready = sem("upper_halves_ready")
        low_pool = sem("lower_halves_by_gpsimd")
        low_dve = sem("lower_halves_by_vector")
        aup_ready, alow_ready = sem("activations_upper"), sem("activations_lower")
        spilled, reloaded = sem("x_in_dram"), sem("x_back")
        i1_ready = sem("i1_copied")
        mod_acc = sem("mod_partial_ready")
        mod_done = sem("mod_columns_ready")
        p_ready = sem("streamed_product_ready")
        p_evac = sem("streamed_product_taken")
        side_ready = [sem(f"bank{i}_ready") for i in range(6)]
        side_free = [sem(f"bank{i}_free") for i in range(6)]
        c_dve, c_act, c_pool = sem("dve_steps"), sem("act_steps"), sem("pool_steps")
        E = {}
        for n in ("xsq", "xsum", "xstd", "h", "conv", "silu", "gsq", "gstd", "gnorm", "cstd", "cnorm", "csq",
                  "misc", "spa", "spe", "spl", "g", "gcl", "egc", "egb", "diff", "decay", "att", "a", "tok", "t", "u", "y", "cm",
                  "uw", "wt", "vnew", "state", "qg", "msq", "mstd", "mnorm", "qtok", "kvtok", "qksq", "qkss", "qkstd",
                  "qkfull", "rinv", "onorm", "qkT", "pmask", "pexp", "pnorm", "pT", "o", "zs", "gate", "branch", "merged", "x",
                  "osq", "ostd", "ognorm", "qry", "topd", "tope", "idx", "idxT", "ohb", "oha", "wready", "wdone",
                  "sk", "vdone", "zero", "masks", "hup", "hsplit", "bhup", "bhsplit", "oup", "osplit", "mup", "msplit"):
            E[n] = sem("e_" + n)
        last_sem = len(sems)

        n_const = [0]
        with nc.Block() as block:
            @block.sync
            def _(sp_):
                sp_.dma_start(X[:, :], xT).then_inc(s_load, 16)
                sp_.dma_start(cact[:, 0:KD], cT).then_inc(s_load, 16)
                sp_.dma_start(rope[:, 0:16], invf).then_inc(s_load, 16)
                sp_.dma_start(TA[:, 0:NT].bitcast(mybir.dt.int32), pos).then_inc(s_load, 16)
                for n in range(8):
                    sp_.dma_start(MODP[n], modw[n]).then_inc(mod0_landed[n], 16)

            @block.gpsimd
            def _(g):
                st = Steps(g, c_pool)
                for t, v in ((ident, 0.0), (ones, 1.0), (cst, 1.0)):
                    st(g.memset(t[:, :], v))
                st(g.memset(heads[:, :], 0.0))
                st.done()
                for i in range(2):
                    st(g.memset(heads[i * CH:(i + 1) * CH, i:i + 1], 1.0))
                    st.done()
                st(g.iota(iota[:, :], [[1, P]], base=0, channel_multiplier=0, allow_small_or_imprecise_dtypes=True))
                st.done()
                st(g.memset(cst[:, 0:1], EPS))
                st(g.memset(cst[:, 1:2], 64 * EPS))
                st(g.affine_select(out=ident[:, :], in_=ident[:, :], compare_op=ALU.not_equal, fill=1.0, base=0,
                                   pattern=[[-1, P]], channel_multiplier=1))
                st.done()
                n_const[0] = st.n

            @block.tensor
            def _(pe):
                pe.wait_ge(c_pool, n_const[0])
                for m in range(2):
                    pe.wait_ge(mod_acc, m + 1)
                    for j in range(KD):
                        mm = pe.matmul(SB[0][:, m * KD + j:m * KD + j + 1], ACCP[m][:, j * P:(j + 1) * P], ones[:, 0:1],
                                       start=True, stop=True)
                mm.then_inc(mod_done, 1)

            @block.vector
            def _(v):
                st = Steps(v, c_dve)
                v.wait_ge(s_load, 64)
                ang = TB[:, 0:64].rearrange("p (w t f) -> p w t f", w=2, t=NT)
                k = TB[:, 64:128].rearrange("p (w t f) -> p w t f", w=2, t=NT)
                st(v.tensor_copy(TA[:, 8:8 + NT], TA[:, 0:NT].bitcast(mybir.dt.int32)))
                st.done()
                for w in range(2):
                    for t in range(NT):
                        st(v.tensor_scalar(ang[:, w, t], rope[:, 0:16], TA[:, 8 + t:9 + t], None, ALU.mult))
                st.done()
                half = float(np.float32(np.pi / 2))
                for w in range(2):
                    st(v.tensor_scalar(k[:, w], ang[:, w], half if w == 0 else 0.0, 1.0 / (2 * np.pi), ALU.add, ALU.mult))
                st.done()
                st(v.tensor_scalar(k[:, :], k[:, :], 12582912.0, -12582912.0, ALU.add, ALU.add))
                st.done()
                c1 = 6.28125
                c2 = round((2 * np.pi - c1) * 2 ** 20) / 2 ** 20
                c3 = float(2 * np.pi - c1 - c2)
                for c in (c1, c2, c3):
                    st(v.scalar_tensor_tensor(ang[:, :], k[:, :], -c, ang[:, :], ALU.mult, ALU.add))
                    st.done()
                st(v.tensor_scalar(ang[:, 0], ang[:, 0], half, None, ALU.add))
                st.done()
                v.tensor_scalar(ang[:, :], ang[:, :], 3.1415925, -3.1415925, ALU.min, ALU.max).then_inc(s_cst, 1)
                v.wait_ge(s_pro, 1)
                for m in range(2):
                    for k in range(KD):
                        n = 4 * m + k // 2
                        w, c = MODP[n][:, (k % 2) * D:(k % 2 + 1) * D], cact[:, KD + k:KD + k + 1]
                        if k % 2 == 0:
                            v.wait_ge(mod0_landed[n], 16)
                        if k:
                            st.done()
                            ins = v.scalar_tensor_tensor(ACCP[m], w, c, ACCP[m], ALU.mult, ALU.add)
                        else:
                            ins = v.tensor_scalar(ACCP[m], w, c, None, ALU.mult)
                        ins.then_inc(mod_acc, 1) if k == KD - 1 else st(ins)
                v.wait_ge(mod_done, 1)
                st(v.tensor_copy(modn[:, :], SB[0][:, 0:2 * KD]))
                st.done()

            @block.scalar
            def _(a):
                a.wait_ge(s_load, 64)
                a.activation(cact[:, KD:2 * KD], cact[:, 0:KD], ACT.Silu).then_inc(s_pro, 1)
                a.wait_ge(s_cst, 1)
                a.activation(rope[:, :], TB[:, 0:64], ACT.Sin).then_inc(s_pro, 1)

        nc.multi_engine_barrier(list(mybir.ALL_ENGINES),
                                sems_to_clear=range(s_load.num, sems[-1].num + 1))

        COS = rope[:, 0:NT * 16].rearrange("p (t f) -> p t f", t=NT)
        SIN = rope[:, NT * 16:2 * NT * 16].rearrange("p (t f) -> p t f", t=NT)

        with nc.Fori(0, DEPTH) as layer:
            with nc.Block() as block:
                jobs = {}
                njobs = [0]

                def take(eng, name):
                    b, n = jobs[name]
                    eng.wait_ge(side_ready[b], n)
                    return SB[b], side_free[b]

                def freed(eng, name):
                    b, n = jobs[name]
                    eng.wait_ge(side_free[b], n)

                def qk_transposed(eng):
                    for t in range(NT):
                        for j in range(2):
                            freed(eng, f"T0{t}{j}")
                            freed(eng, f"T1{t}{j}")

                prod = {}
                for p in ([*range(0, 12)] + [p for k, p in SCHEDULE if k == "proj"]
                          + [PAIR_BR + 6 * b + 3 * j + i for b in range(3) for j in range(2) for i in range(2)]
                          + [*range(PAIR_QRY, PAIR_QRY + 8)]):
                    prod[p] = len(prod)
                NPROD = len(prod)
                NPOOL = 2 * (PAIR_U + NK // 4 - PAIR_BR)
                QB0 = 2 * (PAIR_QRY - PAIR_BR)
                VB0 = 2 * (PAIR_V - PAIR_BR)
                UH = EH // 2
                assert NPROD % 2 == 0

                @block.tensor
                def _(pe):
                    def side(name):
                        b, n = njobs[0] % 6, njobs[0] // 6
                        njobs[0] += 1
                        if n:
                            pe.wait_ge(side_free[b], n)
                        jobs[name] = (b, n + 1)
                        return SB[b], side_ready[b]

                    def pair_in(p):
                        pe.wait_ge(landed[p % RING], 16 * (p // RING + 1))
                        return ring[p % RING][:, :].rearrange("p (b k n) -> p b k n", b=2, k=8)

                    def project(p, token_major=False):
                        w = pair_in(p)
                        n = prod[p]
                        if n >= 2:
                            pe.wait_ge(p_evac, n - 1)
                        o = PT[n % 2]
                        first = True
                        for b in range(2):
                            for t in range(NT if token_major else 1):
                                for k in range(KD):
                                    if p == 0 and b == 0 and k == 4:
                                        pe.wait_ge(E["h"], 2)
                                    if token_major:
                                        mm = pe.matmul(o[:, (2 * b + t) * P:(2 * b + t + 1) * P],
                                                       h3[:, k, t * P:(t + 1) * P], w[:, b, k], start=k == 0, stop=k == 7)
                                    else:
                                        mm = pe.matmul(o[:, b * T:(b + 1) * T], w[:, b, k], h3[:, k], start=k == 0, stop=k == 7)
                                    if first:
                                        mm.then_inc(begun, 1)
                                        first = False
                        mm.then_inc(p_ready, 1)

                    def modsum(m):
                        pe.wait_ge(mod_acc, m - 1)
                        o, rdy = side(f"mod{m}")
                        for j in range(KD):
                            mm = pe.matmul(o[:, j:j + 1], ACC[m % 3][:, j * P:(j + 1) * P], ones[:, 0:1], start=True, stop=True)
                        mm.then_inc(rdy, 1)

                    def mm1(name, lhsT, rhs, n):
                        o, rdy = side(name)
                        pe.matmul(o[:, 0:n], lhsT, rhs, start=True, stop=True).then_inc(rdy, 1)

                    def norm_of_x(n):
                        o, rdy = side(f"xss{n}")
                        for hf in range(2):
                            pe.wait_ge(E["xsum"], 2 * n + hf + 1)
                            mm = pe.matmul(o[:, 0:T], ones[:, :], XSUM[:, hf * T:(hf + 1) * T], start=hf == 0, stop=hf == 1)
                        mm.then_inc(rdy, 1)

                    def head_sums(name):
                        o, rdy = side("ns" + name)
                        for t in range(NT):
                            for c in range(HC):
                                mm = pe.matmul(o[:, t * H + 2 * c:t * H + 2 * c + 2], TB[:, c * T + t * P:c * T + (t + 1) * P],
                                               heads[:, :], start=True, stop=True)
                        mm.then_inc(rdy, 1)

                    def head_spread(name, n):
                        pe.wait_ge(E["rinv"], n + 1)
                        for j in range(2):
                            o, rdy = side(f"np{name}{j}")
                            for c in range(2 * j, 2 * j + 2):
                                for t in range(NT):
                                    mm = pe.matmul(o[:, (c % 2) * T + t * P:(c % 2) * T + (t + 1) * P],
                                                   TB[:, (t * HC + c) * P:(t * HC + c + 1) * P], ident[:, :],
                                                   start=True, stop=True)
                            mm.then_inc(rdy, 1)

                    norm_of_x(0)
                    pe.wait_ge(E["h"], 1)
                    for p in range(4):
                        project(p)
                    pe.wait_ge(p_evac, 1)
                    o, rdy = side("misc")
                    for t in range(NT):
                        mm = pe.transpose(o[:, t * 48:(t + 1) * 48], MISC[0:48, t * P:(t + 1) * P], ident[0:48, 0:48])
                    mm.then_inc(rdy, 1)

                    project(4)
                    project(5)
                    pe.wait_ge(E["masks"], 1)
                    pe.wait_ge(E["gsq"], 1)
                    head_sums("k")
                    project(6)
                    head_spread("k", 0)
                    pe.wait_ge(E["g"], 1)
                    o, rdy = side("gcl")
                    for t in range(NT):
                        pe.matmul(o[:, t * 16:t * 16 + 8], incl, GG[:, t], start=True, stop=True)
                        mm = pe.matmul(o[:, t * 16 + 8:t * 16 + 16], same, GG[:, t], start=True, stop=True)
                    mm.then_inc(rdy, 1)
                    project(PAIR_CQ)
                    pe.wait_ge(E["gsq"], 2)
                    head_sums("q")
                    project(PAIR_MQ)
                    pe.wait_ge(E["csq"], 1)
                    o, rdy = side("css")
                    for c in range(2):
                        pe.matmul(o[:, 0:T], ones[:, :], TA[:, c * T:(c + 1) * T], start=c == 0, stop=c == 1)
                    pe.matmul(o[:, T:2 * T], ones[:, :], TA[:, 2 * T:3 * T], start=True, stop=True).then_inc(rdy, 1)
                    head_spread("q", 1)
                    project(PAIR_MQ + 1)
                    for name, src, ev, n in (("k", KT, "gnorm", 1), ("v", VT, "silu", 3)):
                        pe.wait_ge(E[ev], n)
                        for t in range(NT):
                            o, rdy = side(f"tok{name}{t}")
                            for c in range(HC):
                                mm = pe.transpose(o[:, c * P:(c + 1) * P], src[:, c, t * P:(t + 1) * P], ident[:, :])
                            mm.then_inc(rdy, 1)
                        project(PAIR_MK if name == "k" else PAIR_MK + 1)

                    def half(par):
                        return slice(par * CH, par * CH + CH)

                    def head_step(i):
                        if i < 2 * H:
                            o, rdy = side(f"S{i}")
                            if i < H:
                                if i == 0:
                                    qk_transposed(pe)
                                q, k = QTH[0:QK, i], KTH[0:QK, i]
                            else:
                                if i == H:
                                    pe.wait_ge(E["mnorm"], 2)
                                h = i - H
                                q, k = MQ[half(h % 2), h // 2], MK[half(h % 2), h // 2]
                            pe.matmul(o[:, 0:P], q[:, 0:P], k[:, 0:P], start=True, stop=True)
                            pe.matmul(o[:, P:3 * P], q[:, P:T], k[:, 0:T], start=True, stop=True).then_inc(rdy, 1)
                        i2 = i - 2
                        if 0 <= i2 < 2 * H:
                            pe.wait_ge(E["pnorm"], i2 + 1)
                            o, rdy = side(f"PT{i2}")
                            for b in range(3):
                                mm = pe.transpose(o[:, b * P:(b + 1) * P], PB[i2 % 3][:, b * P:(b + 1) * P], ident[:, :])
                            mm.then_inc(rdy, 1)
                        i3 = i - 3
                        if 0 <= i3 < 2 * H:
                            freed(pe, f"PT{i3}")
                            if i3 == H:
                                pe.wait_ge(p_evac, prod[PAIR_MV + 1] + 1)
                            o, rdy = side(f"O{i3}")
                            oo = o[half(i3 % 2), :]
                            for t in range(NT):
                                v = (KVTOK[:, t, i3 * P + NOPE:(i3 + 1) * P] if i3 < H
                                     else MVT[:, t, (i3 - H) * CH:(i3 - H + 1) * CH])
                                src = PTB[i3 % 2][:, 0:T] if t == 0 else PTB[i3 % 2][:, T:T + P]
                                mm = pe.matmul(oo[:, t * P:T], v, src, start=t == 0, stop=t == 1, skip_group_check=True)
                            mm.then_inc(rdy, 1)

                    for kind, i in SCHEDULE:
                        if kind == "proj":
                            project(i, token_major=i in (PAIR_MV, PAIR_MV + 1))
                        elif kind == "msum":
                            pe.wait_ge(E["msq"], i + 1)
                            head_sums(f"m{i}")
                        elif kind == "mnorm":
                            head_spread(f"m{i}", 2 + i)
                        elif kind == "mlakv":
                            w = pair_in(PAIR_UKV)
                            pe.wait_ge(E["cnorm"], 1)
                            for t in range(NT):
                                for j in range(2):
                                    o, rdy = side(f"kv{t}{j}")
                                    for k in range(2):
                                        mm = pe.matmul(o[:, k * T:(k + 1) * T], CKV[:, t * P:(t + 1) * P],
                                                       w[:, 0, 4 * j + 2 * k:4 * j + 2 * k + 2].rearrange("p k n -> p (k n)"),
                                                       start=True, stop=True)
                                        if t == j == k == 0:
                                            mm.then_inc(begun, 1)
                                    mm.then_inc(rdy, 1)
                        elif kind == "mlaq":
                            w = [pair_in(PAIR_UQ)[:, c].rearrange("p k n -> p (k n)") for c in range(2)]
                            for t in range(NT):
                                for j in range(2):
                                    o, rdy = side(f"q{t}{j}")
                                    n = 512 if j == 0 else 256
                                    for c in range(2):
                                        mm = pe.matmul(o[:, 0:n], CQ[:, c, t * P:(t + 1) * P], w[c][:, 512 * j:512 * j + n],
                                                       start=c == 0, stop=c == 1)
                                        if t == j == c == 0:
                                            mm.then_inc(begun, 1)
                                    mm.then_inc(rdy, 1)
                        elif kind == "mlaT":
                            for n, src in enumerate((QTOK, KFULL)):
                                pe.wait_ge(E["qkfull"], n + 1)
                                for t in range(NT):
                                    for j in range(2):
                                        o, rdy = side(f"T{n}{t}{j}")
                                        for h in range(4):
                                            a = (4 * j + h) * QK
                                            mm = pe.transpose(o[0:QK, h * P:(h + 1) * P], src[:, t, a:a + QK], ident[:, :])
                                        mm.then_inc(rdy, 1)
                        elif kind == "head":
                            head_step(i)
                        elif kind == "decay":
                            for par in range(2):
                                o, rdy = side(f"gcb{i}{par}")
                                for c in range(HC):
                                    h = 2 * c + par
                                    mm = pe.matmul(o[:, c * P:(c + 1) * P], GG[:, i, h:h + 1].to_broadcast([P, P]), incl,
                                                   start=True, stop=True)
                                mm.then_inc(rdy, 1)
                        elif kind == "build":
                            t = slice(i * P, (i + 1) * P)
                            pe.wait_ge(E["gnorm"], 2)
                            for name, b in (("G", QT), ("G", KT))[::-1]:
                                for par in range(2):
                                    o, rdy = side(f"{'GK' if b is KT else 'GQ'}{i}{par}")
                                    for c in range(HC):
                                        mm = pe.matmul(o[:, c * P:(c + 1) * P], KT[half(par), c, t], b[half(par), c, t],
                                                       start=True, stop=True)
                                    mm.then_inc(rdy, 1)
                            pe.wait_ge(E["cm"], len(LEVELS) * i + 1)
                            for par in range(2):
                                o, rdy = side(f"Y{i}{1}{par}")
                                for c in range(HC):
                                    mm = pe.matmul(o[:, c * P:(c + 1) * P], CM[:, par, c], ident[:, :], start=True, stop=True)
                                mm.then_inc(rdy, 1)
                        elif kind == "level":
                            t, s = i
                            n = len(LEVELS) * t + LEVELS.index(s)
                            pe.wait_ge(E["cm"], n + 1)
                            pe.wait_ge(E["u"], n)
                            for par in range(2):
                                o, rdy = side(f"Y{t}{s}{par}")
                                for c in range(HC):
                                    mm = pe.matmul(o[:, c * P:(c + 1) * P], CM[:, par, c], UM[:, par, c], start=True, stop=True)
                                mm.then_inc(rdy, 1)
                            pe.wait_ge(E["t"], (len(LEVELS) - 1) * t + LEVELS.index(s))
                            for par in range(2):
                                if par == 0:
                                    freed(pe, f"Y{t}{s}0")
                                else:
                                    pe.wait_ge(E["y"], (len(LEVELS) - 1) * t + LEVELS.index(s))
                                o, rdy = side(f"U{t}{s}{par}")
                                for c in range(HC):
                                    mm = pe.matmul(o[:, c * P:(c + 1) * P], TM[:, par, c], YM[:, par, c], start=True, stop=True)
                                mm.then_inc(rdy, 1)
                            if s != LEVELS[-1]:
                                for par in range(2):
                                    o, rdy = side(f"TT{t}{s}{par}")
                                    for c in range(HC):
                                        mm = pe.matmul(o[:, c * P:(c + 1) * P], YM[:, par, c], TM[:, par, c],
                                                       start=True, stop=True)
                                    mm.then_inc(rdy, 1)
                        elif kind == "uw":
                            pe.wait_ge(E["u"], len(LEVELS) * (i + 1))
                            pe.wait_ge(E["tok"], 3 * NT)
                            for par in range(2):
                                o, rdy = side(f"uu{i}{par}")
                                for c in range(HC):
                                    mm = pe.matmul(o[:, c * P:(c + 1) * P], UM[:, par, c], VB[:, i, c * P:(c + 1) * P],
                                                   start=True, stop=True)
                                mm.then_inc(rdy, 1)
                            o, rdy = side(f"wt{i}")
                            for c in range(HC):
                                for par in range(2):
                                    h = 2 * c + par
                                    mm = pe.matmul(o[half(par), c * P:(c + 1) * P], KBG[:, i, h * CH:(h + 1) * CH], UM[:, par, c],
                                                   start=True, stop=True, skip_group_check=True)
                            mm.then_inc(rdy, 1)
                        elif kind == "chunk":
                            n, t, hf = i, i // 2, half(i % 2)
                            cols = slice((i % 2) * CH, (i % 2) * CH + CH)
                            pe.wait_ge(E["state"], n + 1)
                            if n == 0:
                                pe.wait_ge(E["wt"], NT)
                            o, rdy = side(f"ws{n}")
                            for c in range(HC):
                                mm = pe.matmul(o[hf, c * P:(c + 1) * P], WT[:, t, c, cols], ST[:, c], start=True, stop=True)
                            mm.then_inc(rdy, 1)
                            pe.wait_ge(E["qg"], 8)
                            o, rdy = side(f"og{n}")
                            for c in range(HC):
                                pe.matmul(o[:, c * CH:(c + 1) * CH], ST[:, c], QG[:, c, n * CH:(n + 1) * CH],
                                          start=c == 0, stop=False, skip_group_check=True)
                            pe.wait_ge(E["vnew"], n + 1)
                            for c in range(HC):
                                for par in range(2):
                                    h = 2 * c + par
                                    mm = pe.matmul(o[half(par), c * CH:(c + 1) * CH], UV[:, t, h * CH:(h + 1) * CH],
                                                   ATT[t][:, par, c, cols], start=False, stop=True, skip_group_check=True)
                            mm.then_inc(rdy, 1)
                            if n < T // CH - 1:
                                o, rdy = side(f"ds{n}")
                                for c in range(HC):
                                    mm = pe.matmul(o[:, c * P:(c + 1) * P], KDEC[hf, t, c * P:(c + 1) * P],
                                                   UV[hf, t, c * P:(c + 1) * P], start=True, stop=True)
                                mm.then_inc(rdy, 1)
                    def split_products(slot, b, low_sem, n_low, out_of, up, low, before=None):
                        pe.wait_ge(low_sem, n_low)
                        wu, wl = UP[2 * (slot % 2) + b], LOW[slot][b]
                        for k in range(KD):
                            if before:
                                before(k)
                            for i, (w, x) in enumerate(((wu, up), (wu, low), (wl, up))):
                                o, start, stop = out_of(k, i)
                                mm = pe.matmul(o, w[:, k], x(k), start=start, stop=stop, skip_group_check=True)
                                if k == 0 and i == 0 and b == 0:
                                    mm.then_inc(begun, 1)
                                if k == 0 and i == 1:
                                    mm.then_inc(block_begun, 1)
                        return mm

                    def against_h(slot, o, low_sem, n_low, up=HUP, low=HLOW, before=None):
                        for b in range(2):
                            mm = split_products(slot, b, low_sem, n_low + b,
                                                lambda k, i, b=b: (o[:, b * T:(b + 1) * T], k == 0 and i == 0, k == KD - 1 and i == 2),
                                                lambda k: up[:, k], lambda k: low[:, k], before if b == 0 else None)
                        mm.then_inc(p_ready, 1)

                    pe.wait_ge(E["bhsplit"], 1)
                    for b in range(3):
                        for j in range(2):
                            for i in range(2):
                                p = PAIR_BR + 6 * b + 3 * j + i
                                pe.wait_ge(p_evac, prod[p] - 1)
                                against_h(p % RING, PT[prod[p] % 2], low_pool, 2 * (p - PAIR_BR) + 1, *BH)
                                if p == PAIR_BR:
                                    pe.wait_ge(E["osq"], 1)
                                    head_sums("o")
                                elif p == PAIR_BR + 1:
                                    head_spread("o", 4)
                            p = PAIR_BR + 6 * b + 3 * j + 2
                            pe.wait_ge(E["osplit"], b + 1)
                            up, low = (x.rearrange("p (c t) -> p c t", c=HC) for x in OSPLIT[b][0:2])
                            for i in range(2):
                                o, rdy = side(f"br{b}{j}{i}")
                                mm = split_products(p % RING, i, low_pool, 2 * (p - PAIR_BR) + 1 + i,
                                                    lambda k, t, o=o: (o[:, k // HC * T:(k // HC + 1) * T], k % HC == 0 and t == 0,
                                                                       k % HC == HC - 1 and t == 2),
                                                    lambda k: up[:, k % HC], lambda k: low[:, k % HC])
                                mm.then_inc(rdy, 1)
                            if (b, j) in ((1, 1), (2, 0)):
                                modsum(2 if b == 1 else 3)
                    def merged_in(k):
                        if k % 2 == 0:
                            pe.wait_ge(E["msplit"], k // 2 + 1)

                    up, low = (x.rearrange("p (k t) -> p k t", k=KD) for x in (MUP, MLOW))
                    for p in range(4):
                        o, rdy = side(f"y{p}")
                        for i in range(2):
                            mm = split_products((PAIR_OUT + p) % RING, i, low_pool, 2 * (PAIR_OUT + p - PAIR_BR) + 1 + i,
                                                lambda k, t, o=o, i=i: (o[:, i * T:(i + 1) * T], k == 0 and t == 0,
                                                                        k == KD - 1 and t == 2),
                                                lambda k: up[:, k], lambda k: low[:, k], merged_in if p == i == 0 else None)
                        mm.then_inc(rdy, 1)
                        if p == 1:
                            modsum(4)
                    norm_of_x(1)
                    def h_in(k):
                        if k % 4 == 0:
                            pe.wait_ge(E["hsplit"], k // 4 + 1)

                    pe.wait_ge(E["sk"], 16)

                    for h in range(H + 1):
                        if h < H:
                            p = PAIR_QRY + h
                            pe.wait_ge(p_evac, prod[p] - 1)
                            against_h(p % RING, PT[prod[p] % 2], low_pool, QB0 + 2 * h + 1,
                                      before=h_in if h == 0 else None)
                        if h:
                            pe.wait_ge(p_evac, prod[PAIR_QRY + h - 1] + 1)
                            o, rdy = side(f"sc{h - 1}")
                            for t in range(NT):
                                for j in range(2):
                                    mm = pe.matmul(o[:, (2 * t + j) * P:(2 * t + j + 1) * P],
                                                   QRY[(h - 1) % 2][:, j, t * P:(t + 1) * P], SK[:, h - 1, j],
                                                   start=True, stop=True)
                            mm.then_inc(rdy, 1)

                    def route(n, slot, n_free):
                        if n_free is not None:
                            pe.wait_ge(E["wdone"], n_free)
                        for s in range(2):
                            pe.wait_ge(E["ohb"], n + s)
                            pe.wait_ge(E["oha"], n + s)
                            for k in range(GRP):
                                a = (GRP * s + k) * EH
                                for j in range(3):
                                    mm = pe.matmul(SB[4 + slot][:, a:a + EH], OHA[s][:, k], OHB[s][:, k, j],
                                                   start=j == 0, stop=j == 2)
                            mm.then_inc(E["wready"], 1)

                    with pe.Fori(0, UH // RING) as i:
                        for s in range(RING):
                            pe.wait_ge(p_evac, RING * i + (NPROD + s - 1))
                            against_h(s, PT[s % 2], low_pool, 8 * i + (QB0 + 2 * H + 2 * s + 1))
                    pe.wait_ge(E["idx"], 1)
                    for t in range(NT):
                        o, rdy = side(f"ix{t}")
                        for j in range(3):
                            src = IDX[:, t, j] if j < 2 else TS[:, t].rearrange("p h k -> p (h k)")
                            mm = pe.transpose(o[:, j * P:(j + 1) * P], src, ident[:, :])
                        mm.then_inc(rdy, 1)

                    def u_and_route(i, s, n_free):
                        pe.wait_ge(p_evac, RING * i + (NPROD + UH + s - 1))
                        against_h(s, PT[s % 2], low_dve, 8 * i + (2 * s + 1))
                        if n_free is None and s == 0:
                            for b in range(6):
                                pe.wait_ge(side_free[b], sum(1 for k, _ in jobs.values() if k == b))
                        route(8 * i + (2 * s + 1), s % 2, n_free)

                    for s in range(RING):
                        u_and_route(0, s, s - 1 if s >= 2 else None)
                    with pe.Fori(1, UH // RING) as i:
                        for s in range(RING):
                            u_and_route(i, s, RING * i + (s - 1))

                    def expert_out(slot, n_low, n_act, first=False, last=False):
                        pe.wait_ge(alow_ready, n_act)
                        for b in range(2):
                            mm = split_products(slot, b, low_dve, n_low + b,
                                                lambda k, i, b=b: (SB[k // 2][:, (k % 2) * T:(k % 2 + 1) * T],
                                                                   first and b == 0 and k % 2 == 0 and i == 0,
                                                                   last and b == 1 and i == 2),
                                                lambda k, b=b: AUP[slot % 2][:, b * T:(b + 1) * T],
                                                lambda k, b=b: ALOW[slot % 2][:, b * T:(b + 1) * T])
                        return mm

                    def v_and_route(i, s, first=False):
                        expert_out(s, 8 * i + (2 * UH + 2 * s + 1), RING * i + (s + 1), first)
                        route(8 * i + (T // GRP + 2 * s + 1), s % 2, RING * i + (T // TOK + s - 1))

                    for s in range(RING):
                        v_and_route(0, s, s == 0)
                    with pe.Fori(1, UH // RING) as i:
                        for s in range(RING):
                            v_and_route(i, s)
                    def v_loop(lo, hi):
                        with pe.Fori(lo, hi) as i:
                            for s in range(RING):
                                expert_out(s, 8 * i + (2 * UH + 2 * s + 1), RING * i + (s + 1))

                    v_loop(UH // RING, 2 * UH // RING - 1)
                    pe.wait_ge(E["wdone"], 2 * T // TOK)
                    for m in range(3):
                        pe.wait_ge(mod_acc, 4 + m)
                        for j in range(KD):
                            mm = pe.matmul(SB[4][:, m * KD + j:m * KD + j + 1], ACC[(5 + m) % 3][:, j * P:(j + 1) * P], ones[:, 0:1],
                                           start=True, stop=True)
                    mm.then_inc(mod_done, 1)
                    i = 2 * UH // RING - 1
                    for s in range(RING):
                        mm = expert_out(s, 8 * i + (2 * UH + 2 * s + 1), RING * i + (s + 1), last=s == RING - 1)
                    mm.then_inc(E["vdone"], 1)

                @block.scalar
                def _(act):
                    st = Steps(act, c_act)

                    def f(o, i, fn, ev=None, **kw):
                        ins = act.activation(o, i, fn, **kw)
                        if ev is None:
                            return st(ins)
                        ins.then_inc(ev, 1)

                    def evac(p, o, i, fn=ACT.Copy):
                        f(o, i, fn, p_evac)

                    def got(p):
                        n = prod[p]
                        act.wait_ge(p_ready, n + 1)
                        return PT[n % 2]

                    def std(name, o, i, scale, bias, ev):
                        b, free = take(act, name)
                        f(o, b[:, i[0]:i[1]], ACT.Sqrt, free, scale=scale, bias=bias)

                    eps, eps64, one = cst[:, 0:1], cst[:, 1:2], cst[:, 2:3]
                    for hf in range(2):
                        cols = slice(4 * T * hf, 4 * T * (hf + 1))
                        f(XSQ[:, cols], X[:, cols], ACT.Square, E["xsq"])
                    std("xss0", XRSTD, (0, T), 1.0 / D, eps, "xstd")
                    def evac_head(p):
                        b = got(p)
                        if p == PAIR_CKV:
                            evac(p, A(16944, 512), b[:, :])
                        elif p < PAIR_CQ:
                            c = 2 * (p - PAIR_GK)
                            evac(p, PRE[:, c:c + 2, 3:3 + T], b[:, :].rearrange("p (b t) -> p b t", b=2))
                        elif p == PAIR_CQ:
                            evac(p, CQ[:, :, :].rearrange("p c t -> p (c t)"), b[:, :])
                        else:
                            dst = MQ if p < PAIR_MK else MK
                            c = 2 * ((p - PAIR_MQ) % 2)
                            evac(p, dst[:, c:c + 2].rearrange("p c t -> p (c t)"), b[:, :])

                    def silu(i):
                        act.wait_ge(E["conv"], i + 1)
                        g = CONV[:, 4 * i:4 * i + 4]
                        f(g, g, ACT.Silu, E["silu"])

                    def square(i):
                        if i:
                            act.wait_ge(E["gnorm"], 1)
                        act.wait_ge(E["silu"], i + 1)
                        f(TB, CONV[:, 4 * i:4 * i + 4].rearrange("p c t -> p (c t)"), ACT.Square, E["gsq"])

                    def root(name, n, scale, bias):
                        std("ns" + name, ROOT[:, n % 2].rearrange("p t h -> p (t h)"), (0, NT * H), scale, bias, None)

                    for p in range(4):
                        evac_head(p)
                    silu(0)
                    square(0)
                    evac_head(4)
                    act.wait_ge(E["spa"], 1)
                    f(G1, G1, ACT.Exp, E["spe"], scale=-1.0)
                    f(BETA, MT[:, :, 40:48], ACT.Exp, E["spe"], scale=-1.0)
                    f(NEGA, col("alog_row", 0, H), ACT.Exp, E["spe"])
                    act.wait_ge(E["spe"], 3)
                    f(G1, G1, ACT.Ln, E["spl"], bias=one)
                    evac_head(5)
                    root("k", 0, 1.0, eps)
                    silu(1)
                    evac_head(6)
                    square(1)
                    evac_head(PAIR_CQ)
                    act.wait_ge(p_evac, PAIR_CQ + 1)
                    f(TA[:, 0:768], A(16432, 768), ACT.Square, E["csq"])
                    root("q", 1, 64.0, eps64)
                    silu(2)
                    evac_head(PAIR_MQ)
                    b, free = take(act, "css")
                    f(TA[:, 0:256], b[:, 0:T], ACT.Sqrt, E["cstd"], scale=1.0 / QR, bias=eps)
                    f(TA[:, 256:512], b[:, T:2 * T], ACT.Sqrt, free, scale=1.0 / KVR, bias=eps)
                    evac_head(PAIR_MQ + 1)
                    act.wait_ge(E["gcl"], 2)
                    f(EGC, GCL[:, :, 0:8], ACT.Exp, E["egc"])
                    f(EDEC, EDEC, ACT.Exp, E["egc"])
                    evac_head(PAIR_MK)
                    evac_head(PAIR_MK + 1)

                    def evac_act(name, o, i, ev=None, fn=ACT.Copy):
                        b, free = take(act, name)
                        f(o, i(b), fn, free)

                    def upper_of(slot, b, n_landed, n_begun):
                        act.wait_ge(landed[slot], n_landed)
                        if n_begun is not None:
                            act.wait_ge(block_begun, n_begun)
                        at = BLK * (2 * (slot % 2) + b)
                        f(upper_r[:, at:at + BLK], ring[slot][:, BLK * b:BLK * (b + 1)], ACT.Copy, up_ready)

                    def upper_pair(p):
                        for b in range(2):
                            n = 2 * (p - PAIR_BR) + b - 2
                            upper_of(p % RING, b, 16 * (p // RING + 1), n if n >= 2 else None)

                    for kind, i in SCHEDULE:
                        if kind == "chunk" and i == 1:
                            take(act, "ds0")
                            upper_pair(PAIR_BR)
                        if kind == "proj":
                            b = got(i)
                            if i in (PAIR_MV, PAIR_MV + 1):
                                a = 2 * P * (i - PAIR_MV)
                                evac(i, MVT[:, :, a:a + 2 * P].rearrange("p t (b n) -> p b t n", b=2),
                                     b[:, :].rearrange("p (b t n) -> p b t n", b=2, t=NT))
                            else:
                                evac(i, ZS[:, 2 * (i - PAIR_Z):2 * (i - PAIR_Z) + 2].rearrange("p c t -> p (c t)"), b[:, :],
                                     ACT.Silu)
                        elif kind == "msum":
                            src = (MQ, MK)[i]
                            act.wait_ge(p_evac, prod[(PAIR_MQ, PAIR_MK)[i] + 1] + 1)
                            act.wait_ge(E["gnorm"], 2) if i == 0 else act.wait_ge(E["mnorm"], 1)
                            f(TB, src[:, :].rearrange("p c t -> p (c t)"), ACT.Square, E["msq"])
                            root(f"m{i}", 2 + i, 1.0 / CH, eps)
                        elif kind == "mlakv":
                            for t in range(NT):
                                for j in range(2):
                                    evac_act(f"kv{t}{j}", KVTOK[:, t, j * 512:(j + 1) * 512], lambda b: b[:, :])
                        elif kind == "mlaq":
                            for t in range(NT):
                                for j in range(2):
                                    n = 512 if j == 0 else 256
                                    evac_act(f"q{t}{j}", QTOK[:, t, j * 512:j * 512 + n], lambda b, n=n: b[:, 0:n])
                        elif kind == "mlasq":
                            act.wait_ge(E["qkss"], 1)
                            f(SSQ, SSQ, ACT.Sqrt, E["qkstd"], scale=1.0 / QK, bias=eps)
                            f(SSK, SSK, ACT.Sqrt, E["qkstd"], scale=1.0 / QK, bias=eps)
                        elif kind == "mlaT":
                            for n, dst in enumerate((QTH, KTH)):
                                for t in range(NT):
                                    for j in range(2):
                                        b, free = take(act, f"T{n}{t}{j}")
                                        f(dst[0:QK, 4 * j:4 * j + 4, t * P:(t + 1) * P],
                                          b[0:QK, :].rearrange("p (h t) -> p h t", h=4), ACT.Copy, free)
                        elif kind == "head":
                            if i == H + 4:
                                for h in range(H):
                                    freed(act, f"O{h}")
                                act.wait_ge(p_evac, prod[PAIR_Z + 1] + 1)
                                f(BH[0].rearrange("p k t -> p (k t)"), HT[:, :], ACT.Copy, E["bhup"])
                                f(OSPLIT[0][0], OSPLIT[0][2], ACT.Copy, E["oup"])
                            if i < 2 * H:
                                act.wait_ge(E["pmask"], i + 1)
                                sc = QK ** -0.5 if i < H else CH ** -0.5
                                for t in range(NT):
                                    a = slice(0, P) if t == 0 else slice(P, 3 * P)
                                    act.activation(PB[i % 3][:, a], PB[i % 3][:, a], ACT.Exp, bias=NM[:, i % 3, t:t + 1],
                                                   scale=sc, accum_out=RS[:, i % 3, t:t + 1]).then_inc(E["pexp"], 1)
                            i2 = i - 2
                            if 0 <= i2 < 2 * H:
                                if i2 >= 2:
                                    take(act, f"O{i2 - 2}")
                                b, free = take(act, f"PT{i2}")
                                f(PTB[i2 % 2], b[:, 0:384], ACT.Copy, free)
                            i3 = i - 3
                            if 0 <= i3 < 2 * H:
                                b, free = take(act, f"O{i3}")
                                rows = slice((i3 % 2) * CH, (i3 % 2) * CH + CH)
                                dst = O_MLA[rows, i3 // 2] if i3 < H else O_MOBA[rows, i3 // 2 - HC]
                                f(dst, b[rows, 0:T], ACT.Copy, free)
                        elif kind == "decay":
                            for par in range(2):
                                b, free = take(act, f"gcb{i}{par}")
                                f(EGB[:, par, :, i * P:(i + 1) * P], b[:, :].rearrange("p (c t) -> p c t", c=HC), ACT.Exp, E["egb"])
                            act.wait_ge(E["diff"], 16 * (i + 1))
                            f(AM[:, :], AM[:, :], ACT.Exp, E["decay"], scale=-1.0)
                            f(ATT[i][:, :], ATT[i][:, :], ACT.Exp, E["decay"])
                        elif kind == "level":
                            t, s = i
                            for par in range(2):
                                b, free = take(act, f"Y{t}{s}{par}")
                                f(YM[:, par].rearrange("p c j -> p (c j)"), b[:, :], ACT.Copy, free if par == 0 else E["y"])
                        elif kind == "chunk":
                            b, free = take(act, f"og{i}")
                            f(O_GDN[:, :, i * CH:(i + 1) * CH], b[:, 0:HC * CH].rearrange("p (c t) -> p c t", c=HC), ACT.Copy, free)
                    def o_upper(b):
                        f(OSPLIT[b][0], OSPLIT[b][2], ACT.Copy, E["oup"])

                    upper_pair(PAIR_BR + 1)
                    for h in range(H, 2 * H):
                        freed(act, f"O{h}")
                    o_upper(1)
                    for n in range(T // CH):
                        freed(act, f"og{n}")
                    act.wait_ge(E["mnorm"], 2)
                    f(TB, VT.rearrange("p c t -> p (c t)"), ACT.Square, E["osq"])
                    root("o", 4, 1.0 / CH, eps)
                    def merged_upper(m):
                        act.wait_ge(E["gate"], 8 + m + 1)
                        f(MUP[:, 512 * m:512 * (m + 1)], MERGED[:, 2 * m:2 * m + 2].rearrange("p k t -> p (k t)"), ACT.Copy, E["mup"])

                    for b in range(3):
                        for j in range(2):
                            for i in range(3):
                                p = PAIR_BR + 6 * b + 3 * j + i
                                n = 4 * b + 2 * j + i
                                if p > PAIR_BR:
                                    upper_pair(p + 1)
                                if i == 2:
                                    continue
                                if n >= 4:
                                    act.wait_ge(E["gate"], n - 3)
                                o = got(p)
                                evac(p, GATE[n % 4], o[:, :], ACT.Sigmoid)
                                if n == 3:
                                    act.wait_ge(E["ognorm"], 1)
                                    o_upper(2)
                                if n == 10:
                                    merged_upper(0)
                                    merged_upper(1)
                    merged_upper(2)
                    merged_upper(3)
                    for p in range(PAIR_OUT + 1, PAIR_QRY + 1):
                        upper_pair(p)
                    for hf in range(2):
                        act.wait_ge(E["x"], 4 * (hf + 1))
                        cols = slice(4 * T * hf, 4 * T * (hf + 1))
                        f(XSQ[:, cols], X[:, cols], ACT.Square, E["xsq"])
                    std("xss1", XRSTD, (0, T), 1.0 / D, eps, "xstd")
                    act.wait_ge(spilled, 16)
                    for hf in range(2):
                        cols = slice(4 * T * hf, 4 * T * (hf + 1))
                        act.wait_ge(E["h"], hf + 3)
                        f(X_r[:, cols], HT[:, cols], ACT.Copy, E["hup"])

                    for h in range(H):
                        upper_pair(PAIR_QRY + h + 1)
                        if h >= 2:
                            take(act, f"sc{h - 2}")
                        o = got(PAIR_QRY + h)
                        evac(PAIR_QRY + h, QRY[h % 2].rearrange("p j t -> p (j t)"), o[:, :])
                    take(act, f"sc{H - 1}")

                    def gelu(n, slot, e):
                        act.wait_ge(p_ready, n)
                        f(act3[:, bass.ds(e, 2)].rearrange("p a t -> p (a t)"), PT[slot % 2][:, :], ACT.Gelu, p_evac)

                    def u_loop(lo, hi):
                        with act.Fori(lo, hi) as i:
                            for s in range(RING):
                                for b in range(2):
                                    upper_of((s + 1) % RING, b, 16 * i + 16 * (PAIR_U // RING + (2 if s == RING - 1 else 1)),
                                             8 * i + (QB0 + 2 * H + 2 * s + b))
                                gelu(RING * i + (NPROD + s + 1), s, 2 * RING * i + 2 * s)

                    u_loop(0, 4)
                    act.wait_ge(E["topd"], 1)
                    f(TS[:, :, :, :], TS[:, :, :, :], ACT.Exp, E["tope"])
                    u_loop(4, UH // RING)
                    u_loop(UH // RING, 3 * UH // RING // 2)
                    act.wait_ge(E["idxT"], NT)
                    u_loop(3 * UH // RING // 2, 2 * UH // RING)

                    def act_upper(slot, n_begun, e, n_w):
                        if n_begun is not None:
                            act.wait_ge(block_begun, n_begun)
                        act.wait_ge(E["wdone"], n_w)
                        f(AUP[slot % 2], act3[:, bass.ds(e, 2)].rearrange("p a t -> p (a t)"), ACT.Copy, aup_ready)

                    act.wait_ge(p_ready, NPROD + 2 * UH)
                    act_upper(0, None, 0, T // TOK)

                    def v_unit(i, s, n_w):
                        for b in range(2):
                            upper_of((s + 1) % RING, b, 16 * i + 16 * (PAIR_V // RING + (2 if s == RING - 1 else 1)),
                                     8 * i + (VB0 + 2 * s + b))
                        if s == 0 and n_w is None:
                            act_upper(1, None, 2, T // TOK)
                        else:
                            act_upper(s + 1, 8 * i + (VB0 + 2 * s + 1), 2 * RING * i + 2 * (s + 1), n_w or T // TOK)

                    for s in range(RING):
                        v_unit(0, s, None)
                    with act.Fori(1, UH // RING - 1) as i:
                        for s in range(RING):
                            v_unit(i, s, T // TOK)
                    for s in range(RING):
                        v_unit(UH // RING - 1, s, 2 * T // TOK if s == RING - 1 else T // TOK)
                    with act.Fori(UH // RING, 2 * UH // RING - 1) as i:
                        for s in range(RING):
                            v_unit(i, s, 2 * T // TOK)
                    for s in range(RING - 1):
                        v_unit(2 * UH // RING - 1, s, 2 * T // TOK)

                @block.vector
                def _(v):
                    st = Steps(v, c_dve)

                    def mod_step(q):
                        m, kp = q // 4 + 2, q % 4
                        acc = ACC[m % 3]
                        v.wait_ge(mod_landed[q % 3], 16 * (q // 3 + 1) + 16 * 8 * layer)
                        if kp == 0 and m >= 5:
                            take(v, f"mod{m - 3}")
                        for kk in range(2):
                            k = 2 * kp + kk
                            w = MODR[q % 3][:, kk * D:(kk + 1) * D]
                            c = cact[:, KD + k:KD + k + 1]
                            if k == 0:
                                ins = v.tensor_scalar(acc, w, c, None, ALU.mult)
                            else:
                                st.done() if kk else v.wait_ge(mod_used, q)
                                ins = v.scalar_tensor_tensor(acc, w, c, acc, ALU.mult, ALU.add)
                            if kk == 0:
                                st(ins)
                            elif kp == 3:
                                ins.then_inc(mod_acc, 1)
                                v.wait_ge(mod_acc, q // 4 + 1)
                                v.engine_nop().then_inc(mod_used, 1)
                            else:
                                ins.then_inc(mod_used, 1)

                    def modcol(m):
                        b, free = take(v, f"mod{m}")
                        o = modc[:, m * KD:(m + 1) * KD]
                        v.tensor_tensor(o, b[:, 0:KD], col("b_mod", m * KD, KD), ALU.add).then_inc(free, 1)
                        if m in (1, 4):
                            freed(v, f"mod{m}")
                            st(v.tensor_scalar(o, o, 1.0, None, ALU.add))
                            st.done()

                    def sum_squares(n, hf):
                        v.wait_ge(E["xsq"], 2 * n + hf - 1)
                        v.tensor_reduce(XSUM[:, hf * T:(hf + 1) * T], XSQ[:, 4 * hf * T:4 * (hf + 1) * T].rearrange("p (k t) -> p t k", k=4),
                                        AX, ALU.add).then_inc(E["xsum"], 1)

                    def modulate(n, sh, sc, meanwhile=None):
                        if n == 1:
                            sum_squares(n, 0)
                        sum_squares(n, 1)
                        if meanwhile:
                            meanwhile()
                        freed(v, f"xss{n - 1}")
                        st(v.reciprocal(XRSTD, XRSTD))
                        st.done()
                        for hf in range(2):
                            ks = slice(4 * hf, 4 * hf + 4)
                            st(v.tensor_tensor(h3[:, ks], x3[:, ks], XRSTD[:, None, :].to_broadcast([P, 4, T]), ALU.mult))
                            st.done()
                            for k in range(4 * hf, 4 * hf + 4):
                                a, c = modc[:, sc * KD + k:sc * KD + k + 1], modc[:, sh * KD + k:sh * KD + k + 1]
                                ins = v.tensor_scalar(h3[:, k], h3[:, k], a, c, ALU.mult, ALU.add)
                                ins.then_inc(E["h"], 1) if k % 4 == 3 else st(ins)

                    def first_columns():
                        v.wait_ge(s_sml, 16)
                        st(v.tensor_tensor(modc[:, 0:2 * KD], modn[:, :], col("b_mod", 0, 2 * KD), ALU.add))
                        st.done()
                        st(v.tensor_scalar(modc[:, KD:2 * KD], modc[:, KD:2 * KD], 1.0, None, ALU.add))

                    modulate(1, 0, 1, first_columns)
                    v.memset(PRE[:, :, 0:3], 0.0).then_inc(E["zero"], 1)

                    def conv(i):
                        v.wait_ge(p_evac, 2 * i + 3)
                        v.wait_ge(E["zero"], 1)
                        last = [0] * 4
                        for j in range(4):
                            for c in range(4):
                                cc = 4 * i + c
                                src, w, o = PRE[:, cc, j:j + T], col("conv", cc * 4 + j), CONV[:, cc]
                                if j:
                                    st.done(last[c])
                                    ins = v.scalar_tensor_tensor(o, src, w, o, ALU.mult, ALU.add)
                                else:
                                    ins = v.tensor_scalar(o, src, w, None, ALU.mult)
                                if j == 3 and c == 3:
                                    ins.then_inc(E["conv"], 1)
                                else:
                                    last[c] = st(ins)

                    def invert(name, n):
                        freed(v, "ns" + name)
                        r = ROOT[:, n % 2].rearrange("p t h -> p (t h)")
                        st(v.reciprocal(r, r))
                        st.done()
                        v.tensor_copy(TB.rearrange("p (h d) -> p h d", d=CH), r[:, :, None].to_broadcast([P, NT * H, CH]))\
                         .then_inc(E["rinv"], 1)

                    def norm(name, dst, ev, gain=None):
                        for j in range(2):
                            b, free = take(v, f"np{name}{j}")
                            flat = dst[:, 2 * j:2 * j + 2].rearrange("p c t -> p (c t)")
                            if gain is None:
                                v.tensor_tensor(flat, flat, b[:, :], ALU.mult).then_inc(free, 1)
                            else:
                                v.scalar_tensor_tensor(flat, flat, gain, b[:, :], ALU.mult, ALU.mult).then_inc(free, 1)
                        for j in range(2):
                            freed(v, f"np{name}{j}")
                        v.engine_nop().then_inc(ev, 1)

                    conv(0)
                    b, free = take(v, "misc")
                    v.tensor_copy(MT, b[:, 0:NT * 48].rearrange("p (t n) -> p t n", t=NT)).then_inc(free, 1)
                    freed(v, "misc")
                    st(v.tensor_tensor(G2, MT[:, :, 32:40], col("dt_row", 0, H)[:, None, :].to_broadcast([P, NT, H]), ALU.add))
                    st.done()
                    v.scalar_tensor_tensor(G1, G2, -1.0, G2, ALU.mult, ALU.max).then_inc(E["spa"], 1)
                    conv(1)
                    v.wait_ge(E["spe"], 3)
                    st(v.tensor_scalar(BETA, BETA, 1.0, None, ALU.add))
                    st.done()
                    st(v.reciprocal(BETA, BETA))
                    v.wait_ge(E["spl"], 1)
                    st(v.scalar_tensor_tensor(G3, G2, 0.0, G1, ALU.max, ALU.add))
                    st.done()
                    v.scalar_tensor_tensor(GG, G3, -1.0, NEGA[:, None, :].to_broadcast([P, NT, H]),
                                           ALU.mult, ALU.mult).then_inc(E["g"], 1)
                    invert("k", 0)
                    conv(2)
                    norm("k", KT, E["gnorm"])
                    invert("q", 1)
                    norm("q", QT, E["gnorm"])
                    v.wait_ge(E["cstd"], 1)
                    freed(v, "css")
                    st(v.reciprocal(TA[:, 512:1024], TA[:, 0:512]))
                    st.done()
                    for c in range(2):
                        st(v.scalar_tensor_tensor(CQ[:, c], CQ[:, c], col("q_gain", c), TA[:, 512:768], ALU.mult, ALU.mult))
                    v.scalar_tensor_tensor(CKV, CKV, col("kv_gain"), TA[:, 768:1024], ALU.mult, ALU.mult).then_inc(E["cnorm"], 1)

                    b, free = take(v, "gcl")
                    v.tensor_copy(GCL, b[:, 0:NT * 16].rearrange("p (t n) -> p t n", t=NT)).then_inc(E["gcl"], 1)
                    v.wait_ge(E["gcl"], 1)
                    v.engine_nop().then_inc(free, 1)
                    v.tensor_tensor(EDEC, GCL[:, :, 8:16], GCL[:, :, 0:8], ALU.subtract).then_inc(E["gcl"], 1)
                    v.wait_ge(E["egc"], 2)
                    st(v.tensor_tensor(EB, BETA, EGC, ALU.mult))
                    v.wait_ge(E["masks"], 1)
                    for t in range(NT):
                        b, free = take(v, f"tokk{t}")
                        s3 = b[:, :].rearrange("p (h d) -> p h d", h=H)
                        st.done()
                        for dst, sc in ((KBG, EB), (KDEC, EDEC)):
                            v.tensor_tensor(dst[:, t].rearrange("p (h d) -> p h d", h=H), s3,
                                            sc[:, t, :, None].to_broadcast([P, H, CH]), ALU.mult).then_inc(E["tok"], 1)
                        v.wait_ge(E["tok"], 2 * t + 2)
                        v.engine_nop().then_inc(free, 1)
                    for t in range(NT):
                        b, free = take(v, f"tokv{t}")
                        v.tensor_tensor(VB[:, t].rearrange("p (h d) -> p h d", h=H), b[:, :].rearrange("p (h d) -> p h d", h=H),
                                        BETA[:, t, :, None].to_broadcast([P, H, CH]), ALU.mult).then_inc(E["tok"], 1)
                        v.wait_ge(E["tok"], 2 * NT + t + 1)
                        v.engine_nop().then_inc(free, 1)
                    st(v.memset(upper[:, 2048:2560], 0.0))

                    def rotate(dst, x1, x2, t, shape, tmp):
                        cb = COS[:, t, None, :].to_broadcast(shape)
                        sb_ = SIN[:, t, None, :].to_broadcast(shape)
                        n = shape[1] * 16
                        t1, t2, t3, t4 = (tmp[:, i * n:(i + 1) * n].rearrange("p (h f) -> p h f", h=shape[1]) for i in range(4))
                        st(v.tensor_tensor(t1, x1, cb, ALU.mult))
                        st(v.tensor_tensor(t2, x2, sb_, ALU.mult))
                        st(v.tensor_tensor(t3, x1, sb_, ALU.mult))
                        st(v.tensor_tensor(t4, x2, cb, ALU.mult))
                        st.done()
                        st(v.tensor_tensor(dst[:, :, 0:16], t1, t2, ALU.subtract))
                        return v.tensor_tensor(dst[:, :, 16:32], t3, t4, ALU.add)

                    def head_step(i):
                        if i < 2 * H:
                            b, free = take(v, f"S{i}")
                            if i >= 3:
                                take(v, f"PT{i - 3}")
                            else:
                                qk_transposed(v)
                            pb = PB[i % 3]
                            st(v.tensor_tensor(pb, b[:, 0:384], cmask, ALU.add))
                            st.done()
                            st(v.tensor_reduce(MX[:, i % 3, 0:1], pb[:, 0:P], AX, ALU.max))
                            v.tensor_reduce(MX[:, i % 3, 1:2], pb[:, P:3 * P], AX, ALU.max).then_inc(free, 1)
                            freed(v, f"S{i}")
                            sc = QK ** -0.5 if i < H else CH ** -0.5
                            v.tensor_scalar(NM[:, i % 3], MX[:, i % 3], -sc, None, ALU.mult).then_inc(E["pmask"], 1)
                        i1 = i - 1
                        if 0 <= i1 < 2 * H:
                            v.wait_ge(E["pexp"], 2 * i1 + 2)
                            st(v.reciprocal(RI[:, i1 % 3], RS[:, i1 % 3]))
                            st.done()
                            st(v.tensor_scalar(PB[i1 % 3][:, 0:P], PB[i1 % 3][:, 0:P], RI[:, i1 % 3, 0:1], None, ALU.mult))
                            v.tensor_scalar(PB[i1 % 3][:, P:3 * P], PB[i1 % 3][:, P:3 * P], RI[:, i1 % 3, 1:2], None,
                                            ALU.mult).then_inc(E["pnorm"], 1)

                    qf, kf = (a.rearrange("p t (h n) -> p t h n", h=H) for a in (QTOK, KFULL))
                    kv4 = KVTOK[:, :].rearrange("p t (h n) -> p t h n", h=H)
                    for kind, i in SCHEDULE:
                        if kind == "msum":
                            invert(f"m{i}", 2 + i)
                        elif kind == "mnorm":
                            norm(f"m{i}", (MQ, MK)[i], E["mnorm"], col(("mq_gain", "mk_gain")[i]))
                        elif kind == "mlasq":
                            for t in range(NT):
                                for j in range(2):
                                    for nm in (f"kv{t}{j}", f"q{t}{j}"):
                                        freed(v, nm)
                            sq = TA.rearrange("p (h n) -> p h n", h=H)
                            for t in range(NT):
                                st.done()
                                st(v.tensor_tensor(sq[:, :, 0:QK], qf[:, t], qf[:, t], ALU.mult))
                                st.done()
                                st(v.tensor_reduce(SSQ[:, t], sq[:, :, 0:QK], AX, ALU.add))
                                st.done()
                                st(v.tensor_tensor(sq[:, :, 0:NOPE], kv4[:, t, :, 0:NOPE], kv4[:, t, :, 0:NOPE], ALU.mult))
                                st.done()
                                st(v.tensor_reduce(SSK[:, t], sq[:, :, 0:NOPE], AX, ALU.add))
                                st(v.tensor_tensor(PESQ[:, t], MT[:, t, 0:ROPE], MT[:, t, 0:ROPE], ALU.mult))
                                st(v.tensor_tensor(KPG[:, t], MT[:, t, 0:ROPE], col("kn_row", NOPE, ROPE), ALU.mult))
                                st.done()
                                st(v.tensor_reduce(SSPE[:, t:t + 1], PESQ[:, t], AX, ALU.add))
                                st.done()
                                ins = v.tensor_scalar(SSK[:, t], SSK[:, t], SSPE[:, t:t + 1], None, ALU.add)
                                ins.then_inc(E["qkss"], 1) if t == NT - 1 else st(ins)
                        elif kind == "mlan":
                            st.done()
                            for t in range(NT):
                                kr = KROPE[:, t, None, :]
                                kp = KPG[:, t, None, :]
                                st(rotate(kr, kp[:, :, 0:16], kp[:, :, 16:32], t, [P, 1, 16], TA))
                                st.done()
                            v.wait_ge(E["qkstd"], 2)
                            for ss in (SSQ, SSK):
                                st(v.reciprocal(ss, ss))
                            st.done()
                            for t in range(NT):
                                st(v.tensor_tensor(qf[:, t], qf[:, t], SSQ[:, t, :, None].to_broadcast([P, H, QK]), ALU.mult))
                                st.done()
                                st(v.tensor_tensor(qf[:, t], qf[:, t], col("qn_row", 0, QK)[:, None, :].to_broadcast([P, H, QK]), ALU.mult))
                                st.done()
                                ins = rotate(qf[:, t, :, NOPE:QK], qf[:, t, :, NOPE:NOPE + 16], qf[:, t, :, NOPE + 16:QK], t, [P, H, 16], TA)
                                if t == NT - 1:
                                    ins.then_inc(E["qkfull"], 1)
                                else:
                                    st(ins)
                                    st.done()
                            for t in range(NT):
                                st(v.tensor_tensor(kf[:, t, :, 0:NOPE], kv4[:, t, :, 0:NOPE],
                                                   SSK[:, t, :, None].to_broadcast([P, H, NOPE]), ALU.mult))
                                st.done()
                                st(v.tensor_tensor(kf[:, t, :, 0:NOPE], kf[:, t, :, 0:NOPE],
                                                   col("kn_row", 0, NOPE)[:, None, :].to_broadcast([P, H, NOPE]), ALU.mult))
                                ins = v.tensor_tensor(kf[:, t, :, NOPE:QK], KROPE[:, t, None, :].to_broadcast([P, H, ROPE]),
                                                      SSK[:, t, :, None].to_broadcast([P, H, ROPE]), ALU.mult)
                                if t == NT - 1:
                                    ins.then_inc(E["qkfull"], 1)
                                else:
                                    st(ins)
                        elif kind == "head":
                            head_step(i)
                            if i == H + 5:
                                v.wait_ge(E["bhup"], 1)
                                v.tensor_tensor(HT_r[:, :], HT[:, :], BH[0].bitcast(F32).rearrange("p k t -> p (k t)"),
                                                ALU.subtract).then_inc(E["bhsplit"], 1)
                                v.wait_ge(E["oup"], 1)
                                v.tensor_tensor(OSPLIT[0][1], OSPLIT[0][2], OSPLIT[0][0].bitcast(F32), ALU.subtract)\
                                 .then_inc(E["osplit"], 1)
                        elif kind == "decay":
                            if i:
                                v.wait_ge(E["uw"], 1)
                            for par in range(2):
                                b, free = take(v, f"gcb{i}{par}")
                                v.wait_ge(E["egb"], 2 * i + par + 1)
                                for c in range(HC):
                                    gc = GCL[:, i, 2 * c + par:2 * c + par + 1]
                                    src = b[:, c * P:(c + 1) * P]
                                    v.tensor_scalar(AM[:, par, c], src, gc, 0.0, ALU.subtract, ALU.max).then_inc(E["diff"], 1)
                                    v.tensor_scalar(ATT[i][:, par, c], src, gc, 0.0, ALU.subtract, ALU.min).then_inc(E["diff"], 1)
                                v.wait_ge(E["diff"], 16 * i + 8 * par + 8)
                                v.engine_nop().then_inc(free, 1)
                            v.wait_ge(E["decay"], 2 * i + 2)
                            for m, mask in ((AM, strict), (ATT[i], incl)):
                                mm = m[:, :].rearrange("p g c j -> p (g c) j")
                                st(v.tensor_tensor(mm, mm, mask[:, None, :].to_broadcast([P, H, P]), ALU.mult))
                            ts = slice(i * P, (i + 1) * P)
                            v.wait_ge(E["gnorm"], 2)
                            for par in range(2):
                                r = slice(par * CH, par * CH + CH)
                                for q2 in range(2):
                                    cs = slice(2 * q2, 2 * q2 + 2)
                                    v.tensor_tensor(QG[r, cs, ts], QT[r, cs, ts], EGB[r, par, cs, ts], ALU.mult).then_inc(E["qg"], 1)
                        elif kind == "build":
                            for par in range(2):
                                b, free = take(v, f"GK{i}{par}")
                                st.done()
                                for c in range(HC):
                                    st(v.scalar_tensor_tensor(AM[:, par, c], b[:, c * P:(c + 1) * P],
                                                              BETA[:, i, 2 * c + par:2 * c + par + 1], AM[:, par, c],
                                                              ALU.mult, ALU.mult))
                                st.done()
                                v.engine_nop().then_inc(free, 1)
                            for par in range(2):
                                b, free = take(v, f"GQ{i}{par}")
                                a = ATT[i][:, par].rearrange("p c j -> p (c j)")
                                v.tensor_tensor(a, b[:, :], a, ALU.mult).then_inc(free, 1)
                            flat = lambda m: m[:, :].rearrange("p g c j -> p (g c) j")
                            idb = ident[:, None, :].to_broadcast([P, H, P])
                            v.tensor_tensor(flat(CM), flat(AM), lmask[:, None, 0:P].to_broadcast([P, H, P]), ALU.mult)\
                             .then_inc(E["cm"], 1)
                            v.wait_ge(E["cm"], len(LEVELS) * i + 1)
                            v.scalar_tensor_tensor(flat(TM), flat(CM), -1.0, idb, ALU.mult, ALU.add).then_inc(E["t"], 1)
                            for par in range(2):
                                b, free = take(v, f"Y{i}{1}{par}")
                                ins = v.scalar_tensor_tensor(UM[:, par], b[:, :].rearrange("p (c j) -> p c j", c=HC), -1.0,
                                                             ident[:, None, :].to_broadcast([P, HC, P]), ALU.mult, ALU.add)
                                if par == 0:
                                    ins.then_inc(free, 1)
                                else:
                                    ins.then_inc(E["u"], 1)
                                    v.wait_ge(E["u"], len(LEVELS) * i + 1)
                                    v.engine_nop().then_inc(free, 1)
                            v.tensor_tensor(flat(CM), flat(AM), lmask[:, None, P:2 * P].to_broadcast([P, H, P]), ALU.mult)\
                             .then_inc(E["cm"], 1)
                        elif kind == "level":
                            t, s = i
                            li = LEVELS.index(s)
                            flat = lambda m: m[:, :].rearrange("p g c j -> p (g c) j")
                            v.wait_ge(E["y"], (len(LEVELS) - 1) * t + li)
                            v.engine_nop().then_inc(side_free[jobs[f"Y{t}{s}1"][0]], 1)
                            if s != LEVELS[-1]:
                                v.tensor_tensor(flat(CM), flat(AM), lmask[:, None, (li + 1) * P:(li + 2) * P]
                                                .to_broadcast([P, H, P]), ALU.mult).then_inc(E["cm"], 1)
                            for par in range(2):
                                b, free = take(v, f"U{t}{s}{par}")
                                ins = v.tensor_tensor(UM[:, par], UM[:, par], b[:, :].rearrange("p (c j) -> p c j", c=HC), ALU.subtract)
                                if par == 0:
                                    ins.then_inc(free, 1)
                                else:
                                    ins.then_inc(E["u"], 1)
                                    v.wait_ge(E["u"], len(LEVELS) * t + li + 1)
                                    v.engine_nop().then_inc(free, 1)
                            if s != LEVELS[-1]:
                                for par in range(2):
                                    b, free = take(v, f"TT{t}{s}{par}")
                                    if par == 0:
                                        take(v, f"TT{t}{s}1")
                                    ins = v.tensor_tensor(TM[:, par], TM[:, par], b[:, :].rearrange("p (c j) -> p c j", c=HC),
                                                          ALU.subtract)
                                    if par == 0:
                                        ins.then_inc(free, 1)
                                    else:
                                        ins.then_inc(E["t"], 1)
                                        v.wait_ge(E["t"], (len(LEVELS) - 1) * t + li + 1)
                                        v.engine_nop().then_inc(free, 1)
                        elif kind == "uw":
                            for par in range(2):
                                b, free = take(v, f"uu{i}{par}")
                                v.tensor_copy(UV[:, i].rearrange("p (c g d) -> p c g d", c=HC, g=2)[:, :, par],
                                              b[:, :].rearrange("p (c g d) -> p c g d", c=HC, g=2)[:, :, par]).then_inc(free, 1)
                            b, free = take(v, f"wt{i}")
                            v.tensor_copy(WT[:, i], b[:, :].rearrange("p (c j) -> p c j", c=HC)).then_inc(E["wt"], 1)
                            v.wait_ge(E["wt"], i + 1)
                            v.engine_nop().then_inc(free, 1)
                            v.engine_nop().then_inc(E["uw"], 1)
                            if i == NT - 1:
                                for par in range(2):
                                    r = slice(par * CH, par * CH + CH)
                                    st(v.tensor_copy(EGL[r], EGB[r, par, :, CH - 1:T:CH]))
                                v.engine_nop().then_inc(E["state"], 1)
                                st.done()
                        elif kind == "chunk":
                            n, t, r = i, i // 2, slice((i % 2) * CH, (i % 2) * CH + CH)
                            b, free = take(v, f"ws{n}")
                            v.tensor_tensor(UV[r, t], UV[r, t], b[r, :], ALU.subtract).then_inc(E["vnew"], 1)
                            v.wait_ge(E["vnew"], n + 1)
                            v.engine_nop().then_inc(free, 1)
                            if n < T // CH - 1:
                                b, free = take(v, f"ds{n}")
                                st(v.tensor_tensor(ST, ST, EGL[:, :, n:n + 1].to_broadcast([P, HC, P]), ALU.mult))
                                ds = YM[:, 0]
                                v.tensor_tensor(ds, b[:, :].rearrange("p (c j) -> p c j", c=HC),
                                                same[:, None, :].to_broadcast([P, HC, P]), ALU.mult).then_inc(free, 1)
                                freed(v, f"ds{n}")
                                v.tensor_tensor(ST, ST, ds, ALU.add).then_inc(E["state"], 1)
                    def o_lower(b):
                        v.wait_ge(E["oup"], b + 1)
                        v.tensor_tensor(OSPLIT[b][1], OSPLIT[b][2], OSPLIT[b][0].bitcast(F32), ALU.subtract).then_inc(E["osplit"], 1)

                    invert("o", 4)
                    norm("o", VT, E["onorm"], col("o_gain"))
                    v.wait_ge(p_evac, prod[PAIR_Z + 1] + 1)
                    og = VT.rearrange("p c t -> p (c t)")
                    v.tensor_tensor(og, og, ZS[:, :].rearrange("p c t -> p (c t)"), ALU.mult).then_inc(E["ognorm"], 1)
                    o_lower(1)

                    def merged_lower(m):
                        v.wait_ge(E["mup"], m + 1)
                        cols = slice(512 * m, 512 * (m + 1))
                        v.tensor_tensor(MLOW[:, cols], MERGED[:, 2 * m:2 * m + 2].rearrange("p k t -> p (k t)"), MUP[:, cols].bitcast(F32),
                                        ALU.subtract).then_inc(E["msplit"], 1)

                    last = [0] * 4
                    for b in range(3):
                        for j in range(2):
                            for i in range(2):
                                n = 4 * b + 2 * j + i
                                o, free = take(v, f"br{b}{j}{i}")
                                v.wait_ge(p_evac, prod[PAIR_BR + 6 * b + 3 * j + i] + 1)
                                gt = GATE[n % 4]
                                m = MERGED[:, 4 * j + 2 * i:4 * j + 2 * i + 2].rearrange("p k t -> p (k t)")
                                if b == 0:
                                    last[2 * j + i] = st(v.tensor_tensor(m, gt, o[:, :], ALU.mult))
                                    st.done()
                                    v.engine_nop().then_inc(free, 1)
                                    v.engine_nop().then_inc(E["gate"], 1)
                                else:
                                    v.tensor_tensor(gt, gt, o[:, :], ALU.mult).then_inc(free, 1)
                                    freed(v, f"br{b}{j}{i}")
                                    v.tensor_tensor(m, m, gt, ALU.add).then_inc(E["gate"], 1)
                                    if b == 1:
                                        v.wait_ge(E["gate"], n + 1)
                                    else:
                                        v.wait_ge(E["gate"], n + 1)
                                if n == 3:
                                    o_lower(2)
                                if n == 7:
                                    modcol(2)
                                if n == 9:
                                    merged_lower(0)
                                    merged_lower(1)
                                    modcol(3)
                                if n == 11:
                                    merged_lower(2)
                                    merged_lower(3)
                                    mod_step(10)
                                if n != 10:
                                    mod_step(n)
                    for p in range(4):
                        b, free = take(v, f"y{p}")
                        for i in range(2):
                            k = 2 * p + i
                            v.scalar_tensor_tensor(x3[:, k], b[:, i * T:(i + 1) * T], modc[:, 2 * KD + k:2 * KD + k + 1], x3[:, k],
                                                   ALU.mult, ALU.add).then_inc(E["x"], 1)
                        v.wait_ge(E["x"], 2 * p + 2)
                        v.engine_nop().then_inc(free, 1)
                        if p == 2:
                            sum_squares(2, 0)
                    modulate(2, 3, 4, lambda: modcol(4))
                    for hf in range(2):
                        cols = slice(4 * T * hf, 4 * T * (hf + 1))
                        v.wait_ge(E["hup"], hf + 1)
                        v.tensor_tensor(HT_r[:, cols], HT[:, cols], X_r[:, cols].bitcast(F32), ALU.subtract).then_inc(E["hsplit"], 1)

                    def top16(srcs, vals, idxs, works):
                        n = len(srcs)
                        for k in range(n):
                            st(v.max(vals[k][:, 0:8], srcs[k]))
                        st.done()
                        for k in range(n):
                            st(v.max_index(idxs[k][:, 0:8], vals[k][:, 0:8], srcs[k]))
                            st(v.match_replace(works[k], vals[k][:, 0:8], srcs[k], -3.0e38))
                        st.done()
                        for k in range(n):
                            st(v.max(vals[k][:, 8:16], works[k]))
                        st.done()
                        for k in range(n):
                            st(v.max_index(idxs[k][:, 8:16], vals[k][:, 8:16], works[k]))

                    for h in range(H):
                        b, free = take(v, f"sc{h}")
                        tj = [(t, j) for t in range(NT) for j in range(2)]
                        top16([b[:, (2 * t + j) * P:(2 * t + j + 1) * P] for t, j in tj], [TV[:, t, j, h] for t, j in tj],
                              [TI[:, t, j, h] for t, j in tj], WORK)
                        st.done()
                        v.engine_nop().then_inc(free, 1)
                        for t in range(NT):
                            st(v.tensor_tensor(CAND[:, t].rearrange("p (a b) -> p a b", a=TOPK),
                                               TV[:, t, 0, h, :, None].to_broadcast([P, TOPK, TOPK]),
                                               TV[:, t, 1, h, None, :].to_broadcast([P, TOPK, TOPK]), ALU.add))
                        st.done()
                        top16([CAND[:, t] for t in range(NT)], [TS[:, t, h] for t in range(NT)],
                              [TP[:, t, h * TOPK:(h + 1) * TOPK] for t in range(NT)], [CWORK[:, t] for t in range(NT)])
                        st.done()
                    TS3 = TS[:, :, :, :].rearrange("p t h k -> p (t h) k")
                    st(v.tensor_copy(SM1.rearrange("p t h -> p (t h)"), TS3[:, :, 0]))
                    st.done()
                    smb = SM1.rearrange("p t h -> p (t h)")[:, :, None].to_broadcast([P, NT * H, TOPK])
                    v.tensor_tensor(TS3, TS3, smb, ALU.subtract).then_inc(E["topd"], 1)
                    st(v.tensor_copy(TIF[:, :, :, :, :].rearrange("p t j h k -> p (t j h k)"),
                                     TI[:, :, :, :, :].rearrange("p t j h k -> p (t j h k)")))
                    for t in range(NT):
                        st.done()
                        st(v.tensor_scalar(TABU[:, 0, 0:P], TP[:, t], 4, None, ALU.logical_shift_right))
                        st(v.tensor_scalar(TABU[:, 1, 0:P], TP[:, t], 15, None, ALU.bitwise_and))
                        st.done()
                        st(v.tensor_copy(TAB[:, :, 0:P], TABU[:, :, 0:P]))
                        st.done()
                        for j in range(2):
                            ab = TAB[:, j, 0:P].rearrange("p (h k) -> p h k", h=H)[:, :, :, None].to_broadcast([P, H, TOPK, TOPK])
                            st(v.tensor_tensor(EQ, iota[:, None, None, 0:TOPK].to_broadcast([P, H, TOPK, TOPK]), ab, ALU.is_equal))
                            st.done()
                            st(v.tensor_tensor(EQ, EQ, TIF[:, t, j, :, None, :].to_broadcast([P, H, TOPK, TOPK]), ALU.mult))
                            st.done()
                            st(v.tensor_reduce(IDX[:, t, j].rearrange("p (h k) -> p h k", h=H), EQ, AX, ALU.add))
                            st.done()
                    v.wait_ge(E["tope"], 1)
                    st(v.tensor_reduce(SM1.rearrange("p t h -> p (t h)"), TS3, AX, ALU.add))
                    st.done()
                    st(v.reciprocal(SM2.rearrange("p t h -> p (t h)"), SM1.rearrange("p t h -> p (t h)")))
                    st.done()
                    v.tensor_tensor(TS3, TS3, SM2.rearrange("p t h -> p (t h)")[:, :, None].to_broadcast([P, NT * H, TOPK]),
                                    ALU.mult).then_inc(E["idx"], 1)
                    def lower(slot, b, n):
                        v.wait_ge(up_ready, n)
                        cols = slice(BLK * b, BLK * (b + 1))
                        at = BLK * (2 * (slot % 2) + b)
                        v.tensor_tensor(ring_r[slot][:, cols], ring[slot][:, cols], upper_r[:, at:at + BLK].bitcast(F32), ALU.subtract).then_inc(low_dve, 1)

                    for b in range(2):
                        lower(0, b, NPOOL + b + 1)
                    for t in range(NT):
                        b, free = take(v, f"ix{t}")
                        ts = slice(t * P, (t + 1) * P)
                        st(v.tensor_copy(IDXT[:, :, ts], b[:, 0:2 * P].rearrange("p (j t) -> p j t", j=2)))
                        g = b[:, 2 * P:3 * P]
                        st(v.tensor_copy(GATES[:, ts, 0], g))
                        st.done()
                        st(v.tensor_tensor(GREST[:, ts], g, GATES[:, ts, 0], ALU.subtract))
                        st.done()
                        v.engine_nop().then_inc(free, 1)
                        st(v.tensor_copy(GATES[:, ts, 1], GREST[:, ts]))
                        st.done()
                        st(v.tensor_tensor(GREST[:, ts], GREST[:, ts], GATES[:, ts, 1], ALU.subtract))
                        st.done()
                        v.tensor_copy(GATES[:, ts, 2], GREST[:, ts]).then_inc(E["idxT"], 1)
                    v.wait_ge(E["idxT"], NT)

                    def onehot_b(c, t0, slot, n_used):
                        if n_used is not None:
                            v.wait_ge(E["wready"], n_used)
                        for k in range(GRP):
                            ins = v.scalar_tensor_tensor(OHB[slot][:, k], iota[:, None, c * EH:(c + 1) * EH].to_broadcast([P, 3, EH]),
                                                         IDXT[:, 1, bass.ds(t0 + k, 1)],
                                                         GATES[:, bass.ds(t0 + k, 1), :].rearrange("p a j -> p (a j)")[:, :, None]
                                                         .to_broadcast([P, 3, EH]), ALU.is_equal, ALU.mult)
                        ins.then_inc(E["ohb"], 1)

                    def apply(c, t0, slot, n):
                        v.wait_ge(E["wready"], n)
                        a = act3[:, c * EH:(c + 1) * EH, bass.ds(t0, TOK)]
                        v.tensor_tensor(a, a, SB[4 + slot][:, :].rearrange("p (t e) -> p e t", t=TOK), ALU.mult)\
                         .then_inc(E["wdone"], 1)

                    def u_unit(i, s, first=False):
                        if not first:
                            for b in range(2):
                                lower(s, b, 8 * i + (NPOOL + 2 * s + b + 1))
                        for g in range(2):
                            onehot_b(0, RING * TOK * i + TOK * s + GRP * g, g, None if first else 8 * i + (2 * s + g - 1))
                        if first:
                            v.wait_ge(p_evac, NPROD + UH)
                            return
                        apply(0, RING * TOK * i + TOK * (s - 1), (s - 1) % 2, 8 * i + 2 * s)

                    for s in range(RING):
                        u_unit(0, s, first=s == 0)
                    with v.Fori(1, UH // RING) as i:
                        for s in range(RING):
                            u_unit(i, s)
                    apply(0, T - TOK, 1, T // GRP)

                    def act_lower(slot, e, n):
                        v.wait_ge(aup_ready, n)
                        v.tensor_tensor(ALOW[slot % 2], act3[:, bass.ds(e, 2)].rearrange("p a t -> p (a t)"),
                                        AUP[slot % 2].bitcast(F32), ALU.subtract).then_inc(alow_ready, 1)

                    def v_unit(i, s, w=True, first=False):
                        for b in range(2):
                            lower(s, b, 8 * i + (VB0 + 2 * s + b + 1))
                            if b == 0:
                                act_lower(s, 2 * RING * i + 2 * s, RING * i + (s + 1))
                        if not w:
                            return
                        for g in range(2):
                            onehot_b(1, RING * TOK * i + TOK * s + GRP * g, g, 8 * i + (T // GRP + 2 * s + g - 1))
                        if first:
                            v.wait_ge(p_evac, NPROD + 2 * UH)
                        else:
                            apply(1, RING * TOK * i + TOK * (s - 1), (s - 1) % 2, 8 * i + (T // GRP + 2 * s))

                    for s in range(RING):
                        v_unit(0, s, first=s == 0)
                    with v.Fori(1, UH // RING) as i:
                        for s in range(RING):
                            v_unit(i, s)
                    apply(1, T - TOK, 1, 2 * T // GRP)
                    for i in range(UH // RING, UH // RING + 6):
                        for s in range(RING):
                            v_unit(i, s, w=False)
                            if s % 2:
                                mod_step(12 + 2 * (i - UH // RING) + s // 2)
                    with v.Fori(UH // RING + 6, 2 * UH // RING) as i:
                        for s in range(RING):
                            v_unit(i, s, w=False)
                    v.wait_ge(mod_done, 1)
                    st(v.tensor_tensor(modc[:, 5 * KD:6 * KD], SB[4][:, 0:KD], col("b_mod", 5 * KD, KD), ALU.add))
                    st(v.tensor_copy(modn[:, :], SB[4][:, KD:3 * KD]))
                    st.done()
                    v.wait_ge(E["vdone"], 1)
                    v.wait_ge(reloaded, 16)
                    for k in range(KD):
                        v.scalar_tensor_tensor(x3[:, k], SB[k // 2][:, (k % 2) * T:(k % 2 + 1) * T], modc[:, 5 * KD + k:5 * KD + k + 1],
                                               x3[:, k], ALU.mult, ALU.add).then_inc(E["x"], 1)
                    v.wait_ge(E["x"], 2 * KD)

                @block.gpsimd
                def _(g):
                    st = Steps(g, c_pool)
                    def mod_fetch(q):
                        if q >= 3:
                            g.wait_ge(mod_used, q - 2)
                        g.dma_start(MODR[q % 3], modw[bass.ds(layer * 24 + (8 + q), 1)].rearrange("a p n -> p (a n)"))\
                         .then_inc(mod_landed[q % 3], 16)

                    for m in (same, cmask, lmask):
                        st(g.memset(m, 0.0))
                    st.done()
                    st(g.memset(same[0:CH, 0:CH], 1.0))
                    st.done()
                    st(g.memset(same[CH:P, CH:P], 1.0))
                    st.done()
                    for i, s in enumerate(LEVELS):
                        m = lmask[:, i * P:(i + 1) * P].rearrange("p (b j) -> p b j", j=2 * s)
                        st(g.memset(m[:, :, 0:s], 1.0))
                    for a in (0, 2 * P):
                        st(g.affine_select(out=cmask[:, a:a + P], in_=cmask[:, a:a + P], compare_op=ALU.is_ge, fill=NEG,
                                           base=0, pattern=[[-1, P]], channel_multiplier=1))
                    st.done()
                    st(g.affine_select(out=strict, in_=same, compare_op=ALU.is_gt, fill=0.0, base=0,
                                       pattern=[[-1, P]], channel_multiplier=1))
                    st(g.affine_select(out=incl, in_=same, compare_op=ALU.is_ge, fill=0.0, base=0,
                                       pattern=[[1, P]], channel_multiplier=-1))
                    for i, s in enumerate(LEVELS):
                        m = lmask[:, i * P:(i + 1) * P].rearrange("p (b j) -> p b j", j=2 * s)
                        st(g.affine_select(out=m, in_=m, compare_op=ALU.is_ge, fill=0.0, base=-s,
                                           pattern=[[-2 * s, P // (2 * s)], [0, 2 * s]], channel_multiplier=1))
                    st.done()
                    for i, s in enumerate(LEVELS):
                        m = lmask[:, i * P:(i + 1) * P].rearrange("p (b j) -> p b j", j=2 * s)
                        st(g.affine_select(out=m, in_=m, compare_op=ALU.is_ge, fill=0.0, base=2 * s - 1,
                                           pattern=[[2 * s, P // (2 * s)], [0, 2 * s]], channel_multiplier=-1))
                    st.done()
                    g.memset(tiny_f[:, 48:64], 0.0).then_inc(E["masks"], 1)

                    def lower(slot, b, n):
                        g.wait_ge(up_ready, n)
                        cols = slice(BLK * b, BLK * (b + 1))
                        g.tensor_tensor(ring_r[slot][:, cols], ring[slot][:, cols], upper_r[:, BLK * (2 * (slot % 2) + b):BLK * (2 * (slot % 2) + b + 1)].bitcast(F32),
                                        ALU.subtract).then_inc(low_pool, 1)

                    fetch_at = {PAIR_BR + 4: (0, 1, 2)}
                    for q in range(3, 12):
                        fetch_at[PAIR_BR + 5 + (q - 3) // 2 * 3 + (q - 3) % 2] = (q,)
                    for p in range(PAIR_BR, PAIR_QRY):
                        if p == PAIR_BR + 4:
                            g.wait_ge(E["ognorm"], 1)
                        for q in fetch_at.get(p, ()):
                            mod_fetch(q)
                        for b in range(2):
                            lower(p % RING, b, 2 * (p - PAIR_BR) + b + 1)
                    with g.Fori(0, (NPOOL - QB0) // 8) as i:
                        for s in range(RING):
                            for b in range(2):
                                lower(s, b, 8 * i + (QB0 + 2 * s + b + 1))

                    g.wait_ge(E["idxT"], NT)

                    def onehot_a(t0, slot, n_ready, n_used):
                        if n_used is not None:
                            g.wait_ge(E["wready"], n_used)
                        g.tensor_copy(I1C[slot], IDXT[:, 0, bass.ds(t0, GRP)]).then_inc(i1_ready, 1)
                        g.wait_ge(i1_ready, n_ready)
                        g.tensor_tensor(I1D[slot], I1C[slot], ones[:, 0:GRP], ALU.mult).then_inc(c_pool, 1)
                        for k in range(GRP):
                            ins = g.tensor_scalar(OHA[slot][:, k], iota[:, :], I1C[slot][:, k:k + 1], None, ALU.is_equal)
                        ins.then_inc(E["oha"], 1)

                    for s in range(2):
                        onehot_a(GRP * s, s, s + 1, None)
                    with g.Fori(1, T // TOK) as i:
                        for s in range(2):
                            onehot_a(TOK * i + GRP * s, s, 2 * i + (s + 1), 2 * i + (s - 1))
                    with g.Fori(0, T // TOK) as i:
                        for s in range(2):
                            onehot_a(TOK * i + GRP * s, s, 2 * i + (s + 1 + T // GRP), 2 * i + (s - 1 + T // GRP))
                    g.wait_ge(alow_ready, UH)
                    for q in range(12, 24):
                        mod_fetch(q)

                @block.sync
                def _(sp_):
                    sp_.dma_start(sml[:, :], small[bass.ds(layer, 1)].rearrange("a p n -> p (a n)")).then_inc(s_sml, 16)

                    def fetch(q, slot):
                        sp_.dma_start(ring[slot][:, :], stream[bass.ds(layer * PAIRS + q, 1)].rearrange("a p n -> p (a n)"))\
                           .then_inc(landed[slot], 16)

                    for s in range(RING):
                        fetch(s, s)
                    def refill(i, slots=range(RING)):
                        for s in slots:
                            sp_.wait_ge(begun, RING * i + (s - 2))
                            fetch(RING * i + s, s)

                    def loop(lo, hi):
                        with sp_.Fori(lo, hi) as i:
                            refill(i)

                    loop(1, PAIR_OUT // RING)
                    sp_.wait_ge(E["ognorm"], 1)
                    sp_.dma_start(A(0, 2048), subk[bass.ds(layer, 1)].rearrange("a p n -> p (a n)")).then_inc(E["sk"], 16)
                    loop(PAIR_OUT // RING, PAIR_QRY // RING)
                    refill(PAIR_QRY // RING, range(3))
                    sp_.wait_ge(E["x"], KD)
                    sp_.dma_start(spill, X[:, :]).then_inc(spilled, 16)
                    refill(PAIR_QRY // RING, range(3, 4))
                    loop(PAIR_QRY // RING + 1, PAIR_V // RING + 1)
                    sp_.wait_ge(begun, PAIR_V + 1)
                    sp_.wait_ge(spilled, 16)
                    sp_.dma_start(X[:, :], spill).then_inc(reloaded, 16)
                    loop(PAIR_V // RING + 1, PAIRS // RING)

            nc.multi_engine_barrier(list(mybir.ALL_ENGINES), sems_to_clear=range(s_load.num, sems[-1].num + 1))
        with nc.Block() as block:
            @block.sync
            def _(sp_):
                sp_.dma_start(out, X[:, :]).then_inc(s_load, 16)
                sp_.wait_ge(s_load, 16)


def _blocks(w, k):
    n = w.shape[1] // P
    return w.reshape(k, P, n, P).transpose(2, 1, 0, 3)


def _layer_stream(l, w_in, w_uq, w_ukv, w_branch, w_out, w_query, peer_u, peer_v):
    sizes = (QR, KVR, ROPE, 512, 512, 512, 512, H, H, 512, 512, 512, 3 * D)
    cuts = np.cumsum(sizes)[:-1]
    cq, ckv, kr, gq, gk, gv, gz, ga, gb, mq, mk, mv, gates = np.split(w_in[l], cuts, axis=1)
    pad = np.zeros((D, P - ROPE - 2 * H), np.float32)
    misc = np.concatenate([kr, ga, gb, pad], axis=1)
    g = [gates[:, b * D:(b + 1) * D] for b in range(3)]
    order = (0, 2, 1)
    head = np.concatenate([ckv, misc, gk, gq, gv, cq], axis=1)
    out = np.zeros((PAIRS, 2, P, 8, P), np.float32)
    flat = out.reshape(PAIRS * 2, P, 8, P)

    def put(pair, blocks):
        flat[2 * pair:2 * pair + len(blocks)] = blocks

    put(0, _blocks(head, 8))
    flat[2 * PAIR_UKV] = w_ukv[l].reshape(P, 8, P)
    for c in range(2):
        flat[2 * PAIR_UQ + c, :, 0:6] = w_uq[l, c * P:(c + 1) * P].reshape(P, 6, P)
    put(PAIR_MQ, _blocks(np.concatenate([mq, mk], axis=1), 8))
    put(PAIR_MV, _blocks(np.concatenate([mv, gz], axis=1), 8))
    for n, b in enumerate(order):
        gb_ = _blocks(g[b], 8)
        br = w_branch[l, b].reshape(HC, P, 4, 2, P).transpose(2, 1, 3, 0, 4).reshape(4, P, 8, P)
        for j in range(2):
            put(PAIR_BR + 6 * n + 3 * j, gb_[4 * j:4 * j + 4])
            put(PAIR_BR + 6 * n + 3 * j + 2, br[2 * j:2 * j + 2])
    put(PAIR_OUT, _blocks(w_out[l], 8))
    put(PAIR_QRY, _blocks(w_query[l], 8))
    put(PAIR_U, peer_u[l].reshape(NK, NK, 8, P).transpose(1, 3, 2, 0))
    put(PAIR_V, peer_v[l].reshape(NK, NK, 8, P).transpose(1, 0, 2, 3))
    return out.transpose(0, 2, 1, 3, 4).reshape(PAIRS, P, 2 * BLK)


def kernel(x, c, positions, w_mod, b_mod, w_in, mla_q_gain, mla_w_uq, mla_kv_gain, mla_w_ukv, mla_qn_gain,
           mla_kn_gain, gdn_conv_w, gdn_a_log, gdn_dt_bias, gdn_o_gain, moba_qn_gain, moba_kn_gain, w_branch,
           w_out, peer_w_query, peer_sub_keys, peer_u, peer_v):
    import concourse.bacc as bacc
    from concourse.bass_utils import run_bass_kernel_spmd

    def row(a):
        return np.broadcast_to(a[None, :], (P, a.shape[0]))

    (x, c, positions, w_mod, b_mod, w_in, mla_w_uq, mla_w_ukv, gdn_conv_w, w_branch, w_out, peer_w_query, peer_sub_keys,
     peer_u, peer_v) = (np.asarray(a) for a in (x, c, positions, w_mod, b_mod, w_in, mla_w_uq, mla_w_ukv, gdn_conv_w,
                                                w_branch, w_out, peer_w_query, peer_sub_keys, peer_u, peer_v))
    small = np.zeros((DEPTH, P, NSMALL), np.float32)
    for l in range(DEPTH):
        def put(name, a):
            lo, hi = SMALL[name]
            small[l, :, lo:hi] = a
        cw = np.concatenate([gdn_conv_w[l][:, 512:1024], gdn_conv_w[l][:, 0:512], gdn_conv_w[l][:, 1024:]], axis=1)
        put("conv", cw.reshape(4, 12, P).transpose(2, 1, 0).reshape(P, 48))
        put("q_gain", np.asarray(mla_q_gain[l]).reshape(2, P).T)
        put("kv_gain", np.asarray(mla_kv_gain[l]).reshape(1, P).T)
        put("mq_gain", np.tile(moba_qn_gain[l], 2)[:, None])
        put("mk_gain", np.tile(moba_kn_gain[l], 2)[:, None])
        put("o_gain", np.tile(gdn_o_gain[l], 2)[:, None])
        put("b_mod", b_mod[l].reshape(48, P).T)
        put("qn_row", row(np.asarray(mla_qn_gain[l])))
        put("kn_row", row(np.asarray(mla_kn_gain[l])))
        put("dt_row", row(np.asarray(gdn_dt_bias[l])))
        put("alog_row", row(np.asarray(gdn_a_log[l])))
    stream = np.concatenate([_layer_stream(l, w_in, mla_w_uq, mla_w_ukv, w_branch, w_out, peer_w_query, peer_u, peer_v)
                             for l in range(DEPTH)])
    modw = np.zeros((DEPTH * 24 + 8, P, 2 * D), np.float32)
    modw[:DEPTH * 24] = w_mod.reshape(DEPTH, 4, 2, P, 6, D).transpose(0, 4, 1, 3, 2, 5).reshape(DEPTH * 24, P, 2 * D)
    subk = peer_sub_keys.transpose(0, 4, 1, 2, 3).reshape(DEPTH, P, 2048)
    invf = (10000.0 ** (-np.arange(16, dtype=np.float32) / np.float32(16))).astype(np.float32)
    arrays = {
        "xT": x[0].reshape(T, KD, P).transpose(2, 1, 0).reshape(P, KD * T),
        "cT": c[0].reshape(KD, P).T,
        "pos": positions[0].reshape(NT, P).T,
        "invf": row(invf),
        "stream": stream, "modw": modw, "small": small, "subk": subk,
    }
    arrays = {k: np.ascontiguousarray(a) for k, a in arrays.items()}
    nc = bacc.Bacc("TRN2", target_bir_lowering=False, num_devices=1)
    aps = {k: nc.dram_tensor(k, a.shape, mybir.dt.from_np(a.dtype), kind="ExternalInput").ap() for k, a in arrays.items()}
    out = nc.dram_tensor("out", (P, KD * T), F32, kind="ExternalOutput").ap()
    spill = nc.dram_tensor("spill", (P, KD * T), F32, kind="Internal").ap()
    build(nc, spill=spill, out=out, **aps)
    r = run_bass_kernel_spmd(nc, [arrays], core_ids=[0])
    got = r.results[0]["out"]
    return got.reshape(P, KD, T).transpose(2, 1, 0).reshape(1, T, D)
```
